# Optimizing a Trainium2 kernel written in Bass

```python
import jax, jax.numpy as jnp
from jax import lax
import numpy as np
import jax
import jax.numpy as jnp

D_MODEL = 2048
BATCH = 1
SEQ = 256
DEPTH = 1

CHUNK = 64
MIX_WIDTH = D_MODEL
POOL_WIDTH = MIX_WIDTH // 2
POOL_WINDOWS = (2, 4, 8, 16)
POOL_GROUP = POOL_WIDTH // len(POOL_WINDOWS)
HGRN_WIDTH = MIX_WIDTH - POOL_WIDTH
HGRN_HEAD_DIM = 128
HGRN_HEADS = HGRN_WIDTH // HGRN_HEAD_DIM
IN_WIDTH = POOL_WIDTH + 4 * HGRN_WIDTH
D_FF = 4 * D_MODEL
EPS = 1e-6


def rmsnorm(x, w):
    xf = x.astype(jnp.float32)
    r = xf * lax.rsqrt(jnp.mean(xf * xf, axis=-1, keepdims=True) + EPS)
    return (r * w.astype(jnp.float32)).astype(x.dtype)

def pool_mixer(u, pool_w, pool_b, pool_scale):
    B, S, _ = u.shape
    uf = u.astype(jnp.float32)
    c = jnp.cumsum(uf, axis=1)
    pos = jnp.arange(S)
    outs = []
    for j, w in enumerate(POOL_WINDOWS):
        sl = slice(j * POOL_GROUP, (j + 1) * POOL_GROUP)
        cj = c[..., sl]
        shifted = jnp.pad(cj, ((0, 0), (w, 0), (0, 0)))[:, :S]
        cnt = jnp.minimum(pos + 1, w).astype(jnp.float32)[None, :, None]
        dj = ((cj - shifted) / cnt - uf[..., sl]).astype(u.dtype)
        outs.append(dj @ pool_w[j] + pool_b[j])
    return jnp.concatenate(outs, axis=-1) * pool_scale

def hgrn2_chunk_scan(q, k, v, logf):
    B, S, H, Dk = q.shape
    Dv = v.shape[-1]
    N = S // CHUNK

    def to_chunks(a):
        return a.reshape(B, N, CHUNK, H, a.shape[-1]).transpose(1, 0, 3, 2, 4)

    causal = jnp.tril(jnp.ones((CHUNK, CHUNK), dtype=bool))[None, None, :, :, None]

    def step(state, inp):
        q_c, k_c, v_c, g_c = inp
        b = jnp.cumsum(g_c, axis=2)
        o_inter = jnp.einsum('bhtd,bhde->bhte', q_c * jnp.exp(b), state)
        diff = b[:, :, :, None, :] - b[:, :, None, :, :]
        decay = jnp.exp(jnp.where(causal, diff, -jnp.inf))
        scores = jnp.einsum('bhtd,bhsd,bhtsd->bhts', q_c, k_c, decay)
        o_intra = jnp.einsum('bhts,bhse->bhte', scores, v_c)
        b_last = b[:, :, -1:, :]
        new_state = jnp.exp(b_last[:, :, 0, :])[..., None] * state + jnp.einsum(
            'bhsd,bhse->bhde', k_c * jnp.exp(b_last - b), v_c)
        return new_state, o_inter + o_intra

    init = jnp.zeros((B, H, Dk, Dv), jnp.float32)
    _, o = lax.scan(step, init, (to_chunks(q), to_chunks(k), to_chunks(v), to_chunks(logf)))
    return o.transpose(1, 0, 3, 2, 4).reshape(B, S, H, Dv)

def hgrn2_mixer(q, f_pre, i, g, lb, norm_w):
    B, S, _ = q.shape
    shp = (B, S, HGRN_HEADS, HGRN_HEAD_DIM)
    qf = q.astype(jnp.float32).reshape(shp)
    vf = i.astype(jnp.float32).reshape(shp)
    sig = jax.nn.sigmoid(f_pre.astype(jnp.float32)).reshape(shp)
    lbh = lb.reshape(HGRN_HEADS, HGRN_HEAD_DIM)
    f = lbh + (1.0 - lbh) * sig
    k = (1.0 - lbh) * (1.0 - sig)
    o = hgrn2_chunk_scan(qf, k, vf, jnp.log(f))
    o = o * jax.nn.sigmoid(g.astype(jnp.float32)).reshape(shp)
    o = o * lax.rsqrt(jnp.mean(o * o, axis=-1, keepdims=True) + EPS)
    o = o * norm_w.astype(jnp.float32).reshape(HGRN_HEADS, HGRN_HEAD_DIM)
    return o.reshape(B, S, HGRN_WIDTH).astype(q.dtype)

def first_inputs(seed: int = 0) -> dict:
    key = jax.random.key(seed)
    ks = jax.random.split(key, 16)
    f32 = jnp.float32
    nrm = lambda k, s, sc: jax.random.normal(k, s, f32) * sc
    gain = lambda k, s: 1.0 + 0.05 * jax.random.normal(k, s, f32)
    return {
        "x": jax.random.normal(ks[0], (BATCH, SEQ, D_MODEL), f32),
        "w_in": nrm(ks[1], (DEPTH, D_MODEL, IN_WIDTH), D_MODEL ** -0.5),
        "pool_w": nrm(ks[2], (DEPTH, len(POOL_WINDOWS), POOL_GROUP, POOL_GROUP), POOL_GROUP ** -0.5),
        "pool_b": nrm(ks[3], (DEPTH, len(POOL_WINDOWS), POOL_GROUP), 0.02),
        "pool_scale": gain(ks[4], (DEPTH, POOL_WIDTH)),
        "lb_logits": nrm(ks[5], (DEPTH + 1, HGRN_WIDTH), 0.5),
        "hgrn_norm_w": gain(ks[6], (DEPTH, HGRN_WIDTH)),
        "w_out": nrm(ks[7], (DEPTH, MIX_WIDTH, D_MODEL), MIX_WIDTH ** -0.5),
        "norm_mix_pre": gain(ks[8], (DEPTH, D_MODEL)),
        "norm_mix_post": gain(ks[9], (DEPTH, D_MODEL)),
        "norm_mlp_pre": gain(ks[10], (DEPTH, D_MODEL)),
        "norm_mlp_post": gain(ks[11], (DEPTH, D_MODEL)),
        "w_mlp_in": nrm(ks[12], (DEPTH, D_MODEL, D_FF), D_MODEL ** -0.5),
        "w_mlp_out": nrm(ks[13], (DEPTH, D_FF, D_MODEL), D_FF ** -0.5),
    }

def first_block(x, w_in, pool_w, pool_b, pool_scale, lb_logits, hgrn_norm_w, w_out,
              norm_mix_pre, norm_mix_post, norm_mlp_pre, norm_mlp_post,
              w_mlp_in, w_mlp_out):
    lb_all = jnp.cumsum(jax.nn.softmax(lb_logits.astype(jnp.float32), axis=0), axis=0)
    P, H4 = POOL_WIDTH, HGRN_WIDTH
    for l in range(DEPTH):
        h = rmsnorm(x, norm_mix_pre[l])
        proj = h @ w_in[l]
        u_pool = proj[..., :P]
        q = proj[..., P:P + H4]
        f_pre = proj[..., P + H4:P + 2 * H4]
        i = proj[..., P + 2 * H4:P + 3 * H4]
        g = proj[..., P + 3 * H4:P + 4 * H4]
        y_pool = pool_mixer(u_pool, pool_w[l], pool_b[l], pool_scale[l])
        y_hgrn = hgrn2_mixer(q, f_pre, i, g, lb_all[l], hgrn_norm_w[l])
        mix = jnp.concatenate([y_pool, y_hgrn], axis=-1) @ w_out[l]
        x = x + rmsnorm(mix, norm_mix_post[l])
        h = rmsnorm(x, norm_mlp_pre[l])
        ff = jnp.square(jax.nn.relu(h @ w_mlp_in[l])) @ w_mlp_out[l]
        x = x + rmsnorm(ff, norm_mlp_post[l])
    return x


GRID_W = 64
CTX_LEN = 256
N_MIXERS = 3
N_MOD = 6
NEG_INF = -1e30
D_FF_2 = 5632
FFN_CONV = 3
CHUNK_2 = 128
A_WIDTH = 2 * D_MODEL
A_GROUPS = 16
NA_HEADS = 16
NA_HEAD_DIM = D_MODEL // NA_HEADS
NA_KH_MAX = 8
NA_KW = 16
RNN_WIDTH = D_MODEL
RNN_HEADS = 16
RNN_HEAD_DIM = RNN_WIDTH // RNN_HEADS
RNN_CONV = 4
RG_C = 8.0
N_A_LAYERS = (DEPTH + N_MIXERS - 1) // N_MIXERS
N_B_LAYERS = (DEPTH + N_MIXERS - 2) // N_MIXERS
N_C_LAYERS = (DEPTH + N_MIXERS - 3) // N_MIXERS


def rmsnorm_2(x, g):
    xf = x.astype(jnp.float32)
    y = xf * lax.rsqrt(jnp.mean(xf * xf, axis=-1, keepdims=True) + EPS)
    return (y * g.astype(jnp.float32)).astype(x.dtype)

def modulate(h, shift, scale):
    return h * (1 + scale) + shift

def dwconv(x, w, b, left):
    k, length = w.shape[0], x.shape[1]
    xp = jnp.pad(x, ((0, 0), (left, k - 1 - left), (0, 0)))
    y = b
    for j in range(k):
        y = y + xp[:, j:j + length] * w[j]
    return y

def conv_ffn(h, w_up, conv_w, conv_b, w_down):
    z = dwconv(h @ w_up, conv_w, conv_b, FFN_CONV // 2)
    g, v = jnp.split(z, 2, axis=-1)
    return (jax.nn.silu(g) * v) @ w_down

def chunk_mlp_mix(h, w_in, g_v, w_s, b_s, w_out):
    bsz, length, _ = h.shape
    z = jax.nn.gelu(h @ w_in)
    u, v = jnp.split(z, 2, axis=-1)
    v = rmsnorm_2(v, g_v).reshape(bsz, length // CHUNK_2, CHUNK_2, A_GROUPS, A_WIDTH // A_GROUPS)
    s = jnp.einsum('gpq,bnqgc->bnpgc', w_s, v) + b_s.T[None, None, :, :, None]
    return (u * s.reshape(bsz, length, A_WIDTH)) @ w_out

def na_mix(hc, hl, w_qkv, rpb, w_out, need_ctx):
    bsz, seq, _ = hl.shape
    rows = seq // GRID_W
    kh = min(NA_KH_MAX, rows)
    scale = NA_HEAD_DIM ** -0.5
    qkv = (hl @ w_qkv).reshape(bsz, rows, GRID_W, 3, NA_HEADS, NA_HEAD_DIM)
    q, k, v = qkv[:, :, :, 0], qkv[:, :, :, 1], qkv[:, :, :, 2]
    if need_ctx:
        qkv_c = (hc @ w_qkv).reshape(bsz, hc.shape[1], 3, NA_HEADS, NA_HEAD_DIM)
        q_c, k_c, v_c = qkv_c[:, :, 0], qkv_c[:, :, 1], qkv_c[:, :, 2]
    else:
        kv_c = (hc @ w_qkv[:, D_MODEL:]).reshape(bsz, hc.shape[1], 2, NA_HEADS, NA_HEAD_DIM)
        k_c, v_c = kv_c[:, :, 0], kv_c[:, :, 1]
    r = jnp.arange(rows)
    r0 = jnp.clip(r - kh // 2, 0, rows - kh)
    key_rows = r0[:, None] + jnp.arange(kh)[None, :]
    col = jnp.arange(GRID_W)
    c0 = jnp.clip(col - NA_KW // 2, 0, GRID_W - NA_KW)
    col_ok = (col[None, :] >= c0[:, None]) & (col[None, :] < c0[:, None] + NA_KW)
    k_blk = k[:, key_rows]
    v_blk = v[:, key_rows]
    s_lat = jnp.einsum('brqhd,brikhd->bhrqik', q, k_blk).astype(jnp.float32) * scale
    dr = key_rows - r[:, None]
    dc = jnp.clip(col[None, :] - col[:, None], -(NA_KW - 1), NA_KW - 1)
    bias = rpb[:, dr[:, None, :, None] + NA_KH_MAX - 1, dc[None, :, None, :] + NA_KW - 1]
    s_lat = jnp.where(col_ok[None, None, None, :, None, :], s_lat + bias[None].astype(jnp.float32), NEG_INF)
    s_ctx = jnp.einsum('brqhd,bkhd->bhrqk', q, k_c).astype(jnp.float32) * scale
    n_win = kh * GRID_W
    logits = jnp.concatenate([s_lat.reshape(bsz, NA_HEADS, rows, GRID_W, n_win), s_ctx], axis=-1)
    p = jax.nn.softmax(logits, axis=-1).astype(v.dtype)
    p_lat = p[..., :n_win].reshape(bsz, NA_HEADS, rows, GRID_W, kh, GRID_W)
    o = jnp.einsum('bhrqik,brikhd->brqhd', p_lat, v_blk) + jnp.einsum('bhrqk,bkhd->brqhd', p[..., n_win:], v_c)
    y_lat = o.reshape(bsz, seq, D_MODEL) @ w_out
    y_ctx = None
    if need_ctx:
        sc = jnp.einsum('bqhd,bkhd->bhqk', q_c, k_c).astype(jnp.float32) * scale
        pc = jax.nn.softmax(sc, axis=-1).astype(v_c.dtype)
        y_ctx = jnp.einsum('bhqk,bkhd->bqhd', pc, v_c).reshape(bsz, hc.shape[1], D_MODEL) @ w_out
    return y_ctx, y_lat

def rglru_gates(xr, w_g, b_g, lam):
    bsz, length, _ = xr.shape
    xh = xr.reshape(bsz, length, RNN_HEADS, RNN_HEAD_DIM)
    g = jnp.einsum('blhi,ghij->gblhj', xh, w_g) + b_g[:, None, None]
    g = jax.nn.sigmoid(g.astype(jnp.float32)).reshape(2, bsz, length, RNN_WIDTH)
    log_a = -RG_C * g[0] * jax.nn.softplus(-lam.astype(jnp.float32))
    a = jnp.exp(log_a)
    b = jnp.sqrt(-jnp.expm1(2.0 * log_a)) * (g[1] * xr.astype(jnp.float32))
    return a, b

def linear_scan(a, b, h0, reverse):
    idx = -1 if reverse else 0
    b = b.at[:, idx].add(a[:, idx] * h0)

    def combine(e1, e2):
        a1, b1 = e1
        a2, b2 = e2
        return a1 * a2, a2 * b1 + b2

    _, h = lax.associative_scan(combine, (a, b), reverse=reverse, axis=1)
    return h

def rglru_mix(hc, hl, w_in, conv_w, conv_b, w_gate, b_gate, lam, w_out, need_ctx):
    left = RNN_CONV // 2
    if need_ctx:
        y_c, x_c = jnp.split(hc @ w_in, 2, axis=-1)
    else:
        x_c = hc @ w_in[:, RNN_WIDTH:]
    x_c = dwconv(x_c, conv_w, conv_b, left)
    y_l, x_l = jnp.split(hl @ w_in, 2, axis=-1)
    x_l = dwconv(x_l, conv_w, conv_b, left)
    h0 = jnp.zeros((hc.shape[0], RNN_WIDTH), jnp.float32)
    h_c_dirs, h_l_dirs = [], []
    for d, rev in enumerate((False, True)):
        a_c, b_c = rglru_gates(x_c, w_gate[d], b_gate[d], lam[d])
        h_c = linear_scan(a_c, b_c, h0, rev)
        h_end = h_c[:, 0] if rev else h_c[:, -1]
        a_l, b_l = rglru_gates(x_l, w_gate[d], b_gate[d], lam[d])
        h_l_dirs.append(linear_scan(a_l, b_l, h_end, rev))
        h_c_dirs.append(h_c)
    h_l = (h_l_dirs[0] + h_l_dirs[1]).astype(hl.dtype)
    y_lat = (jax.nn.gelu(y_l) * h_l) @ w_out
    y_ctx = None
    if need_ctx:
        h_cs = (h_c_dirs[0] + h_c_dirs[1]).astype(hc.dtype)
        y_ctx = (jax.nn.gelu(y_c) * h_cs) @ w_out
    return y_ctx, y_lat

def second_inputs(seed: int = 0) -> dict:
    key = jax.random.key(seed)
    ks = iter(jax.random.split(key, 32))

    def nrm(shape, scale):
        return jax.random.normal(next(ks), shape, jnp.float32) * scale

    D = D_MODEL
    nA, nB, nC = N_A_LAYERS, N_B_LAYERS, N_C_LAYERS
    a0 = jax.random.uniform(next(ks), (nC, 2, RNN_WIDTH), jnp.float32, 0.9, 0.999)
    s = a0 ** (1.0 / RG_C)
    c_lam = jnp.log(s) - jnp.log1p(-s)
    return {
        'x': nrm((BATCH, SEQ, D), 1.0),
        'c': nrm((BATCH, D), 1.0),
        'ctx': nrm((BATCH, CTX_LEN, D), 1.0),
        'c_ctx': nrm((D,), 1.0),
        'ada_w': nrm((DEPTH, D, N_MOD * D), D ** -0.5),
        'ada_b': nrm((DEPTH, N_MOD * D), 0.02),
        'norm_g': 1.0 + nrm((DEPTH, 2, D), 0.05),
        'ffn_w_up': nrm((DEPTH, D, 2 * D_FF_2), D ** -0.5),
        'ffn_conv_w': nrm((DEPTH, FFN_CONV, 2 * D_FF_2), FFN_CONV ** -0.5),
        'ffn_conv_b': nrm((DEPTH, 2 * D_FF_2), 0.02),
        'ffn_w_down': nrm((DEPTH, D_FF_2, D), D_FF_2 ** -0.5),
        'a_w_in': nrm((nA, D, 2 * A_WIDTH), D ** -0.5),
        'a_g_v': 1.0 + nrm((nA, A_WIDTH), 0.05),
        'a_w_s': nrm((nA, A_GROUPS, CHUNK_2, CHUNK_2), CHUNK_2 ** -0.5),
        'a_b_s': nrm((nA, A_GROUPS, CHUNK_2), 0.1),
        'a_w_out': nrm((nA, A_WIDTH, D), A_WIDTH ** -0.5),
        'b_w_qkv': nrm((nB, D, 3 * D), D ** -0.5),
        'b_rpb': nrm((nB, NA_HEADS, 2 * NA_KH_MAX - 1, 2 * NA_KW - 1), 0.2),
        'b_w_out': nrm((nB, D, D), D ** -0.5),
        'c_w_in': nrm((nC, D, 2 * RNN_WIDTH), D ** -0.5),
        'c_conv_w': nrm((nC, RNN_CONV, RNN_WIDTH), RNN_CONV ** -0.5),
        'c_conv_b': nrm((nC, RNN_WIDTH), 0.02),
        'c_w_gate': nrm((nC, 2, 2, RNN_HEADS, RNN_HEAD_DIM, RNN_HEAD_DIM), RNN_HEAD_DIM ** -0.5),
        'c_b_gate': nrm((nC, 2, 2, RNN_HEADS, RNN_HEAD_DIM), 0.1),
        'c_lam': c_lam,
        'c_w_out': nrm((nC, RNN_WIDTH, D), RNN_WIDTH ** -0.5),
        'final_g': 1.0 + nrm((D,), 0.05),
    }

def second_block(x, c, ctx, c_ctx, ada_w, ada_b, norm_g, ffn_w_up, ffn_conv_w, ffn_conv_b, ffn_w_down,
              a_w_in, a_g_v, a_w_s, a_b_s, a_w_out, b_w_qkv, b_rpb, b_w_out,
              c_w_in, c_conv_w, c_conv_b, c_w_gate, c_b_gate, c_lam, c_w_out, final_g):
    bsz = x.shape[0]
    silu_c = jax.nn.silu(c)
    silu_cc = jax.nn.silu(c_ctx)
    h_lat, h_ctx = x, ctx
    for i in range(DEPTH):
        last = i == DEPTH - 1
        kind, j = i % N_MIXERS, i // N_MIXERS
        ctx_in = (not last) or kind != 0
        m_l = (silu_c @ ada_w[i] + ada_b[i]).reshape(bsz, 1, N_MOD, D_MODEL)
        n_l = modulate(rmsnorm_2(h_lat, norm_g[i, 0]), m_l[:, :, 0], m_l[:, :, 1])
        if ctx_in:
            m_c = (silu_cc @ ada_w[i] + ada_b[i]).reshape(N_MOD, D_MODEL)
            n_c = modulate(rmsnorm_2(h_ctx, norm_g[i, 0]), m_c[0], m_c[1])
        if kind == 0:
            y_l = chunk_mlp_mix(n_l, a_w_in[j], a_g_v[j], a_w_s[j], a_b_s[j], a_w_out[j])
            y_c = None if last else chunk_mlp_mix(n_c, a_w_in[j], a_g_v[j], a_w_s[j], a_b_s[j], a_w_out[j])
        elif kind == 1:
            y_c, y_l = na_mix(n_c, n_l, b_w_qkv[j], b_rpb[j], b_w_out[j], not last)
        else:
            y_c, y_l = rglru_mix(n_c, n_l, c_w_in[j], c_conv_w[j], c_conv_b[j], c_w_gate[j], c_b_gate[j],
                                 c_lam[j], c_w_out[j], not last)
        h_lat = h_lat + m_l[:, :, 2] * y_l
        n_l = modulate(rmsnorm_2(h_lat, norm_g[i, 1]), m_l[:, :, 3], m_l[:, :, 4])
        h_lat = h_lat + m_l[:, :, 5] * conv_ffn(n_l, ffn_w_up[i], ffn_conv_w[i], ffn_conv_b[i], ffn_w_down[i])
        if not last:
            h_ctx = h_ctx + m_c[2] * y_c
            n_c = modulate(rmsnorm_2(h_ctx, norm_g[i, 1]), m_c[3], m_c[4])
            h_ctx = h_ctx + m_c[5] * conv_ffn(n_c, ffn_w_up[i], ffn_conv_w[i], ffn_conv_b[i], ffn_w_down[i])
    return rmsnorm_2(h_lat, final_g)


def setup_inputs(seed=0):
    out = dict(first_inputs(seed))
    for name, value in second_inputs(seed + 1).items():
        if name != "x":
            out[name + "_2"] = value
    return out


def reference(
    x, w_in, pool_w, pool_b, pool_scale, lb_logits, hgrn_norm_w, w_out, norm_mix_pre,
    norm_mix_post, norm_mlp_pre, norm_mlp_post, w_mlp_in, w_mlp_out, c_2, ctx_2, c_ctx_2,
    ada_w_2, ada_b_2, norm_g_2, ffn_w_up_2, ffn_conv_w_2, ffn_conv_b_2, ffn_w_down_2, a_w_in_2,
    a_g_v_2, a_w_s_2, a_b_s_2, a_w_out_2, b_w_qkv_2, b_rpb_2, b_w_out_2, c_w_in_2, c_conv_w_2,
    c_conv_b_2, c_w_gate_2, c_b_gate_2, c_lam_2, c_w_out_2, final_g_2,
):
    x = first_block(
        x, w_in, pool_w, pool_b, pool_scale, lb_logits, hgrn_norm_w, w_out, norm_mix_pre,
        norm_mix_post, norm_mlp_pre, norm_mlp_post, w_mlp_in, w_mlp_out,
    )
    return second_block(
        x, c_2, ctx_2, c_ctx_2, ada_w_2, ada_b_2, norm_g_2, ffn_w_up_2, ffn_conv_w_2,
        ffn_conv_b_2, ffn_w_down_2, a_w_in_2, a_g_v_2, a_w_s_2, a_b_s_2, a_w_out_2, b_w_qkv_2,
        b_rpb_2, b_w_out_2, c_w_in_2, c_conv_w_2, c_conv_b_2, c_w_gate_2, c_b_gate_2, c_lam_2,
        c_w_out_2, final_g_2,
    )


_drawn_inputs = setup_inputs


def setup_inputs(seed=0):
    import zlib

    import numpy as np

    out = dict(_drawn_inputs(seed))
    spreads = {}
    factors = {'pool_b': 4.947,
     'ada_b_2': 2.673,
     'ffn_conv_b_2': 7.666,
     'a_g_v_2': 3.61,
     'a_b_s_2': 2.764}
    for name, (base, spread) in spreads.items():
        noise = np.random.default_rng([zlib.crc32(name.encode()), seed]).standard_normal(out[name].shape)
        drawn = base * np.exp(spread * noise) if base else spread * noise
        out[name] = jnp.asarray(drawn.astype(out[name].dtype))
    for name, factor in factors.items():
        out[name] = (out[name] * factor).astype(out[name].dtype)
    return out
```

```python
import concourse.bass as bass
from concourse import mybir
from contextlib import ExitStack, contextmanager

F32 = mybir.dt.float32
F32R = mybir.dt.float32r
I32 = mybir.dt.int32
ACT = mybir.ActivationFunctionType
ALU = mybir.AluOpType
AX = mybir.AxisListType

P = 128
T = 256
D = 2048
KT = D // P
NC = 512
MT = NC // P
UK = 2
UW = UK * NC
RING = 4
GU = KT // UK
EPS = 1e-6
HEADS = 8
HD = 128
POOLT = 8
WINDOWS = (2, 4, 8, 16)
PAD = 16
LEVELS = (128, 64, 32, 16, 8, 4, 2, 1)
FF1 = 8192
FF2T = 5632 // P
AV = 4096

G_IN = 0
G_OUT = 10
G_MLP = 14
G_AV = G_MLP + 32
G_AU = G_AV + 8
G_FF = G_AU + 16
G_FT = G_FF + 24
G_DT = G_FT + 6
DTU = 6
UNITS = GU * G_DT + 4 * DTU
ADA_PER_GROUP = 4
ADA_GROUPS = 48
ADA_PER_VEC = 32
H_A, H_F = 16, 24


class Count:

    def __init__(self, sem):
        self.sem, self.done, self.off = sem, 0, 0

    def value(self):
        return self.off + self.done

    @contextmanager
    def loop(self, i, trips, per):
        off, done = self.off, self.done
        self.off = off + i * per
        yield
        assert self.done - done == per, (self.done - done, per)
        self.off, self.done = off, done + trips * per


def build(nc, xT, wstream, astream, cT, adab, gains, cwp, gvp, bsp, wsT, poolw, poolp, lbl, masks, corr, out):
    ctx = ExitStack()
    with ctx:
        slab = ctx.enter_context(nc.sbuf_tensor("slab", [P, 212800 // 4], F32))
        base = nc.sbuf_base - 212800 if isinstance(nc.sbuf_base, int) else nc.sbuf_base() - 212800
        at = [base]

        def region(size):
            o = at[0]
            at[0] += size
            assert at[0] <= base + 212800, at[0] - base
            return o

        def place(name, offset, shape, dt=F32):
            return nc.alloc_sbuf_tensor_at(name, shape, dt, offset=offset)

        sem = lambda n: ctx.enter_context(nc.semaphore(n))
        KB = 1024
        raw = place("raw", region(16 * KB), [P, RING, UW])
        whi = place("whi", region(16 * KB), [P, RING, UW], F32R)
        wlo = place("wlo", region(16 * KB), [P, RING, UW], F32R)
        xs = place("xs", region(32 * KB), [P, KT, 2 * T], F32R)
        o_hs = region(32 * KB)
        hs = place("hs", o_hs, [P, KT, 2 * T], F32R)
        x = place("x", region(16 * KB), [P, KT, T])
        o_v = region(32 * KB)
        o_out = region(16 * KB)
        o_ada = region(16 * KB)
        o_vs = region(4 * KB)
        t0 = place("t0", region(4 * KB), [P, 2, 2 * T])
        t1 = place("t1", region(4 * KB), [P, 2, 2 * T])

        vtok = place("vtok", o_v, [P, 2, AV])
        vs = place("vs", o_vs, [P, 2, NC])
        ws = place("ws", o_out, [P, 16, P])
        bs = place("bs", o_out + 8 * KB, [P, 16, P])
        zt = place("zt", o_v, [P, MT, T])
        gt = place("gt", o_v + 4 * KB, [P, MT, T])
        acc = place("acc", o_out, [P, KT, T])
        aring = place("aring", o_ada, [P, 2, UW])
        aacc = place("aacc", o_ada + 8 * KB, [P, D])
        rstd = place("rstd", o_vs, [P, T])
        ssa = place("ssa", o_vs + KB, [P, T])
        ssb = place("ssb", o_vs + 2 * KB, [P, T])

        fg = place("fg", o_v, [P, HEADS, T])
        qq = place("qq", o_v + 8 * KB, [P, HEADS, T])
        mixf = place("mixf", o_v + 8 * KB, [P, HEADS, T])
        vv = place("vv", o_v + 16 * KB, [P, 2, HEADS * HD])
        oo = place("oo", o_v + 24 * KB, [P, HEADS, T])
        kk = place("kk", o_out, [P, 4 * T])
        bb = place("bb", o_out + 4 * KB, [P, 4 * T])
        kl = place("kl", o_out + 8 * KB, [P, 2, 4 * T])
        arg = place("arg", o_ada, [P, 2, 2, 2 * T])
        qe = place("qe", o_ada + 8 * KB, [P, 2, 2 * T])
        lgf = place("lgf", o_ada + 12 * KB, [P, 4 * T])
        PW = PAD + T
        uu = place("uu", o_out, [P, POOLT, PW])
        sa = place("sa", o_out + 9 * KB, [P, POOLT, PW])
        sb_ = place("sb_", o_out + 18 * KB, [P, POOLT, PW])
        sq8 = place("sq8", o_out + 9 * KB, [P, HEADS, T])
        sc = place("sc", o_hs, [P, 2, 3, 4, P])
        pw = place("pw", o_hs + 12 * KB, [P, 8, T])
        sgf = place("sgf", o_hs + 20 * KB, [P, 4 * T])
        fft = place("fft", o_hs + 24 * KB, [P, 4 * T])
        NM = 7 * 64 + P
        mk = place("mk", o_hs + 28 * KB, [P, NM], I32)

        gain = place("gain", region(7 * 64), [P, 7, KT])
        cw = place("cw", region(2 * FF2T * 4 * 4), [P, 2 * FF2T, 4])
        gv = place("gv", region(128), [P, 32])
        ab = place("ab", region(6 * 64), [P, 6, KT])
        mod = place("mod", region(6 * 64), [P, 6, KT])
        sc_c = place("sc_c", region(64), [P, KT])
        geff = place("geff", region(64), [P, KT])
        inv = place("inv", region(512), [P, P])
        one = place("one", region(32), [P, 1])
        ssv = place("ssv", region(64), [P, 2, 8])
        rv = place("rv", region(32), [P, 2])
        pp = place("pp", o_vs + 3 * KB, [P, 3, 8])
        lb2 = place("lb2", o_vs + 3 * KB + 96, [P, 2, 8])
        lbt = place("lbt", o_vs + 3 * KB + 160, [P, 8])
        oml = place("oml", o_vs + 3 * KB + 192, [P, 8])
        lbm = place("lbm", o_vs + 3 * KB + 224, [P, 8])
        cor = place("cor", o_vs + 3 * KB + 256, [P, 4, 16])
        cf = place("cf", o_vs + 3 * KB + 512, [P, KT])

        bank = [ctx.enter_context(nc.psum_tensor(f"bank{i}", [P, NC], F32)) for i in range(4)]
        mis = [ctx.enter_context(nc.psum_tensor(f"mis{i}", [P, NC], F32)) for i in range(4)]

        raw_arrived = [sem(f"raw_arrived{i}") for i in range(RING)]
        ada_arrived = [sem(f"ada_arrived{i}") for i in range(2)]
        x_arrived = sem("x_arrived")
        par_arrived = sem("par_arrived")
        mix_arrived = sem("mix_arrived")
        ws_arrived = sem("ws_arrived")
        out_sent = sem("out_sent")
        hi_ready = sem("hi_ready")
        lo_ready = sem("lo_ready")
        unit_used = sem("unit_used")
        bank_free = sem("bank_free")
        hid_hi = sem("hid_hi")
        hid_lo = sem("hid_lo")
        prod_ready = sem("prod_ready")
        mixs_ready = sem("mixs_ready")
        vs_ready = sem("vs_ready")
        zt_ready = sem("zt_ready")
        sg_ready = sem("sg_ready")
        gate_ready = sem("gate_ready")
        ada_used = sem("ada_used")
        ada_sum = sem("ada_sum")
        sq_ready = sem("sq_ready")
        sq_used = sem("sq_used")
        var_ready = sem("var_ready")
        sd_ready = sem("sd_ready")
        nt_ready = sem("nt_ready")
        xs_hi = sem("xs_hi")
        xs_lo = sem("xs_lo")
        mix_t = sem("mix_t")
        mix_hi = sem("mix_hi")
        mix_lo = sem("mix_lo")
        h_sg = sem("h_sg")
        h_ff = sem("h_ff")
        h_ln = sem("h_ln")
        h_arg = sem("h_arg")
        h_exp = sem("h_exp")
        h_ops = sem("h_ops")
        h_sc = sem("h_sc")
        h_evac = sem("h_evac")
        h_o = sem("h_o")
        h_oc = sem("h_oc")
        p_d = sem("p_d")
        p_mm = sem("p_mm")
        h_gs = sem("h_gs")
        h_og = sem("h_og")
        h_sq = sem("h_sq")
        h_ss = sem("h_ss")
        h_va = sem("h_va")
        h_sd = sem("h_sd")
        silu_e = sem("silu_e")
        lb_s = sem("lb_s")
        cst = sem("cst")
        acc_copied = sem("acc_copied")
        out_ready = sem("out_ready")
        dve_step = sem("dve_step")
        act_step = sem("act_step")
        ms_ready = sem("ms_ready")
        out_ready_x = sem("out_ready_x")
        ssv_ready = sem("ssv_ready")
        var_v = sem("var_v")
        sd_v = sem("sd_v")

        def half_level(hf, l):
            return hf * (len(LEVELS) + 1) + l

        block = ctx.enter_context(nc.Block())

        @block.sync
        def _(sp):
            def unit(n, slot):
                if not (isinstance(n, int) and n < RING):
                    sp.wait_ge(lo_ready, n - RING + 1)
                sp.dma_start(raw[:, slot, :], wstream[bass.ds(n, 1), :, :].rearrange("o p w -> p (o w)")
                             ).then_inc(raw_arrived[slot], 16)

            def ada(k, slot, wait=True):
                if wait:
                    sp.wait_ge(ada_used, k - 1)
                sp.dma_start(aring[:, slot, :], astream[bass.ds(k, 1), :, :].rearrange("o p w -> p (o w)")
                             ).then_inc(ada_arrived[slot], 16)

            def group(n, k=None, first=False):
                for i in range(GU):
                    unit(n + i, i % RING)
                    if k is not None and i < ADA_PER_GROUP:
                        ada(k + i, i % 2, wait=not (first and i < 2))

            sp.dma_start(x[:, :, :], xT).then_inc(x_arrived, 16)
            for dst, src in ((gain, gains), (cw, cwp), (gv, gvp), (ab, adab), (cf, cT)):
                sp.dma_start(dst[:], src).then_inc(par_arrived, 16)
            for i in range(RING):
                unit(i, i)
            for dst, src in ((pw, poolw), (pp, poolp), (lb2, lbl), (mk, masks), (cor, corr)):
                sp.dma_start(dst[:], src).then_inc(mix_arrived, 16)
            with sp.Fori(0, G_MLP) as g:
                group(g * GU + RING)
            sp.wait_ge(mix_lo, 8)
            group(G_MLP * GU + RING, 0, first=True)
            with sp.Fori(1, 32) as g:
                group(g * GU + (G_MLP * GU + RING), g * ADA_PER_GROUP)
            sp.wait_ge(acc_copied, 1)
            sp.dma_start(ws[:], wsT).then_inc(ws_arrived, 16)
            sp.dma_start(bs[:], bsp.rearrange("(o g) q -> o g q", o=1).to_broadcast([P, 16, P])
                         ).then_inc(ws_arrived, 16)
            with sp.Fori(32, ADA_GROUPS) as g:
                group(g * GU + (G_MLP * GU + RING), g * ADA_PER_GROUP)
            with sp.Fori(G_MLP + ADA_GROUPS, G_DT) as g:
                group(g * GU + RING)
            for n in range(G_DT * GU + RING, UNITS):
                unit(n, n % RING)
            sp.wait_ge(out_ready, 1)
            sp.dma_start(out, acc[:, :, :]).then_inc(out_sent, 16)
            sp.wait_ge(out_sent, 16)

        @block.tensor
        def _(pe):
            def feature_unit(src, kt0, n, slot, first, last, pb, wait=None):
                if wait is not None:
                    pe.wait_ge(*wait)
                pe.wait_ge(lo_ready, n + 1)
                for k in range(UK):
                    for m in range(MT):
                        o = bank[pb + m // 2][:, (m % 2) * T:(m % 2 + 1) * T]
                        c = slice(k * NC + m * P, k * NC + (m + 1) * P)
                        h, l = src[:, kt0 + k, 0:T], src[:, kt0 + k, T:2 * T]
                        st = first and k == 0 and m % 2 == 0
                        sp_ = last and k == UK - 1
                        pe.matmul(o, whi[:, slot, c], h, start=st, stop=False, skip_group_check=True)
                        pe.matmul(o, whi[:, slot, c], l, start=False, stop=False, skip_group_check=True)
                        mm = pe.matmul(o, wlo[:, slot, c], h, start=False, stop=sp_, skip_group_check=True)
                mm.then_inc(unit_used, 1)

            def token_unit(kt0, n, slot, first, last, pb, wait=None):
                if wait is not None:
                    pe.wait_ge(*wait)
                pe.wait_ge(lo_ready, n + 1)
                for k in range(UK):
                    c = slice(k * NC, (k + 1) * NC)
                    for b in range(2):
                        o = bank[pb + b][:, :]
                        h = xs[:, kt0 + k, b * P:(b + 1) * P]
                        l = xs[:, kt0 + k, T + b * P:T + (b + 1) * P]
                        pe.matmul(o, h, whi[:, slot, c], start=first and k == 0, stop=False)
                        pe.matmul(o, l, whi[:, slot, c], start=False, stop=False)
                        mm = pe.matmul(o, h, wlo[:, slot, c], start=False, stop=last and k == UK - 1)
                mm.then_inc(unit_used, 1)

            def group(j, src, pb, n=None, wait=None, token=False, units=GU, s0=0, between=None):
                n = j * GU if n is None else n
                if not (isinstance(j, int) and j < 2):
                    pe.wait_ge(bank_free, j * 2 - 2)
                for u in range(units):
                    w = wait(u) if wait else None
                    if token:
                        token_unit(UK * u, n + u, (s0 + u) % RING, u == 0, u == units - 1, pb, w)
                    else:
                        feature_unit(src, UK * u, n + u, (s0 + u) % RING, u == 0, u == units - 1, pb, w)
                    if between:
                        between(u)

            def stats(s):
                for i in range(8):
                    pe.wait_ge(sq_ready, 8 * s + i + 1)
                    pe.matmul(mis[2][:, :], inv[:, :], t0[:, i % 2, :], start=i == 0, stop=i == 7
                              ).then_inc(sq_used, 1)

            def ada_reduce(m):
                pe.wait_ge(ada_used, m * ADA_PER_VEC + ADA_PER_VEC)
                for c in range(KT):
                    mm = pe.matmul(mis[3][:, c:c + 1], aacc[:, c * P:(c + 1) * P], one[:, :], start=True, stop=True)
                mm.then_inc(ada_sum, 1)

            def level(hf, l):
                i = half_level(hf, l)
                b = mis[i % 2]
                pe.wait_ge(h_ops, i + 1)
                if i >= 2:
                    pe.wait_ge(h_evac, i - 1)
                if LEVELS[l] == 128:
                    for h in range(4):
                        mm = pe.matmul(b[:, h * P:(h + 1) * P], kl[:, i % 2, h * T:h * T + P],
                                       qe[:, i % 2, h * P:(h + 1) * P], start=True, stop=True)
                else:
                    for s in range(8):
                        h, tt = s // 2, s % 2
                        mm = pe.matmul(b[:, s * 64:(s + 1) * 64],
                                       kl[:, i % 2, h * T + tt * P:h * T + (tt + 1) * P],
                                       qe[:, i % 2, s * 64:(s + 1) * 64], start=True, stop=True)
                mm.then_inc(h_sc, 1)

            def diagonal(hf):
                i = half_level(hf, len(LEVELS))
                pe.wait_ge(h_ops, i + 1)
                if hf:
                    pe.wait_ge(h_evac, half_level(0, len(LEVELS)) + 1)
                for s in range(8):
                    h, tt = s // 2, s % 2
                    mm = pe.matmul(mis[2 + tt][:, h * P:(h + 1) * P], kk[:, h * T + tt * P:h * T + (tt + 1) * P],
                                   qq[:, 4 * hf + h, tt * P:(tt + 1) * P], start=True, stop=True)
                mm.then_inc(h_sc, 1)

            def weigh(hf):
                pe.wait_ge(h_evac, half_level(hf, len(LEVELS)) + 1)
                pe.wait_ge(bank_free, 12)
                if hf == 0:
                    pe.wait_ge(h_evac, half_level(1, len(LEVELS)) + 1)
                for h in range(4):
                    hh = 4 * hf + h
                    b = mis[hh // 2]
                    o = (hh % 2) * T
                    v = [vv[:, c, hh * P:(hh + 1) * P] for c in range(2)]
                    pe.matmul(b[:, o:o + P], v[0], sc[:, hf, 0, h, :], start=True, stop=True)
                    pe.matmul(b[:, o + P:o + T], v[0], sc[:, hf, 2, h, :], start=True, stop=False)
                    mm = pe.matmul(b[:, o + P:o + T], v[1], sc[:, hf, 1, h, :], start=False, stop=True)
                mm.then_inc(h_o, 1)

            def pool():
                pe.wait_ge(p_d, 1)
                pe.wait_ge(h_oc, 2)
                for e in range(POOLT):
                    for k in range(2):
                        mm = pe.matmul(mis[e // 2][:, (e % 2) * T:(e % 2 + 1) * T],
                                       pw[:, 2 * (e // 2) + k, (e % 2) * P:(e % 2 + 1) * P],
                                       uu[:, 2 * (e // 2) + k, PAD:], start=k == 0, stop=k == 1)
                mm.then_inc(p_mm, 1)

            def head_stats():
                pe.wait_ge(h_sq, 1)
                for i in range(4):
                    mm = pe.matmul(mis[i][:, :], inv[:, :], sq8[:, 2 * i:2 * i + 2, :], start=True, stop=True)
                mm.then_inc(h_ss, 1)

            pe.wait_ge(cst, 1)
            stats(0)
            xs0 = lambda z: (lambda u: (xs_lo, 8 * z + u + 1))
            work = {}
            for l in range(9):
                work[(2 + (l + 4) // 8, (l + 4) % 8)] = (0, l)
                work[(4 + (l + 4) // 8, (l + 4) % 8)] = (1, l)
            for j in range(G_OUT):
                def between(u, j=j):
                    if (j, u) in work:
                        hf, l = work[(j, u)]
                        level(hf, l) if l < len(LEVELS) else diagonal(hf)
                    if (j, u) == (6, 1):
                        weigh(0)
                        weigh(1)
                    if (j, u) == (8, 4):
                        pool()
                group(j, xs, 2 * (j % 2), wait=xs0(0), token=j in (4, 5), between=between)
            head_stats()
            for g in range(4):
                group(G_OUT + g, hs, 2 * (g % 2), wait=lambda u: (mix_lo, u + 1))
            stats(1)
            stats(2)
            with pe.Fori(0, 4) as q:
                with pe.Fori(0, 2) as p:
                    for a in range(2):
                        group(q * 8 + p * 2 + (G_MLP + a), xs, 2 * a, wait=xs0(1))
                with pe.Fori(0, 2) as p:
                    for a in range(2):
                        group(q * 8 + p * 2 + (G_MLP + 4 + a), hs, 2 * a,
                              wait=lambda u: (hid_lo, q * 8 + (2 + 2 * (u // 2 + 1))))
                ada_reduce(q)
            stats(3)
            stats(4)
            with pe.Fori(0, 4) as p:
                for a in range(2):
                    group(p * 2 + (G_AV + a), xs, 2 * a, wait=xs0(2), token=True)
            ada_reduce(4)

            def spatial(g):
                pe.wait_ge(vs_ready, g + 1)
                pe.wait_ge(hid_lo, g * 2 + (2 + 2 * H_A))
                for t in range(MT):
                    for c in range(2):
                        mm = pe.matmul(mis[t // 2][:, (t % 2) * T + c * P:(t % 2) * T + (c + 1) * P],
                                       vs[:, c, t * P:(t + 1) * P], ws[:, bass.ds(g * 2 + t // 2, 1), :],
                                       start=True, stop=True)
                    if t % 2:
                        mm.then_inc(mixs_ready, 1)

            pe.wait_ge(ws_arrived, 32)
            for half in range(2):
                with pe.Fori(0, 2) as p:
                    for a in range(2):
                        group(p * 2 + (G_AU + 8 * half + a), xs, 2 * a, wait=xs0(2))
                        spatial(p * 2 + (4 * half + a))
                with pe.Fori(0, 2) as p:
                    for a in range(2):
                        group(p * 2 + (G_AU + 8 * half + 4 + a), hs, 2 * a,
                              wait=lambda u: (hid_lo, 2 + 2 * (H_A + 4 * half + u // 2 + 1)))
                if half == 0:
                    ada_reduce(5)
            stats(5)
            with pe.Fori(0, 2) as c:
                with pe.Fori(0, 4) as p:
                    for a in range(2):
                        group(c * 12 + p * 2 + (G_FF + a), xs, 2 * a, wait=xs0(3))
                with pe.Fori(0, 2) as p:
                    for a in range(2):
                        group(c * 12 + p * 2 + (G_FF + 8 + a), hs, 2 * a,
                              wait=lambda u: (hid_lo, c * 8 + (2 + 2 * (H_F + u // 2 + 1))))
            with pe.Fori(0, 3) as p:
                for a in range(2):
                    group(p * 2 + (G_FT + a), xs, 2 * a, wait=xs0(3))
            for g in range(4):
                group(G_DT + g, hs, 2 * (g % 2), n=G_DT * GU + g * DTU, units=DTU, s0=2 * (g % 2),
                      wait=lambda u: (hid_lo, 2 + 2 * (H_F + 8 + u // 2 + 1)))
            stats(6)

        @block.scalar
        def _(act):
            step = Count(act_step)

            def link(ins):
                ins.then_inc(act_step, 1)
                step.done += 1
                act.wait_ge(act_step, step.value())

            def split(n, slot):
                act.wait_ge(raw_arrived[slot], rounds(n, slot))
                if not (isinstance(n, int) and n < RING):
                    act.wait_ge(unit_used, n - RING + 1)
                act.activation(whi[:, slot, :], raw[:, slot, :], ACT.Copy).then_inc(hi_ready, 1)

            def rounds(n, slot):
                return 16 * (n // RING + 1) if isinstance(n, int) else (n - slot) * 4 + 16

            def body(n, evac, units=GU, s0=0, after=None, pre=None):
                for i in range(units):
                    if i == units - 1:
                        evac()
                    if isinstance(n, int) and n + RING + i >= UNITS:
                        continue
                    split(n + RING + i, (s0 + i) % RING)
                    if after:
                        after(i)

            def squares(s, src, ready):
                if ready is not None:
                    act.wait_ge(*ready)
                for i in range(8):
                    if 8 * s + i - 1 > 0:
                        act.wait_ge(sq_used, 8 * s + i - 1)
                    act.activation(t0[:, i % 2, :], src[:, 2 * i:2 * i + 2, :], ACT.Square).then_inc(sq_ready, 1)
                act.wait_ge(var_ready, s + 1)
                act.activation(ssa[:, :], ssb[:, :], ACT.Sqrt).then_inc(sd_ready, 1)

            def split_xs(z):
                for i in range(8):
                    act.wait_ge(nt_ready, 8 * z + i + 1)
                    act.activation(xs[:, 2 * i:2 * i + 2, 0:T], t1[:, i % 2, :], ACT.Copy).then_inc(xs_hi, 1)

            def copy_out(dst, j, n, units=GU):
                act.wait_ge(unit_used, n + units)
                for b in range(2):
                    act.activation(dst(b), bank[2 * (j % 2) + b][:, :], ACT.Copy).then_inc(bank_free, 1)

            def relu2(j, h, a, tile):
                act.wait_ge(unit_used, j * GU + GU)
                for b in range(2):
                    act.wait_ge(hid_lo, h * 2 + (b + 1))
                    act.activation(t0[:, b, :], bank[2 * a + b][:, :], ACT.Relu).then_inc(bank_free, 1)
                    act.wait_ge(bank_free, j * 2 + (b + 1))
                    link(act.activation(t1[:, b, :], t0[:, b, :], ACT.Square))
                    act.activation(hs[:, bass.ds(tile + 2 * b, 2), 0:T], t1[:, b, :], ACT.Copy).then_inc(hid_hi, 1)

            def gelu_v(j, g, a):
                act.wait_ge(unit_used, j * GU + GU)
                for b in range(2):
                    dst = vtok[:, b, bass.ds(g * NC, NC)]
                    act.activation(dst, bank[2 * a + b][:, :], ACT.Gelu_apprx_tanh).then_inc(bank_free, 1)
                    act.wait_ge(bank_free, j * 2 + (b + 1))
                    act.activation(t0[:, b, :], dst, ACT.Square, accum_out=ssv[:, b, bass.ds(g, 1)])

            def gelu_u(j, g, h, a, tile):
                act.wait_ge(unit_used, j * GU + GU)
                for b in range(2):
                    act.wait_ge(hid_lo, h * 2 + (b + 1))
                    act.activation(t0[:, b, :], bank[2 * a + b][:, :], ACT.Gelu_apprx_tanh).then_inc(bank_free, 1)
                for b in range(2):
                    act.wait_ge(prod_ready, g * 2 + (b + 1))
                    act.activation(hs[:, bass.ds(tile + 2 * b, 2), 0:T], t1[:, b, :], ACT.Copy).then_inc(hid_hi, 1)

            def conv(j, a, pair, off, h):
                act.wait_ge(unit_used, j * GU + GU)
                if off == 0:
                    act.wait_ge(hid_lo, h * 2 + 2)
                for b in range(2):
                    if off:
                        act.wait_ge(gate_ready, pair * 2 + (b + 1))
                    for m in range(2):
                        tile = pair * 4 + (off + 2 * b + m)
                        ins = act.activation(zt[:, 2 * b + m, :], bank[2 * a + b][:, m * T:(m + 1) * T], ACT.Identity,
                                             bias=cw[:, bass.ds(tile, 1), 3], scale=cw[:, bass.ds(tile, 1), 1])
                    ins.then_inc(zt_ready, 1)

            def gate(j, a, pair, h):
                conv(j, a, pair, 0, h)
                for b in range(2):
                    act.wait_ge(bank_free, j * 2 + (b + 1))
                    act.activation(gt[:, 2 * b:2 * b + 2, :], zt[:, 2 * b:2 * b + 2, :], ACT.Sigmoid
                                   ).then_inc(sg_ready, 1)

            def value(j, a, pair, h, tile):
                conv(j, a, pair, FF2T, h)
                for b in range(2):
                    act.wait_ge(prod_ready, pair * 2 + (b + 1 + 16))
                    act.activation(hs[:, bass.ds(tile + 2 * b, 2), 0:T], t1[:, b, :], ACT.Copy).then_inc(hid_hi, 1)

            def prep(hf):
                act.wait_ge(bank_free, 4 * hf + 4)
                if hf:
                    act.wait_ge(h_ff, 1)
                act.activation(sgf[:, :], fg[:, 4 * hf:4 * hf + 4, :], ACT.Sigmoid).then_inc(h_sg, 1)
                act.wait_ge(h_ff, hf + 1)
                if hf:
                    act.wait_ge(h_arg, 1)
                act.activation(lgf[:, :], fft[:, :], ACT.Ln).then_inc(h_ln, 1)

            def exps(hf, l):
                i = half_level(hf, l)
                act.wait_ge(h_arg, hf * 8 + l + 1)
                act.activation(arg[:, i % 2, :, :], arg[:, i % 2, :, :], ACT.Exp).then_inc(h_exp, 1)

            act.wait_ge(x_arrived, 16)
            squares(0, x, None)
            split_xs(0)
            act.wait_ge(par_arrived, 16 * 5)
            act.activation(sc_c[:, :], cf[:, :], ACT.Sigmoid).then_inc(silu_e, 1)
            act.wait_ge(lb_s, 1)
            act.activation(lb2[:, :, :], lb2[:, :, :], ACT.Exp).then_inc(lb_s, 1)
            for i in range(RING):
                split(i, i)
            dsts = [lambda b: fg[:, 2 * b:2 * b + 2, :], lambda b: qq[:, 2 * b:2 * b + 2, :],
                    lambda b: fg[:, 4 + 2 * b:6 + 2 * b, :], lambda b: qq[:, 4 + 2 * b:6 + 2 * b, :],
                    lambda b: vv[:, b, 0:NC], lambda b: vv[:, b, NC:2 * NC],
                    lambda b: uu[:, 2 * b:2 * b + 2, PAD:], lambda b: uu[:, 4 + 2 * b:6 + 2 * b, PAD:],
                    lambda b: fg[:, 2 * b:2 * b + 2, :], lambda b: fg[:, 4 + 2 * b:6 + 2 * b, :]]

            def mix_half(lo, hi):
                for i in range(lo, hi):
                    act.wait_ge(mix_t, i + 1)
                    src = mixf if i < 4 else oo
                    i4 = i % 4
                    act.activation(hs[:, 2 * i:2 * i + 2, 0:T], src[:, 2 * i4:2 * i4 + 2, :], ACT.Copy
                                   ).then_inc(mix_hi, 1)

            for j in range(G_OUT):
                def after(i, j=j):
                    for hf, j0 in ((0, 2), (1, 4)):
                        l = (j - j0) * 8 + i
                        if l == 0:
                            prep(hf)
                        if 1 <= l <= len(LEVELS):
                            exps(hf, l - 1)
                    if (j, i) == (6, 3):
                        for hf in range(2):
                            act.wait_ge(h_o, hf + 1)
                            for b in range(2):
                                ins = act.activation(oo[:, 4 * hf + 2 * b:4 * hf + 2 * b + 2, :], mis[2 * hf + b][:, :],
                                                     ACT.Copy)
                            ins.then_inc(h_oc, 1)
                    if (j, i) == (8, 6):
                        mix_half(0, 4)

                def evac(j=j):
                    if j == 6:
                        act.wait_ge(ms_ready, 1)
                    if j == 8:
                        act.wait_ge(h_ff, 2)
                    copy_out(dsts[j], j, j * GU)
                    if j == G_OUT - 1:
                        act.wait_ge(bank_free, 2 * G_OUT)
                        act.activation(fg[:, :, :], fg[:, :, :], ACT.Sigmoid).then_inc(h_gs, 1)
                        act.wait_ge(h_og, 1)
                        act.activation(sq8[:, :, :], oo[:, :, :], ACT.Square).then_inc(h_sq, 1)
                        act.wait_ge(h_va, 1)
                        act.activation(sq8[:, :, :], sq8[:, :, :], ACT.Sqrt).then_inc(h_sd, 1)
                        mix_half(4, 8)
                body(j * GU, evac, after=after)
            for g in range(4):
                j = G_OUT + g
                body(j * GU, lambda: copy_out(lambda b: acc[:, 4 * g + 2 * b:4 * g + 2 * b + 2, :], j, j * GU))
            act.wait_ge(bank_free, 2 * (G_OUT + 4))
            squares(1, acc, None)
            squares(2, x, (out_ready_x, 1))
            split_xs(1)
            with act.Fori(0, 4) as q, step.loop(q, 4, 8):
                with act.Fori(0, 2) as p, step.loop(p, 2, 4):
                    for a in range(2):
                        j = q * 8 + p * 2 + (G_MLP + a)
                        body(j * GU, lambda: relu2(j, q * 4 + p * 2 + a, a, p * 8 + 4 * a))
                with act.Fori(0, 2) as p:
                    for a in range(2):
                        body((q * 8 + p * 2 + (G_MLP + 4 + a)) * GU, lambda: None)
            act.wait_ge(bank_free, 2 * G_AV)
            squares(3, acc, None)
            squares(4, x, (out_ready_x, 2))
            split_xs(2)
            with act.Fori(0, 4) as p:
                for a in range(2):
                    j = p * 2 + (G_AV + a)
                    body(j * GU, lambda: gelu_v(j, p * 2 + a, a))
            act.activation(t0[:, 0, 0:1], one[:, :], ACT.Copy).then_inc(ssv_ready, 1)
            act.wait_ge(var_v, 1)
            act.activation(rv[:, :], rv[:, :], ACT.Sqrt).then_inc(sd_v, 1)
            for half in range(2):
                with act.Fori(0, 2) as p:
                    for a in range(2):
                        j = p * 2 + (G_AU + 8 * half + a)
                        g = p * 2 + (4 * half + a)
                        body(j * GU, lambda: gelu_u(j, g, g + H_A, a, p * 8 + 4 * a))
                with act.Fori(0, 2) as p:
                    for a in range(2):
                        body((p * 2 + (G_AU + 8 * half + 4 + a)) * GU, lambda: None)
            squares(5, x, (bank_free, 2 * G_FF))
            split_xs(3)
            with act.Fori(0, 2) as c:
                with act.Fori(0, 4) as p:
                    j = c * 12 + p * 2 + G_FF
                    pair = c * 4 + p
                    body(j * GU, lambda: gate(j, 0, pair, pair + H_F))
                    body((j + 1) * GU, lambda: value(j + 1, 1, pair, pair + H_F, p * 4))
                with act.Fori(0, 2) as p:
                    for a in range(2):
                        body((c * 12 + p * 2 + (G_FF + 8 + a)) * GU, lambda: None)
            with act.Fori(0, 3) as p:
                j = p * 2 + G_FT
                body(j * GU, lambda: gate(j, 0, p + 8, p + (H_F + 8)))
                body((j + 1) * GU, lambda: value(j + 1, 1, p + 8, p + (H_F + 8), p * 4))
            for g in range(4):
                body(G_DT * GU + g * DTU, lambda: None, units=DTU, s0=2 * (g % 2))
            squares(6, x, (bank_free, 2 * (G_DT + 4)))

        @block.vector
        def _(dve):
            step = Count(dve_step)
            adas = Count(ada_used)

            def link(ins):
                ins.then_inc(dve_step, 1)
                step.done += 1
                dve.wait_ge(dve_step, step.value())

            def split(n, slot):
                dve.wait_ge(hi_ready, n + 1)
                dve.tensor_tensor(wlo[:, slot, :], raw[:, slot, :], whi[:, slot, :].bitcast(F32), ALU.subtract
                                  ).then_inc(lo_ready, 1)

            def ada(k, slot, kt, half):
                dve.wait_ge(ada_arrived[slot], (k - slot) * 8 + 16)
                a = aacc[:, half * UW:(half + 1) * UW]
                dve.wait_ge(ada_used, k)
                dve.scalar_tensor_tensor(out=a, in0=aring[:, slot, :], scalar=sc_c[:, bass.ds(kt, 1)], in1=a,
                                         op0=ALU.mult, op1=ALU.add).then_inc(ada_used, 1)

            def body(n, evac, units=GU, s0=0, after=None, k=None, kt=None, pre=None):
                if pre:
                    pre()
                for i in range(units):
                    if i == units - 1:
                        evac()
                    if isinstance(n, int) and n + RING + i >= UNITS:
                        continue
                    split(n + RING + i, (s0 + i) % RING)
                    if k is not None and i < ADA_PER_GROUP:
                        ada(k + i, i % 2, kt + i // 2, i % 2)
                    if after:
                        after(i)

            def ada_take(m):
                dve.wait_ge(ada_sum, m + 1)
                dve.tensor_tensor(mod[:, bass.ds(m, 1), :], mis[3][:, 0:KT], ab[:, bass.ds(m, 1), :], ALU.add)
                link(dve.memset(aacc[:, :], 0.0))

            def root(s):
                dve.wait_ge(sq_used, 8 * s + 8)
                link(dve.tensor_copy(ssa[:, :], mis[2][:, 0:T]))
                dve.scalar_tensor_tensor(out=ssb[:, :], in0=mis[2][:, T:2 * T], scalar=EPS, in1=ssa[:, :],
                                         op0=ALU.add, op1=ALU.add).then_inc(var_ready, 1)
                dve.wait_ge(sd_ready, s + 1)
                link(dve.reciprocal(rstd[:, :], ssa[:, :]))

            def normed_into_x(g):
                for t in range(KT):
                    ins = dve.scalar_tensor_tensor(out=acc[:, t, :], in0=acc[:, t, :], scalar=gain[:, g, t:t + 1],
                                                   in1=rstd[:, :], op0=ALU.mult, op1=ALU.mult)
                link(ins)
                dve.tensor_tensor(x[:, :, :], x[:, :, :], acc[:, :, :], ALU.add).then_inc(out_ready_x, 1)

            def make_xs(z, gn, shift=None):
                def normed(i):
                    if i >= 2:
                        dve.wait_ge(xs_lo, 8 * z + i - 1)
                    for m in range(2):
                        ins = dve.scalar_tensor_tensor(out=t1[:, i % 2, m * T:(m + 1) * T], in0=x[:, 2 * i + m, :],
                                                       scalar=gn[:, 2 * i + m:2 * i + m + 1], in1=rstd[:, :],
                                                       op0=ALU.mult, op1=ALU.mult)
                    if shift is not None:
                        link(ins)
                        for m in range(2):
                            tt = t1[:, i % 2, m * T:(m + 1) * T]
                            ins = dve.tensor_scalar(tt, tt, shift[:, 2 * i + m:2 * i + m + 1], None, ALU.add)
                    ins.then_inc(nt_ready, 1)

                normed(0)
                for i in range(8):
                    if i < 7:
                        normed(i + 1)
                    dve.wait_ge(xs_hi, 8 * z + i + 1)
                    dve.tensor_tensor(xs[:, 2 * i:2 * i + 2, T:2 * T], t1[:, i % 2, :].rearrange("p (a t) -> p a t", a=2),
                                      xs[:, 2 * i:2 * i + 2, 0:T].bitcast(F32), ALU.subtract).then_inc(xs_lo, 1)

            def hidden_lo(h, tile, b):
                dve.wait_ge(hid_hi, h * 2 + (b + 1))
                dve.tensor_tensor(hs[:, bass.ds(tile + 2 * b, 2), T:2 * T], t1[:, b, :].rearrange("p (a t) -> p a t", a=2),
                                  hs[:, bass.ds(tile + 2 * b, 2), 0:T].bitcast(F32), ALU.subtract).then_inc(hid_lo, 1)

            def add_up(j, a, tile):
                dve.wait_ge(unit_used, j * GU + GU)
                for b in range(2):
                    o = acc[:, bass.ds(tile + 2 * b, 2), :]
                    dve.tensor_tensor(o, bank[2 * a + b][:, :].rearrange("p (a t) -> p a t", a=2), o, ALU.add
                                      ).then_inc(bank_free, 1)

            def gated_into_x(n_done, a, tile, gate):
                dve.wait_ge(unit_used, n_done)
                for m in range(MT):
                    o = x[:, bass.ds(tile + m, 1), :]
                    ins = dve.scalar_tensor_tensor(out=o, in0=bank[2 * a + m // 2][:, (m % 2) * T:(m % 2 + 1) * T],
                                                   scalar=mod[:, gate, bass.ds(tile + m, 1)], in1=o,
                                                   op0=ALU.mult, op1=ALU.add)
                    if m % 2:
                        ins.then_inc(bank_free, 1)

            def scaled_v(g):
                for b in range(2):
                    ins = dve.tensor_scalar(vs[:, b, :], vtok[:, b, bass.ds(g * NC, NC)], rv[:, b:b + 1], None, ALU.mult)
                ins.then_inc(vs_ready, 1)

            def spatial_gate(j, g, h, tile):
                for b in range(2):
                    dve.wait_ge(mixs_ready, g * 2 + (b + 1))
                    for m in range(2):
                        o = t1[:, b, m * T:(m + 1) * T].rearrange("p (c q) -> p c q", c=2)
                        ins = dve.scalar_tensor_tensor(
                            out=o, in0=mis[b][:, m * T:(m + 1) * T].rearrange("p (c q) -> p c q", c=2),
                            scalar=gv[:, bass.ds(g * 4 + (2 * b + m), 1)],
                            in1=bs[:, bass.ds(g * 2 + b, 1), :].to_broadcast([P, 2, P]), op0=ALU.mult, op1=ALU.add)
                    link(ins)
                    dve.wait_ge(bank_free, j * 2 + (b + 1))
                    dve.tensor_tensor(t1[:, b, :], t1[:, b, :], t0[:, b, :], ALU.mult).then_inc(prod_ready, 1)
                for b in range(2):
                    hidden_lo(h, tile, b)

            def conv(j, a, pair, off):
                for b in range(2):
                    dve.wait_ge(zt_ready, pair * 4 + (b + 1 + (2 if off else 0)))
                    for tap in (0, 2):
                        for m in range(2):
                            tile = pair * 4 + (off + 2 * b + m)
                            o = zt[:, 2 * b + m, 1:T] if tap == 0 else zt[:, 2 * b + m, 0:T - 1]
                            s = m * T + (0 if tap == 0 else 1)
                            ins = dve.scalar_tensor_tensor(out=o, in0=bank[2 * a + b][:, s:s + T - 1],
                                                           scalar=cw[:, bass.ds(tile, 1), tap], in1=o,
                                                           op0=ALU.mult, op1=ALU.add)
                        if tap == 0:
                            link(ins)
                    ins.then_inc(bank_free, 1)

            def gate(j, a, pair):
                conv(j, a, pair, 0)
                for b in range(2):
                    dve.wait_ge(sg_ready, pair * 2 + (b + 1))
                    g2 = gt[:, 2 * b:2 * b + 2, :]
                    dve.tensor_tensor(g2, g2, zt[:, 2 * b:2 * b + 2, :], ALU.mult).then_inc(gate_ready, 1)

            def value(j, a, pair, h, tile):
                conv(j, a, pair, FF2T)
                for b in range(2):
                    dve.wait_ge(bank_free, j * 2 + (b + 1))
                    dve.tensor_tensor(t1[:, b, :].rearrange("p (a t) -> p a t", a=2), gt[:, 2 * b:2 * b + 2, :],
                                      zt[:, 2 * b:2 * b + 2, :], ALU.mult).then_inc(prod_ready, 1)
                for b in range(2):
                    hidden_lo(h, tile, b)

            def prep(hf):
                dve.wait_ge(h_sg, hf + 1)
                if hf:
                    dve.wait_ge(h_sc, len(LEVELS) + 1)
                link(dve.tensor_scalar(kk[:, :], sgf[:, :], -1.0, 1.0, ALU.mult, ALU.add))
                for h in range(4):
                    hh, c = 4 * hf + h, slice(h * T, (h + 1) * T)
                    ins = dve.tensor_scalar(fft[:, c], sgf[:, c], oml[:, hh:hh + 1], lbt[:, hh:hh + 1], ALU.mult, ALU.add)
                ins.then_inc(h_ff, 1)
                for h in range(4):
                    hh, c = 4 * hf + h, slice(h * T, (h + 1) * T)
                    ins = dve.tensor_scalar(kk[:, c], kk[:, c], oml[:, hh:hh + 1], None, ALU.mult)
                link(ins)
                dve.wait_ge(h_ln, hf + 1)
                for s in range(8):
                    c = slice(s * P, (s + 1) * P)
                    ins = dve.tensor_tensor_scan(bb[:, c], ones128, lgf[:, c], 0.0, ALU.mult, ALU.add)
                link(ins)

            def halves(ap, m):
                return ap.rearrange("p (n s m) -> p n s m", s=2, m=m)

            def args(hf, l):
                i, m = half_level(hf, l), LEVELS[l]
                n = 4 * T // (2 * m)
                if i >= 2:
                    dve.wait_ge(h_ops, i - 1)
                v = halves(bb[:, :], m)
                end = v[:, :, 0, m - 1:m].to_broadcast([P, n, m])
                o = arg[:, i % 2, :, :].rearrange("p s (n m) -> p s n m", m=m)
                dve.tensor_tensor(o[:, 0], end, v[:, :, 0, :], ALU.subtract)
                if m == 128:
                    dve.tensor_copy(o[:, 1], v[:, :, 1, :]).then_inc(h_arg, 1)
                else:
                    dve.tensor_tensor(o[:, 1], v[:, :, 1, :], end, ALU.subtract).then_inc(h_arg, 1)

            def operands(hf, l):
                i = half_level(hf, l)
                if l == len(LEVELS):
                    dve.nop().then_inc(h_ops, 1)
                    return
                m = LEVELS[l]
                dve.wait_ge(h_exp, hf * 8 + l + 1)
                if i >= 2:
                    dve.wait_ge(h_sc, i - 1)
                e = arg[:, i % 2, :, :].rearrange("p s (n m) -> p s n m", m=m)
                dve.tensor_tensor(halves(kl[:, i % 2, :], m)[:, :, 0, :], halves(kk[:, :], m)[:, :, 0, :], e[:, 0], ALU.mult)
                qh = qq[:, 4 * hf:4 * hf + 4, :].rearrange("p h t -> p (h t)")
                dve.tensor_tensor(qe[:, i % 2, :].rearrange("p (n m) -> p n m", m=m), halves(qh, m)[:, :, 1, :], e[:, 1],
                                  ALU.mult).then_inc(h_ops, 1)

            def keep(hf, l):
                i = half_level(hf, l)
                dve.wait_ge(h_sc, i + 1)
                if l >= 2:
                    dve.wait_ge(h_evac, i)
                if l == len(LEVELS):
                    for tt in range(2):
                        ins = dve.copy_predicated(sc[:, hf, tt, :, :],
                                                  mk[:, NM - P:].rearrange("p (o t) -> p o t", o=1).to_broadcast([P, 4, P]),
                                                  mis[2 + tt][:, :].rearrange("p (h t) -> p h t", h=4))
                    ins.then_inc(h_evac, 1)
                    return
                m, b = LEVELS[l], mis[i % 2]
                if m == 128:
                    dve.tensor_copy(sc[:, hf, 2, :, :], b[:, :].rearrange("p (h t) -> p h t", h=4)).then_inc(h_evac, 1)
                    return
                mask = mk[:, (l - 1) * 64:l * 64].rearrange("p (n m) -> p n m", m=m)
                n = 64 // m
                for tt in range(2):
                    for h in range(4):
                        o = halves(sc[:, hf, tt, h, :], m)[:, :, 1, :]
                        d = b[:, (2 * h + tt) * 64:(2 * h + tt + 1) * 64].rearrange("p (n m) -> p n m", m=m)
                        ins = dve.copy_predicated(o, mask, d)
                ins.then_inc(h_evac, 1)

            def pooled():
                dve.wait_ge(bank_free, 16)
                link(dve.tensor_tensor(sa[:, :, 1:], uu[:, :, 1:], uu[:, :, :PW - 1], ALU.add))
                link(dve.tensor_tensor(sb_[:, 2:, 3:], sa[:, 2:, 3:], sa[:, 2:, 1:PW - 2], ALU.add))
                link(dve.tensor_tensor(sa[:, 4:, 7:], sb_[:, 4:, 7:], sb_[:, 4:, 3:PW - 4], ALU.add))
                link(dve.tensor_tensor(sb_[:, 6:, 15:], sa[:, 6:, 15:], sa[:, 6:, 7:PW - 8], ALU.add))
                for g in range(4):
                    s = (sa, sb_)[g % 2]
                    o = s[:, 2 * g:2 * g + 2, PAD:PAD + 16]
                    ins = dve.tensor_tensor(o, o, cor[:, g:g + 1, :].to_broadcast([P, 2, 16]), ALU.mult)
                link(ins)
                for g, w in enumerate(WINDOWS):
                    s = (sa, sb_)[g % 2]
                    o = uu[:, 2 * g:2 * g + 2, PAD:]
                    ins = dve.scalar_tensor_tensor(out=o, in0=s[:, 2 * g:2 * g + 2, PAD:], scalar=1.0 / w, in1=o,
                                                   op0=ALU.mult, op1=ALU.subtract)
                ins.then_inc(p_d, 1)

            def mix_lower(i):
                src = mixf if i < 4 else oo
                i4 = i % 4
                dve.wait_ge(mix_hi, i + 1)
                dve.tensor_tensor(hs[:, 2 * i:2 * i + 2, T:2 * T], src[:, 2 * i4:2 * i4 + 2, :],
                                  hs[:, 2 * i:2 * i + 2, 0:T].bitcast(F32), ALU.subtract).then_inc(mix_lo, 1)

            def pool_out():
                dve.wait_ge(p_mm, 1)
                for e in range(POOLT):
                    ins = dve.tensor_scalar(mixf[:, e, :], mis[e // 2][:, (e % 2) * T:(e % 2 + 1) * T], pp[:, 0, e:e + 1],
                                            pp[:, 1, e:e + 1], ALU.add, ALU.mult)
                    if e % 2:
                        ins.then_inc(mix_t, 1)

            def head_norm():
                dve.wait_ge(h_gs, 1)
                dve.wait_ge(h_oc, 2)
                dve.tensor_tensor(oo[:, :, :], oo[:, :, :], fg[:, :, :], ALU.mult).then_inc(h_og, 1)
                dve.wait_ge(h_ss, 1)
                for i in range(4):
                    ins = dve.tensor_scalar(sq8[:, 2 * i:2 * i + 2, :], mis[i][:, :].rearrange("p (a t) -> p a t", a=2),
                                            float(D // HD), EPS, ALU.mult, ALU.add)
                ins.then_inc(h_va, 1)
                dve.wait_ge(h_sd, 1)
                link(dve.reciprocal(sq8[:, :, :], sq8[:, :, :]))
                for h in range(HEADS):
                    ins = dve.scalar_tensor_tensor(out=oo[:, h, :], in0=oo[:, h, :], scalar=pp[:, 2, h:h + 1],
                                                   in1=sq8[:, h, :], op0=ALU.mult, op1=ALU.mult)
                    if h % 2:
                        ins.then_inc(mix_t, 1)

            dve.memset(inv[:, :], 1.0 / D)
            dve.memset(one[:, :], 1.0).then_inc(cst, 1)
            dve.memset(t1[:, :, :], 0.0).then_inc(hid_lo, 2)
            dve.memset(kl[:, :, :], 0.0)
            ones128_t = place("ones128_t", o_hs + 31 * KB, [P, P])
            ones128 = ones128_t[:, :]
            dve.memset(ones128, 1.0)
            link(dve.memset(sc[:, :, :, :, :], 0.0))
            dve.wait_ge(x_arrived, 16)
            dve.wait_ge(par_arrived, 16 * 5)
            root(0)
            make_xs(0, gain[:, 0, :])
            dve.wait_ge(mix_arrived, 16 * 5)
            link(dve.tensor_tensor(lbm[:, :], lb2[:, 0, :], lb2[:, 1, :], ALU.max))
            link(dve.tensor_tensor(lb2[:, 0, :], lb2[:, 0, :], lbm[:, :], ALU.subtract))
            dve.tensor_tensor(lb2[:, 1, :], lb2[:, 1, :], lbm[:, :], ALU.subtract).then_inc(lb_s, 1)
            dve.wait_ge(silu_e, 1)
            link(dve.tensor_tensor(sc_c[:, :], sc_c[:, :], cf[:, :], ALU.mult))
            dve.wait_ge(lb_s, 2)
            link(dve.tensor_tensor(lbm[:, :], lb2[:, 0, :], lb2[:, 1, :], ALU.add))
            link(dve.reciprocal(lbm[:, :], lbm[:, :]))
            link(dve.tensor_tensor(lbt[:, :], lb2[:, 0, :], lbm[:, :], ALU.mult))
            link(dve.tensor_scalar(oml[:, :], lbt[:, :], -1.0, 1.0, ALU.mult, ALU.add))
            for i in range(RING):
                split(i, i)
            for j in range(G_OUT):
                def after(i, j=j):
                    for hf, j0 in ((0, 2), (1, 4)):
                        l = (j - j0) * 8 + i
                        if l == 0:
                            prep(hf)
                            args(hf, 0)
                        if 1 <= l <= len(LEVELS):
                            if l < len(LEVELS):
                                args(hf, l)
                            operands(hf, l - 1)
                        if l == len(LEVELS) + 1:
                            operands(hf, l - 1)
                        if 3 <= l <= len(LEVELS) + 3:
                            keep(hf, l - 3)
                    if (j, i) == (6, 0):
                        dve.wait_ge(h_sc, 18)
                        dve.memset(uu[:, :, 0:PAD], 0.0)
                        link(dve.memset(sa[:, :, 0:PAD], 0.0))
                        dve.memset(sb_[:, :, 0:PAD], 0.0).then_inc(ms_ready, 1)
                    if (j, i) == (8, 0):
                        pooled()
                    if (j, i) == (8, 6):
                        pool_out()
                        for k in range(4):
                            mix_lower(k)

                def evac(j=j):
                    if j == G_OUT - 1:
                        head_norm()
                        for k in range(4, 8):
                            mix_lower(k)
                body(j * GU, evac, after=after)
            for g in range(4):
                body((G_OUT + g) * GU, lambda: None)
            root(1)
            normed_into_x(1)
            root(2)
            dve.memset(acc[:, :, :], 0.0)
            link(dve.memset(aacc[:, :], 0.0))
            make_xs(1, gain[:, 2, :])
            with dve.Fori(0, 4) as q, step.loop(q, 4, 1):
                with dve.Fori(0, 2) as p:
                    for a in range(2):
                        j = q * 8 + p * 2 + (G_MLP + a)
                        g = q * 8 + p * 2 + a
                        h = q * 4 + p * 2 + a
                        body(j * GU, lambda: [hidden_lo(h, p * 8 + 4 * a, b) for b in range(2)],
                             k=g * ADA_PER_GROUP, kt=p * 4 + 2 * a)
                with dve.Fori(0, 2) as p:
                    for a in range(2):
                        j = q * 8 + p * 2 + (G_MLP + 4 + a)
                        g = q * 8 + p * 2 + (4 + a)
                        body(j * GU, lambda: add_up(j, a, p * 8 + 4 * a), k=g * ADA_PER_GROUP, kt=p * 4 + (8 + 2 * a))
                ada_take(q)
            root(3)
            normed_into_x(3)
            root(4)
            dve.nop().then_inc(acc_copied, 1)
            link(dve.scalar_tensor_tensor(out=geff[:, :], in0=mod[:, 1, :], scalar=1.0, in1=gain[:, 4, :],
                                          op0=ALU.add, op1=ALU.mult))
            make_xs(2, geff[:, :], shift=mod[:, 0, :])
            with dve.Fori(0, 4) as p:
                for a in range(2):
                    j = p * 2 + (G_AV + a)
                    body(j * GU, lambda: None, k=(p * 2 + (32 + a)) * ADA_PER_GROUP, kt=p * 4 + 2 * a)
            ada_take(4)
            dve.wait_ge(ssv_ready, 1)
            for b in range(2):
                ins = dve.tensor_reduce(rv[:, b:b + 1], ssv[:, b, :], AX.X, ALU.add)
            link(ins)
            dve.tensor_scalar(rv[:, :], rv[:, :], 1.0 / AV, EPS, ALU.mult, ALU.add).then_inc(var_v, 1)
            dve.wait_ge(sd_v, 1)
            link(dve.reciprocal(rv[:, :], rv[:, :]))
            dve.wait_ge(ws_arrived, 32)
            for half in range(2):
                with dve.Fori(0, 2) as p, step.loop(p, 2, 4):
                    for a in range(2):
                        j = p * 2 + (G_AU + 8 * half + a)
                        g = p * 2 + (4 * half + a)
                        kw = dict(k=(p * 2 + (40 + a)) * ADA_PER_GROUP, kt=p * 4 + 2 * a) if half == 0 else {}
                        body(j * GU, lambda: spatial_gate(j, g, g + H_A, p * 8 + 4 * a), pre=lambda: scaled_v(g), **kw)
                with dve.Fori(0, 2) as p:
                    for a in range(2):
                        j = p * 2 + (G_AU + 8 * half + 4 + a)
                        kw = dict(k=(p * 2 + (44 + a)) * ADA_PER_GROUP, kt=p * 4 + (8 + 2 * a)) if half == 0 else {}
                        body(j * GU, lambda: gated_into_x(j * GU + GU, a, p * 8 + 4 * a, 2), **kw)
                if half == 0:
                    ada_take(5)
            root(5)
            link(dve.scalar_tensor_tensor(out=geff[:, :], in0=mod[:, 4, :], scalar=1.0, in1=gain[:, 5, :],
                                          op0=ALU.add, op1=ALU.mult))
            make_xs(3, geff[:, :], shift=mod[:, 3, :])
            with dve.Fori(0, 2) as c, step.loop(c, 2, 16):
                with dve.Fori(0, 4) as p, step.loop(p, 4, 4):
                    j = c * 12 + p * 2 + G_FF
                    pair = c * 4 + p
                    body(j * GU, lambda: gate(j, 0, pair))
                    body((j + 1) * GU, lambda: value(j + 1, 1, pair, pair + H_F, p * 4))
                with dve.Fori(0, 2) as p:
                    for a in range(2):
                        j = c * 12 + p * 2 + (G_FF + 8 + a)
                        body(j * GU, lambda: gated_into_x(j * GU + GU, a, p * 8 + 4 * a, 5))
            with dve.Fori(0, 3) as p, step.loop(p, 3, 4):
                j = p * 2 + G_FT
                body(j * GU, lambda: gate(j, 0, p + 8))
                body((j + 1) * GU, lambda: value(j + 1, 1, p + 8, p + (H_F + 8), p * 4))
            for g in range(4):
                n = G_DT * GU + g * DTU
                body(n, lambda: gated_into_x(n + DTU, g % 2, 4 * g, 5), units=DTU, s0=2 * (g % 2))
            root(6)
            for t in range(KT):
                ins = dve.scalar_tensor_tensor(out=acc[:, t, :], in0=x[:, t, :], scalar=gain[:, 6, t:t + 1],
                                               in1=rstd[:, :], op0=ALU.mult, op1=ALU.mult)
            ins.then_inc(out_ready, 1)


def kernel(**inputs):
    import numpy as np
    import concourse.bacc as bacc
    from concourse.bass_utils import run_bass_kernel_spmd as run

    def get(name):
        return np.asarray(inputs[name])

    def units(w, cols, rows=None):
        w = w if rows is None else w[rows[0]:rows[1]]
        k = w.shape[0] // (UK * P)
        return [w[:, c:c + NC].reshape(k, UK, P, NC).transpose(0, 2, 1, 3).reshape(k, P, UW) for c in cols]

    w_in, w_out = get("w_in")[0], get("w_out")[0]
    w1, w2 = get("w_mlp_in")[0], get("w_mlp_out")[0]
    aw, ao = get("a_w_in_2")[0], get("a_w_out_2")[0]
    fu, fd = get("ffn_w_up_2")[0], get("ffn_w_down_2")[0]
    all4 = [0, NC, 2 * NC, 3 * NC]
    s = []
    s += units(w_in, [2048, 1024, 2560, 1536, 3072, 3584, 0, 512, 4096, 4608])
    s += units(w_out, all4)
    for q in range(4):
        s += units(w1, [q * D + c for c in all4])
        s += units(w2, all4, (q * D, (q + 1) * D))
    s += units(aw, [AV + NC * i for i in range(8)])
    for h in range(2):
        s += units(aw, [h * D + c for c in all4])
        s += units(ao, all4, (h * D, (h + 1) * D))
    for c in range(3):
        for p in range(4 if c < 2 else 3):
            s += units(fu, [c * D + p * NC, FF2T * P + c * D + p * NC])
        s += units(fd, all4, (c * D, min((c + 1) * D, FF2T * P)))
    wstream = np.concatenate(s)
    ada = get("ada_w_2")[0].reshape(KT, P, 6, 2, UW).transpose(2, 0, 3, 1, 4).reshape(-1, P, UW)

    def cols(v):
        return v.reshape(-1, P).T

    gains = np.stack([cols(get("norm_mix_pre")[0]), cols(get("norm_mix_post")[0]), cols(get("norm_mlp_pre")[0]),
                      cols(get("norm_mlp_post")[0]), cols(get("norm_g_2")[0, 0]), cols(get("norm_g_2")[0, 1]),
                      cols(get("final_g_2"))], axis=1)
    cw = np.stack([cols(get("ffn_conv_w_2")[0, i]) for i in range(3)] + [cols(get("ffn_conv_b_2")[0])], axis=2)
    masks = np.zeros((P, 7 * 64 + P), np.int32)
    for l, m in enumerate(LEVELS[1:]):
        for t in range(64):
            blk = t // m
            masks[2 * m * blk:2 * m * blk + m, l * 64 + t] = 1
    masks[np.arange(P), 7 * 64 + np.arange(P)] = 1
    corr = np.ones((P, 4, 16), np.float32)
    for g, w in enumerate(WINDOWS):
        for t in range(w - 1):
            corr[:, g, t] = w / (t + 1)
    arrays = {
        "xT": get("x")[0].T.reshape(KT, P, T).transpose(1, 0, 2),
        "wstream": wstream,
        "astream": ada,
        "cT": cols(get("c_2")[0]),
        "adab": get("ada_b_2")[0].reshape(6, KT, P).transpose(2, 0, 1),
        "gains": gains,
        "cwp": cw,
        "gvp": cols(get("a_g_v_2")[0]),
        "bsp": get("a_b_s_2")[0],
        "wsT": get("a_w_s_2")[0].transpose(2, 0, 1),
        "poolw": get("pool_w")[0].reshape(4, 2, P, T).transpose(2, 0, 1, 3).reshape(P, 8, T),
        "poolp": np.stack([cols(get("pool_b")[0].reshape(-1)), cols(get("pool_scale")[0]), cols(get("hgrn_norm_w")[0])], axis=1),
        "lbl": get("lb_logits").reshape(2, HEADS, HD).transpose(2, 0, 1),
        "masks": masks,
        "corr": corr,
    }
    nc = bacc.Bacc("TRN2", target_bir_lowering=False, num_devices=1)
    args = []
    for name, a in arrays.items():
        a = arrays[name] = np.ascontiguousarray(a)
        args.append(nc.dram_tensor(name, a.shape, mybir.dt.from_np(a.dtype), kind="ExternalInput").ap())
    args.append(nc.dram_tensor("outT", (P, KT, T), F32, kind="ExternalOutput").ap())
    build(nc, *args)
    r = run(nc, [arrays], core_ids=[0])
    return r.results[0]["outT"].transpose(2, 1, 0).reshape(1, T, D)
```

```python
import concourse.bass as bass
from concourse import mybir
from contextlib import ExitStack, contextmanager

F32 = mybir.dt.float32
F32R = mybir.dt.float32r
I32 = mybir.dt.int32
ACT = mybir.ActivationFunctionType
ALU = mybir.AluOpType
AX = mybir.AxisListType

P = 128
T = 256
D = 2048
KT = D // P
NC = 512
MT = NC // P
UK = 2
UW = UK * NC
RING = 4
GU = KT // UK
EPS = 1e-6
SPAN = 218 * 1024
RING_OF_POOL = 1024
HEADS = 8
HD = 128
POOLT = 8
WINDOWS = (2, 4, 8, 16)
PAD = 16
LEVELS = (128, 64, 32, 16, 8, 4, 2, 1)
FF1 = 8192
FF2T = 5632 // P
AV = 4096

G_IN = 0
G_OUT = 10
G_MLP = 14
G_AV = G_MLP + 32
G_AU = G_AV + 8
G_FF = G_AU + 16
G_FT = G_FF + 24
G_DT = G_FT + 6
DTU = 6
UNITS = GU * G_DT + 4 * DTU
ADA_PER_GROUP = 4
ADA_GROUPS = 48
ADA_PER_VEC = 32
BY_POOL = (1, 3, 5, 6)
H_A, H_F = 16, 24


class Count:

    def __init__(self, sem):
        self.sem, self.done, self.off = sem, 0, 0

    def value(self):
        return self.off + self.done

    @contextmanager
    def loop(self, i, trips, per):
        off, done = self.off, self.done
        self.off = off + i * per
        yield
        assert self.done - done == per, (self.done - done, per)
        self.off, self.done = off, done + trips * per


def build(nc, xT, wstream, astream, cT, adab, gains, cwp, gvp, bsp, wsT, poolw, poolp, lbl, masks, corr, eye_in, out):
    ctx = ExitStack()
    with ctx:
        slab = ctx.enter_context(nc.sbuf_tensor("slab", [P, SPAN // 4], F32))
        base = nc.sbuf_base - SPAN
        at = [base]

        def region(size):
            o = at[0]
            at[0] += size
            assert at[0] <= base + SPAN, at[0] - base
            return o

        def place(name, offset, shape, dt=F32):
            return nc.alloc_sbuf_tensor_at(name, shape, dt, offset=offset)

        sem = lambda n: ctx.enter_context(nc.semaphore(n))
        KB = 1024
        raw = place("raw", region(16 * KB), [P, RING, UW])
        whi = place("whi", region(16 * KB), [P, RING, UW], F32R)
        wlo = place("wlo", region(16 * KB), [P, RING, UW], F32R)
        xs = place("xs", region(32 * KB), [P, KT, 2 * T], F32R)
        o_hs = region(32 * KB)
        hs = place("hs", o_hs, [P, KT, 2 * T], F32R)
        x = place("x", region(16 * KB), [P, KT, T])
        o_v = region(32 * KB)
        o_out = region(16 * KB)
        o_ada = region(16 * KB)
        o_vs = region(4 * KB)
        sqs = place("sqs", region(2 * KB), [P, 2 * T])
        t0 = place("t0", region(4 * KB), [P, 2, 2 * T])
        t1 = place("t1", region(4 * KB), [P, 2, 2 * T])

        vtok = place("vtok", o_v, [P, 2, AV])
        vs = place("vs", o_vs, [P, 2, NC])
        ws = place("ws", o_out, [P, 16, P])
        bs = place("bs", o_out + 8 * KB, [P, 16, P])
        zt = place("zt", o_v, [P, MT, T])
        gt = place("gt", o_v + 4 * KB, [P, MT, T])
        acc = place("acc", o_out, [P, KT, T])
        aring = place("aring", o_ada, [P, 2, UW])
        aacc = place("aacc", o_ada + 8 * KB, [P, D])
        rstd = place("rstd", o_vs, [P, T])
        ssa = place("ssa", o_vs + KB, [P, T])
        ssb = place("ssb", o_vs + 2 * KB, [P, T])

        fg = place("fg", o_v, [P, HEADS, T])
        qq = place("qq", o_v + 8 * KB, [P, HEADS, T])
        mixf = place("mixf", o_v + 8 * KB, [P, HEADS, T])
        vv = place("vv", o_v + 16 * KB, [P, 2, HEADS * HD])
        oo = place("oo", o_v + 24 * KB, [P, HEADS, T])
        kk = place("kk", o_out, [P, 4 * T])
        bb = place("bb", o_out + 4 * KB, [P, 4 * T])
        kl = place("kl", o_out + 8 * KB, [P, 2, 4 * T])
        arg = place("arg", o_ada, [P, 2, 2, 2 * T])
        qe = place("qe", o_ada + 8 * KB, [P, 2, 2 * T])
        lgf = place("lgf", o_ada + 12 * KB, [P, 4 * T])
        PW = PAD + T
        uu = place("uu", o_out, [P, POOLT, PW])
        sa = place("sa", o_out + 9 * KB, [P, POOLT, PW])
        sb_ = place("sb_", o_out + 18 * KB, [P, POOLT, PW])
        sq8 = place("sq8", o_out + 9 * KB, [P, HEADS, T])
        sc = place("sc", o_hs, [P, 2, 3, 4, P])
        pw = place("pw", o_hs + 12 * KB, [P, 8, T])
        sgf = place("sgf", o_hs + 20 * KB, [P, 4 * T])
        fft = place("fft", o_hs + 24 * KB, [P, 4 * T])
        NM = 7 * 64 + P
        mk = place("mk", o_hs + 28 * KB, [P, NM], I32)

        gain = place("gain", region(7 * 64), [P, 7, KT])
        cw = place("cw", region(2 * FF2T * 4 * 4), [P, 2 * FF2T, 4])
        gv = place("gv", region(128), [P, 32])
        ab = place("ab", region(6 * 64), [P, 6, KT])
        mod = place("mod", region(6 * 64), [P, 6, KT])
        sc_c = place("sc_c", region(64), [P, KT])
        geff = place("geff", region(64), [P, KT])
        asum = place("asum", region(64), [P, KT])
        eye = place("eye", region(512), [P, P])
        inv = place("inv", region(512), [P, P])
        one = place("one", region(32), [P, 1])
        junk = place("junk", region(32), [P, 1])
        ssv = place("ssv", region(64), [P, 2, 8])
        rv = place("rv", region(32), [P, 2])
        pp = place("pp", o_vs + 3 * KB, [P, 3, 8])
        lb2 = place("lb2", o_vs + 3 * KB + 96, [P, 2, 8])
        lbt = place("lbt", o_vs + 3 * KB + 160, [P, 8])
        oml = place("oml", o_vs + 3 * KB + 192, [P, 8])
        lbm = place("lbm", o_vs + 3 * KB + 224, [P, 8])
        cor = place("cor", o_vs + 3 * KB + 256, [P, 4, 16])
        cf = place("cf", o_vs + 3 * KB + 512, [P, KT])

        bank = [ctx.enter_context(nc.psum_tensor(f"bank{i}", [P, NC], F32)) for i in range(4)]
        mis = [ctx.enter_context(nc.psum_tensor(f"mis{i}", [P, NC], F32)) for i in range(4)]

        raw_arrived = [sem(f"raw_arrived{i}") for i in range(RING)]
        ada_arrived = [sem(f"ada_arrived{i}") for i in range(2)]
        x_arrived = [sem(f"x_arrived{i}") for i in range(4)]
        par_arrived = sem("par_arrived")
        mix_arrived = sem("mix_arrived")
        ws_arrived = sem("ws_arrived")
        out_sent = sem("out_sent")
        hi_ready = sem("hi_ready")
        lo_ready = sem("lo_ready")
        unit_used = sem("unit_used")
        bank_free = sem("bank_free")
        hid_hi = sem("hid_hi")
        hid_lo = sem("hid_lo")
        prod_ready = sem("prod_ready")
        mixs_ready = sem("mixs_ready")
        vs_ready = sem("vs_ready")
        zt_ready = sem("zt_ready")
        sg_ready = sem("sg_ready")
        gate_ready = sem("gate_ready")
        ada_used = sem("ada_used")
        ada_sum = sem("ada_sum")
        ada_read = sem("ada_read")
        sq_ready = sem("sq_ready")
        sq_used = sem("sq_used")
        sq_sum = sem("sq_sum")
        var_ready = sem("var_ready")
        sd_ready = sem("sd_ready")
        nt_ready = sem("nt_ready")
        xs_hi = sem("xs_hi")
        xs_lo = sem("xs_lo")
        mix_t = sem("mix_t")
        mix_hi = sem("mix_hi")
        mix_lo = sem("mix_lo")
        h_sg = sem("h_sg")
        h_ff = sem("h_ff")
        h_ln = sem("h_ln")
        h_arg = sem("h_arg")
        h_exp = sem("h_exp")
        h_ops = sem("h_ops")
        h_sc = sem("h_sc")
        h_evac = sem("h_evac")
        h_o = sem("h_o")
        h_oc = sem("h_oc")
        p_d = sem("p_d")
        p_mm = sem("p_mm")
        h_gs = sem("h_gs")
        h_og = sem("h_og")
        h_sq = sem("h_sq")
        h_ss = sem("h_ss")
        h_va = sem("h_va")
        h_sd = sem("h_sd")
        silu_e = sem("silu_e")
        lb_s = sem("lb_s")
        cst = sem("cst")
        out_ready = sem("out_ready")
        dve_step = sem("dve_step")
        act_step = sem("act_step")
        ms_ready = sem("ms_ready")
        x_sum = sem("x_sum")
        term_ready = sem("term_ready")
        lg_sum = sem("lg_sum")
        ssv_ready = sem("ssv_ready")
        var_v = sem("var_v")
        sd_v = sem("sd_v")

        def half_level(hf, l):
            return hf * (len(LEVELS) + 1) + l

        def two_before(hf, l):
            if l >= 2:
                return half_level(hf, l - 2)
            return half_level(0, len(LEVELS) - 2 + l) if hf else None

        block = ctx.enter_context(nc.Block())

        def halves(ap, m):
            return ap.rearrange("p (n s m) -> p n s m", s=2, m=m)

        @block.sync
        def _(sp):
            def unit(n, slot):
                if not (isinstance(n, int) and n < RING):
                    sp.wait_ge(lo_ready, n - RING + 1)
                sp.dma_start(raw[:, slot, :], wstream[bass.ds(n, 1), :, :].rearrange("o p w -> p (o w)")
                             ).then_inc(raw_arrived[slot], 16)

            def ada(k, slot, wait=True):
                if wait:
                    sp.wait_ge(ada_used, k - 1)
                sp.dma_start(aring[:, slot, :], astream[bass.ds(k, 1), :, :].rearrange("o p w -> p (o w)")
                             ).then_inc(ada_arrived[slot], 16)

            def group(n, k=None, first=False):
                for i in range(GU):
                    unit(n + i, i % RING)
                    if k is not None and i < ADA_PER_GROUP:
                        ada(k + i, i % 2, wait=not (first and i < 2))

            for i in range(4):
                sp.dma_start(x[:, 4 * i:4 * i + 4, :], xT[:, 4 * i:4 * i + 4, :]).then_inc(x_arrived[i], 16)
            for dst, src in ((gain, gains), (cw, cwp), (gv, gvp), (ab, adab), (cf, cT), (eye, eye_in)):
                sp.dma_start(dst[:], src).then_inc(par_arrived, 16)
            for i in range(RING):
                unit(i, i)
            for dst, src in ((pw, poolw), (pp, poolp), (lb2, lbl), (mk, masks), (cor, corr)):
                sp.dma_start(dst[:], src).then_inc(mix_arrived, 16)
            with sp.Fori(0, G_MLP) as g:
                group(g * GU + RING)
            sp.wait_ge(mix_lo, 8)
            group(G_MLP * GU + RING, 0, first=True)
            with sp.Fori(1, 32) as g:
                group(g * GU + (G_MLP * GU + RING), g * ADA_PER_GROUP)
            sp.wait_ge(x_sum, 16)
            sp.dma_start(ws[:], wsT).then_inc(ws_arrived, 16)
            sp.dma_start(bs[:], bsp.rearrange("(o g) q -> o g q", o=1).to_broadcast([P, 16, P])
                         ).then_inc(ws_arrived, 16)
            with sp.Fori(32, ADA_GROUPS) as g:
                group(g * GU + (G_MLP * GU + RING), g * ADA_PER_GROUP)
            with sp.Fori(G_MLP + ADA_GROUPS, G_DT) as g:
                group(g * GU + RING)
            for n in range(G_DT * GU + RING, UNITS):
                unit(n, n % RING)
            for i in range(4):
                sp.wait_ge(out_ready, i + 1)
                sp.dma_start(out[:, 4 * i:4 * i + 4, :], acc[:, 4 * i:4 * i + 4, :]).then_inc(out_sent, 16)
            sp.wait_ge(out_sent, 64)

        @block.tensor
        def _(pe):
            def feature_unit(src, kt0, n, slot, first, last, pb, wait=None):
                if wait is not None:
                    pe.wait_ge(*wait)
                pe.wait_ge(lo_ready, n + 1)
                for k in range(UK):
                    for m in range(MT):
                        o = bank[pb + m // 2][:, (m % 2) * T:(m % 2 + 1) * T]
                        c = slice(k * NC + m * P, k * NC + (m + 1) * P)
                        h, l = src[:, kt0 + k, 0:T], src[:, kt0 + k, T:2 * T]
                        st = first and k == 0 and m % 2 == 0
                        sp_ = last and k == UK - 1
                        pe.matmul(o, whi[:, slot, c], h, start=st, stop=False, skip_group_check=True)
                        pe.matmul(o, whi[:, slot, c], l, start=False, stop=False, skip_group_check=True)
                        mm = pe.matmul(o, wlo[:, slot, c], h, start=False, stop=sp_, skip_group_check=True)
                mm.then_inc(unit_used, 1)

            def token_unit(kt0, n, slot, first, last, pb, wait=None):
                if wait is not None:
                    pe.wait_ge(*wait)
                pe.wait_ge(lo_ready, n + 1)
                for k in range(UK):
                    c = slice(k * NC, (k + 1) * NC)
                    for b in range(2):
                        o = bank[pb + b][:, :]
                        h = xs[:, kt0 + k, b * P:(b + 1) * P]
                        l = xs[:, kt0 + k, T + b * P:T + (b + 1) * P]
                        pe.matmul(o, h, whi[:, slot, c], start=first and k == 0, stop=False)
                        pe.matmul(o, l, whi[:, slot, c], start=False, stop=False)
                        mm = pe.matmul(o, h, wlo[:, slot, c], start=False, stop=last and k == UK - 1)
                mm.then_inc(unit_used, 1)

            def group(j, src, pb, n=None, wait=None, token=False, units=GU, s0=0, between=None):
                n = j * GU if n is None else n
                if not (isinstance(j, int) and j < 2):
                    pe.wait_ge(bank_free, j * 2 - 2)
                for u in range(units):
                    w = wait(u) if wait else None
                    if token:
                        token_unit(UK * u, n + u, (s0 + u) % RING, u == 0, u == units - 1, pb, w)
                    else:
                        feature_unit(src, UK * u, n + u, (s0 + u) % RING, u == 0, u == units - 1, pb, w)
                    if between:
                        between(u)

            def stats(s):
                for i in range(8):
                    pe.wait_ge(sq_ready, 8 * s + i + 1)
                    pe.matmul(mis[2][:, :], inv[:, :], t0[:, i % 2, :], start=i == 0, stop=i == 7
                              ).then_inc(sq_used, 1)

            def stats_of_sum(s):
                pe.wait_ge(sq_used, 8 * s + 8)
                pe.matmul(mis[2][:, :], inv[:, :], sqs[:, :], start=True, stop=True).then_inc(sq_sum, 1)

            def ada_reduce(m):
                def between(u):
                    if u == 5:
                        pe.wait_ge(ada_used, m * ADA_PER_VEC + ADA_PER_VEC)
                    if u in (5, 6):
                        for c in range(8 * (u - 5), 8 * (u - 4)):
                            mm = pe.transpose(mis[c // MT][:, (c % MT) * P:(c % MT + 1) * P],
                                              aacc[:, c * P:(c + 1) * P], eye[:, :])
                        mm.then_inc(ada_sum, 1)
                return between

            def level(hf, l):
                i = l % 2
                b = mis[i]
                pe.wait_ge(h_ops, hf * 8 + l + 1)
                if two_before(hf, l) is not None:
                    pe.wait_ge(h_evac, two_before(hf, l) + 1)
                if LEVELS[l] == 128:
                    for h in range(4):
                        mm = pe.matmul(b[:, h * P:(h + 1) * P], kl[:, i, h * T:h * T + P],
                                       qe[:, i, h * P:(h + 1) * P], start=True, stop=True)
                else:
                    for s in range(8):
                        h, tt = s // 2, s % 2
                        mm = pe.matmul(b[:, s * 64:(s + 1) * 64],
                                       kl[:, i, h * T + tt * P:h * T + (tt + 1) * P],
                                       qe[:, i, s * 64:(s + 1) * 64], start=True, stop=True)
                mm.then_inc(h_sc, 1)

            def diagonal(hf):
                pe.wait_ge(lg_sum, hf + 1)
                if hf:
                    pe.wait_ge(h_evac, half_level(0, len(LEVELS)) + 1)
                for s in range(8):
                    h, tt = s // 2, s % 2
                    mm = pe.matmul(mis[2 + tt][:, h * P:(h + 1) * P], kk[:, h * T + tt * P:h * T + (tt + 1) * P],
                                   qq[:, 4 * hf + h, tt * P:(tt + 1) * P], start=True, stop=True)
                mm.then_inc(h_sc, 1)

            def weigh(hf):
                pe.wait_ge(h_evac, half_level(hf, len(LEVELS)) + 1)
                pe.wait_ge(bank_free, 12)
                if hf == 0:
                    pe.wait_ge(h_evac, half_level(1, len(LEVELS)) + 1)
                for h in range(4):
                    hh = 4 * hf + h
                    b = mis[hh // 2]
                    o = (hh % 2) * T
                    v = [vv[:, c, hh * P:(hh + 1) * P] for c in range(2)]
                    pe.matmul(b[:, o:o + P], v[0], sc[:, hf, 0, h, :], start=True, stop=True)
                    pe.matmul(b[:, o + P:o + T], v[0], sc[:, hf, 2, h, :], start=True, stop=False)
                    mm = pe.matmul(b[:, o + P:o + T], v[1], sc[:, hf, 1, h, :], start=False, stop=True)
                mm.then_inc(h_o, 1)

            def pool():
                pe.wait_ge(p_d, 1)
                pe.wait_ge(h_oc, 2)
                for e in range(POOLT):
                    for k in range(2):
                        mm = pe.matmul(mis[e // 2][:, (e % 2) * T:(e % 2 + 1) * T],
                                       pw[:, 2 * (e // 2) + k, (e % 2) * P:(e % 2 + 1) * P],
                                       uu[:, 2 * (e // 2) + k, PAD:], start=k == 0, stop=k == 1)
                mm.then_inc(p_mm, 1)

            def head_stats(hf):
                pe.wait_ge(h_sq, hf + 1)
                pe.wait_ge(mix_t, 4)
                for i in range(2 * hf, 2 * hf + 2):
                    mm = pe.matmul(mis[i][:, :], inv[:, :], sq8[:, 2 * i:2 * i + 2, :], start=True, stop=True)
                mm.then_inc(h_ss, 1)

            pe.wait_ge(cst, 1)
            stats(0)
            xs0 = lambda z: (lambda u: (xs_lo, 8 * z + u + 1))
            work = {}
            for l in range(9):
                work[(2 + (l + 5) // 8, (l + 5) % 8)] = (0, l)
                work[(4 + (l + 5) // 8, (l + 5) % 8)] = (1, l)
            for j in range(G_OUT):
                def between(u, j=j):
                    if (j, u) in work:
                        hf, l = work[(j, u)]
                        level(hf, l) if l < len(LEVELS) else diagonal(hf)
                    if (j, u) == (6, 1):
                        weigh(0)
                        weigh(1)
                    if (j, u) == (8, 5):
                        pool()
                    if (j, u) == (9, 5):
                        head_stats(0)
                group(j, xs, 2 * (j % 2), wait=xs0(0), token=j in (4, 5), between=between)
            for g in range(4):
                def between(u, g=g):
                    if g == 0 and u == 1:
                        head_stats(1)
                group(G_OUT + g, hs, 2 * (g % 2), wait=lambda u: (mix_lo, u + 1), between=between)
            stats_of_sum(1)
            stats(2)
            with pe.Fori(0, 4) as q:
                with pe.Fori(0, 2) as p:
                    for a in range(2):
                        group(q * 8 + p * 2 + (G_MLP + a), xs, 2 * a, wait=xs0(1))
                for g in range(4):
                    group(q * 8 + (G_MLP + 4 + g), hs, 2 * (g % 2), between=ada_reduce(q) if g == 3 else None,
                          wait=lambda u: (hid_lo, q * 8 + (2 + 2 * (u // 2 + 1))))
            pe.wait_ge(ada_read, 4)
            stats_of_sum(3)
            stats(4)
            with pe.Fori(0, 3) as p:
                for a in range(2):
                    group(p * 2 + (G_AV + a), xs, 2 * a, wait=xs0(2), token=True)
            for a in range(2):
                group(G_AV + 6 + a, xs, 2 * a, wait=xs0(2), token=True, between=ada_reduce(4) if a else None)

            def spatial(g):
                pe.wait_ge(vs_ready, g + 1)
                pe.wait_ge(hid_lo, g * 2 + (2 + 2 * H_A))
                for t in range(MT):
                    for c in range(2):
                        mm = pe.matmul(mis[t // 2][:, (t % 2) * T + c * P:(t % 2) * T + (c + 1) * P],
                                       vs[:, c, t * P:(t + 1) * P], ws[:, bass.ds(g * 2 + t // 2, 1), :],
                                       start=True, stop=True)
                    if t % 2:
                        mm.then_inc(mixs_ready, 1)

            pe.wait_ge(ws_arrived, 32)
            for half in range(2):
                with pe.Fori(0, 2) as p:
                    for a in range(2):
                        group(p * 2 + (G_AU + 8 * half + a), xs, 2 * a, wait=xs0(2))
                        spatial(p * 2 + (4 * half + a))
                hid = lambda u: (hid_lo, 2 + 2 * (H_A + 4 * half + u // 2 + 1))
                with pe.Fori(0, 2 if half else 1) as p:
                    for a in range(2):
                        group(p * 2 + (G_AU + 8 * half + 4 + a), hs, 2 * a, wait=hid)
                if not half:
                    for a in range(2):
                        group(G_AU + 6 + a, hs, 2 * a, wait=hid, between=ada_reduce(5) if a else None)
            stats_of_sum(5)
            with pe.Fori(0, 2) as c:
                with pe.Fori(0, 4) as p:
                    for a in range(2):
                        group(c * 12 + p * 2 + (G_FF + a), xs, 2 * a, wait=xs0(3))
                with pe.Fori(0, 2) as p:
                    for a in range(2):
                        group(c * 12 + p * 2 + (G_FF + 8 + a), hs, 2 * a,
                              wait=lambda u: (hid_lo, c * 8 + (2 + 2 * (H_F + u // 2 + 1))))
            with pe.Fori(0, 3) as p:
                for a in range(2):
                    group(p * 2 + (G_FT + a), xs, 2 * a, wait=xs0(3))
            for g in range(4):
                group(G_DT + g, hs, 2 * (g % 2), n=G_DT * GU + g * DTU, units=DTU, s0=2 * (g % 2),
                      wait=lambda u: (hid_lo, 2 + 2 * (H_F + 8 + u // 2 + 1)))
            stats_of_sum(6)

        @block.scalar
        def _(act):
            step = Count(act_step)

            def link(ins):
                ins.then_inc(act_step, 1)
                step.done += 1
                act.wait_ge(act_step, step.value())

            def split(n, slot):
                act.wait_ge(raw_arrived[slot], rounds(n, slot))
                if not (isinstance(n, int) and n < RING):
                    act.wait_ge(unit_used, n - RING + 1)
                act.activation(whi[:, slot, :], raw[:, slot, :], ACT.Copy).then_inc(hi_ready, 1)

            def rounds(n, slot):
                return 16 * (n // RING + 1) if isinstance(n, int) else (n - slot) * 4 + 16

            def body(n, evac, units=GU, s0=0, after=None, late=False):
                for i in range(units):
                    if i == units - 1 and not late:
                        evac()
                    if isinstance(n, int) and n + RING + i >= UNITS:
                        continue
                    split(n + RING + i, (s0 + i) % RING)
                    if after:
                        after(i)
                if late:
                    evac()

            def squares(s, src, first=0, last=8, ready=None):
                if last == 8:
                    link(act.activation(junk[:, :], one[:, :], ACT.Sqrt))
                for i in range(first, last):
                    if ready is not None:
                        act.wait_ge(*ready(i))
                    if 8 * s + i - 1 > 0:
                        act.wait_ge(sq_used, 8 * s + i - 1)
                    act.activation(t0[:, i % 2, :], src[:, 2 * i:2 * i + 2, :], ACT.Square).then_inc(sq_ready, 1)

            def root(s):
                act.wait_ge(var_ready, s + 1)
                act.activation(ssa[:, :], ssb[:, :], ACT.Sqrt).then_inc(sd_ready, 1)

            def group_squares(s, src, j, g):
                squares(s, src, 2 * g, 2 * g + 2, ready=lambda i: (bank_free, 2 * j + 1 + i % 2))

            def split_xs(z, first=0, last=8, shift=None):
                for i in range(first, last):
                    act.wait_ge(nt_ready, 8 * z + i + 1)
                    if shift is not None:
                        for m in range(2):
                            t = 2 * i + m
                            ins = act.activation(xs[:, t, 0:T], t1[:, i % 2, m * T:(m + 1) * T], ACT.Identity,
                                                 bias=shift[:, t:t + 1])
                        ins.then_inc(xs_hi, 1)
                        continue
                    act.activation(xs[:, 2 * i:2 * i + 2, 0:T], t1[:, i % 2, :], ACT.Copy).then_inc(xs_hi, 1)

            def copy_out(dst, j, n, units=GU):
                act.wait_ge(unit_used, n + units)
                for b in range(2):
                    act.activation(dst(b), bank[2 * (j % 2) + b][:, :], ACT.Copy).then_inc(bank_free, 1)

            def relu2(j, h, a, tile):
                act.wait_ge(unit_used, j * GU + GU)
                for b in range(2):
                    act.wait_ge(hid_lo, h * 2 + (b + 1))
                    act.activation(t0[:, b, :], bank[2 * a + b][:, :], ACT.Relu).then_inc(bank_free, 1)
                    act.wait_ge(bank_free, j * 2 + (b + 1))
                    link(act.activation(t1[:, b, :], t0[:, b, :], ACT.Square))
                    act.activation(hs[:, bass.ds(tile + 2 * b, 2), 0:T], t1[:, b, :], ACT.Copy).then_inc(hid_hi, 1)

            def gelu_v(j, g, a):
                act.wait_ge(unit_used, j * GU + GU)
                for b in range(2):
                    dst = vtok[:, b, bass.ds(g * NC, NC)]
                    act.activation(dst, bank[2 * a + b][:, :], ACT.Gelu_apprx_tanh).then_inc(bank_free, 1)
                    act.wait_ge(bank_free, j * 2 + (b + 1))
                    act.activation(t0[:, b, :], dst, ACT.Square, accum_out=ssv[:, b, bass.ds(g, 1)])

            def gelu_u(j, g, h, a, tile):
                act.wait_ge(unit_used, j * GU + GU)
                for b in range(2):
                    act.wait_ge(hid_lo, h * 2 + (b + 1))
                    act.activation(t0[:, b, :], bank[2 * a + b][:, :], ACT.Gelu_apprx_tanh).then_inc(bank_free, 1)
                for b in range(2):
                    act.wait_ge(prod_ready, g * 2 + (b + 1))
                    act.activation(hs[:, bass.ds(tile + 2 * b, 2), 0:T], t1[:, b, :], ACT.Copy).then_inc(hid_hi, 1)

            def conv(j, a, pair, off, h):
                act.wait_ge(unit_used, j * GU + GU)
                if off == 0:
                    act.wait_ge(hid_lo, h * 2 + 2)
                for b in range(2):
                    if off:
                        act.wait_ge(gate_ready, pair * 2 + (b + 1))
                    for m in range(2):
                        tile = pair * 4 + (off + 2 * b + m)
                        ins = act.activation(zt[:, 2 * b + m, :], bank[2 * a + b][:, m * T:(m + 1) * T], ACT.Identity,
                                             bias=cw[:, bass.ds(tile, 1), 3], scale=cw[:, bass.ds(tile, 1), 1])
                    ins.then_inc(zt_ready, 1)

            def gate(j, a, pair, h):
                conv(j, a, pair, 0, h)
                for b in range(2):
                    act.wait_ge(bank_free, j * 2 + (b + 1))
                    act.activation(gt[:, 2 * b:2 * b + 2, :], zt[:, 2 * b:2 * b + 2, :], ACT.Sigmoid
                                   ).then_inc(sg_ready, 1)

            def value(j, a, pair, h, tile):
                conv(j, a, pair, FF2T, h)
                for b in range(2):
                    act.wait_ge(prod_ready, pair * 2 + (b + 1 + 16))
                    act.activation(hs[:, bass.ds(tile + 2 * b, 2), 0:T], t1[:, b, :], ACT.Copy).then_inc(hid_hi, 1)

            def prep(hf):
                act.wait_ge(bank_free, 4 * hf + 4)
                if hf:
                    act.wait_ge(h_ff, 1)
                act.activation(sgf[:, :], fg[:, 4 * hf:4 * hf + 4, :], ACT.Sigmoid).then_inc(h_sg, 1)

            def logs(hf):
                act.wait_ge(h_ff, hf + 1)
                if hf:
                    act.wait_ge(lg_sum, 1)
                act.activation(lgf[:, :], fft[:, :], ACT.Ln).then_inc(h_ln, 1)

            def exps(hf, l):
                i = l
                act.wait_ge(h_arg, hf * 8 + l + 1)
                act.activation(arg[:, i % 2, :, :], arg[:, i % 2, :, :], ACT.Exp).then_inc(h_exp, 1)

            act.wait_ge(cst, 1)
            squares(0, x, ready=lambda i: (x_arrived[i // 2], 16))
            split(0, 0)
            split(1, 1)
            root(0)
            split_xs(0, 0, 1)
            split(2, 2)
            split_xs(0, 1, 2)
            split(3, 3)
            split_xs(0, 2)

            def bounds():
                act.activation(sc_c[:, :], cf[:, :], ACT.Sigmoid).then_inc(silu_e, 1)
                act.wait_ge(lb_s, 1)
                act.activation(lb2[:, :, :], lb2[:, :, :], ACT.Exp).then_inc(lb_s, 1)

            dsts = [lambda b: fg[:, 2 * b:2 * b + 2, :], lambda b: qq[:, 2 * b:2 * b + 2, :],
                    lambda b: fg[:, 4 + 2 * b:6 + 2 * b, :], lambda b: qq[:, 4 + 2 * b:6 + 2 * b, :],
                    lambda b: vv[:, b, 0:NC], lambda b: vv[:, b, NC:2 * NC],
                    lambda b: uu[:, 2 * b:2 * b + 2, PAD:], lambda b: uu[:, 4 + 2 * b:6 + 2 * b, PAD:],
                    lambda b: fg[:, 2 * b:2 * b + 2, :], lambda b: fg[:, 4 + 2 * b:6 + 2 * b, :]]

            def gate_heads(hf):
                h4 = slice(4 * hf, 4 * hf + 4)
                act.wait_ge(bank_free, 2 * (8 + hf) + 2)
                act.activation(fg[:, h4, :], fg[:, h4, :], ACT.Sigmoid).then_inc(h_gs, 1)
                act.wait_ge(h_og, hf + 1)
                act.activation(sq8[:, h4, :], oo[:, h4, :], ACT.Square).then_inc(h_sq, 1)

            def root_heads(hf):
                h4 = slice(4 * hf, 4 * hf + 4)
                act.wait_ge(h_va, hf + 1)
                act.activation(sq8[:, h4, :], sq8[:, h4, :], ACT.Sqrt).then_inc(h_sd, 1)

            def mix_half(lo, hi):
                for i in range(lo, hi):
                    act.wait_ge(mix_t, i + 1)
                    src = mixf if i < 4 else oo
                    i4 = i % 4
                    act.activation(hs[:, 2 * i:2 * i + 2, 0:T], src[:, 2 * i4:2 * i4 + 2, :], ACT.Copy
                                   ).then_inc(mix_hi, 1)

            for j in range(G_OUT):
                def after(i, j=j):
                    if (j, i) == (1, 0):
                        act.wait_ge(par_arrived, 16 * 6)
                        bounds()
                    for hf, j0 in ((0, 2), (1, 4)):
                        l = (j - j0) * 8 + i
                        if l == 0:
                            prep(hf)
                        if l == 1:
                            logs(hf)
                        if 2 <= l <= len(LEVELS) + 1:
                            exps(hf, l - 2)
                    if (j, i) == (6, 3):
                        for hf in range(2):
                            act.wait_ge(h_o, hf + 1)
                            for b in range(2):
                                ins = act.activation(oo[:, 4 * hf + 2 * b:4 * hf + 2 * b + 2, :], mis[2 * hf + b][:, :],
                                                     ACT.Copy)
                            ins.then_inc(h_oc, 1)
                    if (j, i) == (8, 7):
                        mix_half(0, 4)
                    if (j, i) == (9, 1):
                        gate_heads(0)
                    if (j, i) == (9, 5):
                        root_heads(0)

                def evac(j=j):
                    if j == 6:
                        act.wait_ge(ms_ready, 1)
                    if j == 8:
                        act.wait_ge(h_ff, 2)
                    copy_out(dsts[j], j, j * GU)
                    if j == G_OUT - 1:
                        gate_heads(1)
                body(j * GU, evac, after=after)
            for g in range(4):
                def after(i, g=g):
                    if (g, i) == (0, 0):
                        mix_half(4, 6)
                    if (g, i) == (0, 1):
                        root_heads(1)
                    if (g, i) == (0, 2):
                        mix_half(6, 8)

                def evac(j=G_OUT + g, g=g):
                    copy_out(lambda b: acc[:, 4 * g + 2 * b:4 * g + 2 * b + 2, :], j, j * GU)
                    group_squares(1, acc, j, g)
                body((G_OUT + g) * GU, evac, after=after)
            root(1)
            squares(2, x, ready=lambda i: (x_sum, i + 1))
            root(2)
            split_xs(1)

            def mlp_quarter(q, last):
                with act.Fori(0, 2) as p, step.loop(p, 2, 4):
                    for a in range(2):
                        j = q * 8 + p * 2 + (G_MLP + a)
                        body(j * GU, lambda: relu2(j, q * 4 + p * 2 + a, a, p * 8 + 4 * a))
                if last:
                    for g in range(4):
                        j = G_MLP + 28 + g
                        body(j * GU, lambda: group_squares(3, acc, j, g))
                else:
                    with act.Fori(0, 2) as p:
                        for a in range(2):
                            body((q * 8 + p * 2 + (G_MLP + 4 + a)) * GU, lambda: None)

            with act.Fori(0, 3) as q, step.loop(q, 3, 8):
                mlp_quarter(q, False)
            mlp_quarter(3, True)
            root(3)
            squares(4, x, ready=lambda i: (x_sum, i + 9))
            root(4)
            split_xs(2, shift=mod[:, 0, :])
            with act.Fori(0, 4) as p:
                for a in range(2):
                    j = p * 2 + (G_AV + a)
                    body(j * GU, lambda: gelu_v(j, p * 2 + a, a))
            act.activation(t0[:, 0, 0:1], one[:, :], ACT.Copy).then_inc(ssv_ready, 1)
            act.wait_ge(var_v, 1)
            act.activation(rv[:, :], rv[:, :], ACT.Sqrt).then_inc(sd_v, 1)
            for half in range(2):
                with act.Fori(0, 2) as p:
                    for a in range(2):
                        j = p * 2 + (G_AU + 8 * half + a)
                        g = p * 2 + (4 * half + a)
                        body(j * GU, lambda: gelu_u(j, g, g + H_A, a, p * 8 + 4 * a))
                if half:
                    for g in range(4):
                        j = G_AU + 12 + g
                        body(j * GU, lambda: group_squares(5, x, j, g))
                else:
                    with act.Fori(0, 2) as p:
                        for a in range(2):
                            body((p * 2 + (G_AU + 4 + a)) * GU, lambda: None)
            root(5)
            split_xs(3, shift=mod[:, 3, :])
            with act.Fori(0, 2) as c:
                with act.Fori(0, 4) as p:
                    j = c * 12 + p * 2 + G_FF
                    pair = c * 4 + p
                    body(j * GU, lambda: gate(j, 0, pair, pair + H_F), late=True)
                    body((j + 1) * GU, lambda: value(j + 1, 1, pair, pair + H_F, p * 4), late=True)
                with act.Fori(0, 2) as p:
                    for a in range(2):
                        body((c * 12 + p * 2 + (G_FF + 8 + a)) * GU, lambda: None)
            with act.Fori(0, 3) as p:
                j = p * 2 + G_FT
                body(j * GU, lambda: gate(j, 0, p + 8, p + (H_F + 8)), late=True)
                body((j + 1) * GU, lambda: value(j + 1, 1, p + 8, p + (H_F + 8), p * 4), late=True)
            for g in range(4):
                body(G_DT * GU + g * DTU, lambda: group_squares(6, x, G_DT + g, g), units=DTU, s0=2 * (g % 2))
            root(6)

        @block.gpsimd
        def _(pool):
            def args(hf, l):
                i, m = l, LEVELS[l]
                n = 4 * T // (2 * m)
                if hf * 8 + l >= 2:
                    pool.wait_ge(h_ops, hf * 8 + l - 1)
                v = halves(bb[:, :], m)
                end = v[:, :, 0, m - 1:m].to_broadcast([P, n, m])
                o = arg[:, i % 2, :, :].rearrange("p s (n m) -> p s n m", m=m)
                pool.tensor_tensor(o[:, 0], end, v[:, :, 0, :], ALU.subtract)
                if m == 128:
                    pool.tensor_copy(o[:, 1], v[:, :, 1, :]).then_inc(h_arg, 1)
                else:
                    pool.tensor_tensor(o[:, 1], v[:, :, 1, :], end, ALU.subtract).then_inc(h_arg, 1)

            for hf in range(2):
                pool.wait_ge(lg_sum, hf + 1)
                for l in range(len(LEVELS)):
                    args(hf, l)
            for s in BY_POOL:
                for i in range(8):
                    pool.wait_ge(sq_ready, 8 * s + i + 1)
                    if i == 0:
                        pool.tensor_copy(sqs[:, :], t0[:, 0, :]).then_inc(sq_used, 1)
                    else:
                        pool.wait_ge(sq_used, 8 * s + i)
                        pool.tensor_tensor(sqs[:, :], sqs[:, :], t0[:, i % 2, :], ALU.add).then_inc(sq_used, 1)

        @block.vector
        def _(dve):
            step = Count(dve_step)
            adas = Count(ada_used)

            def link(ins):
                ins.then_inc(dve_step, 1)
                step.done += 1
                dve.wait_ge(dve_step, step.value())

            def split(n, slot):
                dve.wait_ge(hi_ready, n + 1)
                dve.tensor_tensor(wlo[:, slot, :], raw[:, slot, :], whi[:, slot, :].bitcast(F32), ALU.subtract
                                  ).then_inc(lo_ready, 1)

            def ada(k, slot, kt, half):
                dve.wait_ge(ada_arrived[slot], (k - slot) * 8 + 16)
                a = aacc[:, half * UW:(half + 1) * UW]
                dve.wait_ge(ada_used, k)
                dve.scalar_tensor_tensor(out=a, in0=aring[:, slot, :], scalar=sc_c[:, bass.ds(kt, 1)], in1=a,
                                         op0=ALU.mult, op1=ALU.add).then_inc(ada_used, 1)

            def body(n, evac, units=GU, s0=0, after=None, k=None, kt=None, pre=None, late=False):
                if pre:
                    pre()
                for i in range(units):
                    if i == units - 1 and not late:
                        evac()
                    if isinstance(n, int) and n + RING + i >= UNITS:
                        continue
                    split(n + RING + i, (s0 + i) % RING)
                    if k is not None and i < ADA_PER_GROUP:
                        ada(k + i, i % 2, kt + i // 2, i % 2)
                    if after:
                        after(i)
                if late:
                    evac()

            def ada_take(m):
                dve.wait_ge(ada_sum, m * 2 + 2)
                dve.memset(aacc[:, :], 0.0)
                for b in range(4):
                    ins = dve.tensor_reduce(asum[:, 4 * b:4 * b + 4], mis[b][:, :].rearrange("p (c k) -> p c k", c=4),
                                            AX.X, ALU.add)
                link(ins)
                dve.tensor_tensor(mod[:, bass.ds(m, 1), :], asum[:, :], ab[:, bass.ds(m, 1), :], ALU.add
                                  ).then_inc(ada_read, 1)

            def mean(s):
                if s in BY_POOL:
                    dve.wait_ge(sq_sum, BY_POOL.index(s) + 1)
                else:
                    dve.wait_ge(sq_used, 8 * s + 8)
                link(dve.tensor_copy(ssa[:, :], mis[2][:, 0:T]))
                dve.scalar_tensor_tensor(out=ssb[:, :], in0=mis[2][:, T:2 * T], scalar=EPS, in1=ssa[:, :],
                                         op0=ALU.add, op1=ALU.add).then_inc(var_ready, 1)

            def invert(s):
                dve.wait_ge(sd_ready, s + 1)
                link(dve.reciprocal(rstd[:, :], ssa[:, :]))

            def root(s):
                mean(s)
                invert(s)

            def normed_into_x(v, g):
                for i in range(9):
                    if i < 8:
                        for t in range(2 * i, 2 * i + 2):
                            ins = dve.scalar_tensor_tensor(out=acc[:, t, :], in0=acc[:, t, :],
                                                           scalar=gain[:, g, t:t + 1], in1=rstd[:, :],
                                                           op0=ALU.mult, op1=ALU.mult)
                        ins.then_inc(term_ready, 1)
                    if i >= 1:
                        c = slice(2 * i - 2, 2 * i)
                        dve.wait_ge(term_ready, 8 * v + i)
                        dve.tensor_tensor(x[:, c, :], x[:, c, :], acc[:, c, :], ALU.add).then_inc(x_sum, 1)

            def make_xs(z, gn, shift=None, meanwhile=None):
                def normed(i):
                    if i >= 2:
                        dve.wait_ge(xs_lo, 8 * z + i - 1)
                    for m in range(2):
                        ins = dve.scalar_tensor_tensor(out=t1[:, i % 2, m * T:(m + 1) * T], in0=x[:, 2 * i + m, :],
                                                       scalar=gn[:, 2 * i + m:2 * i + m + 1], in1=rstd[:, :],
                                                       op0=ALU.mult, op1=ALU.mult)
                    ins.then_inc(nt_ready, 1)

                normed(0)
                for i in range(8):
                    if i < 7:
                        normed(i + 1)
                    dve.wait_ge(xs_hi, 8 * z + i + 1)
                    if shift is None:
                        dve.tensor_tensor(xs[:, 2 * i:2 * i + 2, T:2 * T],
                                          t1[:, i % 2, :].rearrange("p (a t) -> p a t", a=2),
                                          xs[:, 2 * i:2 * i + 2, 0:T].bitcast(F32), ALU.subtract).then_inc(xs_lo, 1)
                    else:
                        for m in range(2):
                            t = 2 * i + m
                            ins = dve.scalar_tensor_tensor(out=xs[:, t, T:2 * T], in0=t1[:, i % 2, m * T:(m + 1) * T],
                                                           scalar=shift[:, t:t + 1], in1=xs[:, t, 0:T].bitcast(F32),
                                                           op0=ALU.add, op1=ALU.subtract)
                        ins.then_inc(xs_lo, 1)
                    if meanwhile:
                        meanwhile(i)

            def hidden_lo(h, tile, b):
                dve.wait_ge(hid_hi, h * 2 + (b + 1))
                dve.tensor_tensor(hs[:, bass.ds(tile + 2 * b, 2), T:2 * T], t1[:, b, :].rearrange("p (a t) -> p a t", a=2),
                                  hs[:, bass.ds(tile + 2 * b, 2), 0:T].bitcast(F32), ALU.subtract).then_inc(hid_lo, 1)

            def add_up(j, a, tile):
                dve.wait_ge(unit_used, j * GU + GU)
                for b in range(2):
                    o = acc[:, bass.ds(tile + 2 * b, 2), :]
                    dve.tensor_tensor(o, bank[2 * a + b][:, :].rearrange("p (a t) -> p a t", a=2), o, ALU.add
                                      ).then_inc(bank_free, 1)

            def gated_into_x(n_done, a, tile, gate):
                dve.wait_ge(unit_used, n_done)
                for m in range(MT):
                    o = x[:, bass.ds(tile + m, 1), :]
                    ins = dve.scalar_tensor_tensor(out=o, in0=bank[2 * a + m // 2][:, (m % 2) * T:(m % 2 + 1) * T],
                                                   scalar=mod[:, gate, bass.ds(tile + m, 1)], in1=o,
                                                   op0=ALU.mult, op1=ALU.add)
                    if m % 2:
                        ins.then_inc(bank_free, 1)

            def scaled_v(g):
                for b in range(2):
                    ins = dve.tensor_scalar(vs[:, b, :], vtok[:, b, bass.ds(g * NC, NC)], rv[:, b:b + 1], None, ALU.mult)
                ins.then_inc(vs_ready, 1)

            def spatial_gate(j, g, h, tile):
                for b in range(2):
                    dve.wait_ge(mixs_ready, g * 2 + (b + 1))
                    for m in range(2):
                        o = t1[:, b, m * T:(m + 1) * T].rearrange("p (c q) -> p c q", c=2)
                        ins = dve.scalar_tensor_tensor(
                            out=o, in0=mis[b][:, m * T:(m + 1) * T].rearrange("p (c q) -> p c q", c=2),
                            scalar=gv[:, bass.ds(g * 4 + (2 * b + m), 1)],
                            in1=bs[:, bass.ds(g * 2 + b, 1), :].to_broadcast([P, 2, P]), op0=ALU.mult, op1=ALU.add)
                    link(ins)
                    dve.wait_ge(bank_free, j * 2 + (b + 1))
                    dve.tensor_tensor(t1[:, b, :], t1[:, b, :], t0[:, b, :], ALU.mult).then_inc(prod_ready, 1)
                for b in range(2):
                    hidden_lo(h, tile, b)

            def conv(j, a, pair, off):
                for b in range(2):
                    dve.wait_ge(zt_ready, pair * 4 + (b + 1 + (2 if off else 0)))
                    for tap in (0, 2):
                        for m in range(2):
                            tile = pair * 4 + (off + 2 * b + m)
                            o = zt[:, 2 * b + m, 1:T] if tap == 0 else zt[:, 2 * b + m, 0:T - 1]
                            s = m * T + (0 if tap == 0 else 1)
                            ins = dve.scalar_tensor_tensor(out=o, in0=bank[2 * a + b][:, s:s + T - 1],
                                                           scalar=cw[:, bass.ds(tile, 1), tap], in1=o,
                                                           op0=ALU.mult, op1=ALU.add)
                        if tap == 0:
                            link(ins)
                    ins.then_inc(bank_free, 1)

            def gate(j, a, pair):
                conv(j, a, pair, 0)
                for b in range(2):
                    dve.wait_ge(sg_ready, pair * 2 + (b + 1))
                    g2 = gt[:, 2 * b:2 * b + 2, :]
                    dve.tensor_tensor(g2, g2, zt[:, 2 * b:2 * b + 2, :], ALU.mult).then_inc(gate_ready, 1)

            def value(j, a, pair, h, tile):
                conv(j, a, pair, FF2T)
                for b in range(2):
                    dve.wait_ge(bank_free, j * 2 + (b + 1))
                    dve.tensor_tensor(t1[:, b, :].rearrange("p (a t) -> p a t", a=2), gt[:, 2 * b:2 * b + 2, :],
                                      zt[:, 2 * b:2 * b + 2, :], ALU.mult).then_inc(prod_ready, 1)
                for b in range(2):
                    hidden_lo(h, tile, b)

            def prep(hf):
                dve.wait_ge(h_sg, hf + 1)
                if hf:
                    dve.wait_ge(h_sc, len(LEVELS) + 1)
                link(dve.tensor_scalar(kk[:, :], sgf[:, :], -1.0, 1.0, ALU.mult, ALU.add))
                for h in range(4):
                    hh, c = 4 * hf + h, slice(h * T, (h + 1) * T)
                    ins = dve.tensor_scalar(fft[:, c], sgf[:, c], oml[:, hh:hh + 1], lbt[:, hh:hh + 1], ALU.mult, ALU.add)
                ins.then_inc(h_ff, 1)
                for h in range(4):
                    hh, c = 4 * hf + h, slice(h * T, (h + 1) * T)
                    ins = dve.tensor_scalar(kk[:, c], kk[:, c], oml[:, hh:hh + 1], None, ALU.mult)
                link(ins)

            def sums(hf):
                dve.wait_ge(h_ln, hf + 1)
                if hf:
                    dve.wait_ge(h_arg, len(LEVELS))
                for s in range(8):
                    c = slice(s * P, (s + 1) * P)
                    ins = dve.tensor_tensor_scan(bb[:, c], ones128, lgf[:, c], 0.0, ALU.mult, ALU.add)
                ins.then_inc(lg_sum, 1)

            def operands(hf, l):
                i, m = l, LEVELS[l]
                dve.wait_ge(h_exp, hf * 8 + l + 1)
                if two_before(hf, l) is not None:
                    dve.wait_ge(h_sc, two_before(hf, l) + 1)
                e = arg[:, i % 2, :, :].rearrange("p s (n m) -> p s n m", m=m)
                dve.tensor_tensor(halves(kl[:, i % 2, :], m)[:, :, 0, :], halves(kk[:, :], m)[:, :, 0, :], e[:, 0], ALU.mult)
                qh = qq[:, 4 * hf:4 * hf + 4, :].rearrange("p h t -> p (h t)")
                dve.tensor_tensor(qe[:, i % 2, :].rearrange("p (n m) -> p n m", m=m), halves(qh, m)[:, :, 1, :], e[:, 1],
                                  ALU.mult).then_inc(h_ops, 1)

            def keep(hf, l):
                i = half_level(hf, l)
                dve.wait_ge(h_sc, i + 1)
                if l >= 2:
                    dve.wait_ge(h_evac, i)
                if l == len(LEVELS):
                    for tt in range(2):
                        ins = dve.copy_predicated(sc[:, hf, tt, :, :],
                                                  mk[:, NM - P:].rearrange("p (o t) -> p o t", o=1).to_broadcast([P, 4, P]),
                                                  mis[2 + tt][:, :].rearrange("p (h t) -> p h t", h=4))
                    ins.then_inc(h_evac, 1)
                    return
                m, b = LEVELS[l], mis[l % 2]
                if m == 128:
                    dve.tensor_copy(sc[:, hf, 2, :, :], b[:, :].rearrange("p (h t) -> p h t", h=4)).then_inc(h_evac, 1)
                    return
                mask = mk[:, (l - 1) * 64:l * 64].rearrange("p (n m) -> p n m", m=m)
                n = 64 // m
                for tt in range(2):
                    for h in range(4):
                        o = halves(sc[:, hf, tt, h, :], m)[:, :, 1, :]
                        d = b[:, (2 * h + tt) * 64:(2 * h + tt + 1) * 64].rearrange("p (n m) -> p n m", m=m)
                        ins = dve.copy_predicated(o, mask, d)
                ins.then_inc(h_evac, 1)

            def pooled(part):
                if part == 0:
                    dve.wait_ge(bank_free, 16)
                    link(dve.tensor_tensor(sa[:, :, 1:], uu[:, :, 1:], uu[:, :, :PW - 1], ALU.add))
                    return
                if part == 1:
                    link(dve.tensor_tensor(sb_[:, 2:, 3:], sa[:, 2:, 3:], sa[:, 2:, 1:PW - 2], ALU.add))
                    link(dve.tensor_tensor(sa[:, 4:, 7:], sb_[:, 4:, 7:], sb_[:, 4:, 3:PW - 4], ALU.add))
                    return
                link(dve.tensor_tensor(sb_[:, 6:, 15:], sa[:, 6:, 15:], sa[:, 6:, 7:PW - 8], ALU.add))
                for g in range(4):
                    s = (sa, sb_)[g % 2]
                    o = s[:, 2 * g:2 * g + 2, PAD:PAD + 16]
                    ins = dve.tensor_tensor(o, o, cor[:, g:g + 1, :].to_broadcast([P, 2, 16]), ALU.mult)
                link(ins)
                for g, w in enumerate(WINDOWS):
                    s = (sa, sb_)[g % 2]
                    o = uu[:, 2 * g:2 * g + 2, PAD:]
                    ins = dve.scalar_tensor_tensor(out=o, in0=s[:, 2 * g:2 * g + 2, PAD:], scalar=1.0 / w, in1=o,
                                                   op0=ALU.mult, op1=ALU.subtract)
                ins.then_inc(p_d, 1)

            def mix_lower(i):
                src = mixf if i < 4 else oo
                i4 = i % 4
                dve.wait_ge(mix_hi, i + 1)
                dve.tensor_tensor(hs[:, 2 * i:2 * i + 2, T:2 * T], src[:, 2 * i4:2 * i4 + 2, :],
                                  hs[:, 2 * i:2 * i + 2, 0:T].bitcast(F32), ALU.subtract).then_inc(mix_lo, 1)

            def pool_out():
                dve.wait_ge(p_mm, 1)
                for e in range(POOLT):
                    ins = dve.tensor_scalar(mixf[:, e, :], mis[e // 2][:, (e % 2) * T:(e % 2 + 1) * T], pp[:, 0, e:e + 1],
                                            pp[:, 1, e:e + 1], ALU.add, ALU.mult)
                    if e % 2:
                        ins.then_inc(mix_t, 1)

            def gate_heads(hf):
                h4 = slice(4 * hf, 4 * hf + 4)
                dve.wait_ge(h_gs, hf + 1)
                dve.wait_ge(h_oc, 2)
                dve.tensor_tensor(oo[:, h4, :], oo[:, h4, :], fg[:, h4, :], ALU.mult).then_inc(h_og, 1)

            def norm_heads(hf):
                dve.wait_ge(h_ss, hf + 1)
                for i in range(2 * hf, 2 * hf + 2):
                    ins = dve.tensor_scalar(sq8[:, 2 * i:2 * i + 2, :], mis[i][:, :].rearrange("p (a t) -> p a t", a=2),
                                            float(D // HD), EPS, ALU.mult, ALU.add)
                ins.then_inc(h_va, 1)
                dve.wait_ge(h_sd, hf + 1)
                for i in range(2 * hf, 2 * hf + 2):
                    link(dve.reciprocal(sq8[:, 2 * i:2 * i + 2, :], sq8[:, 2 * i:2 * i + 2, :]))
                    for h in range(2 * i, 2 * i + 2):
                        ins = dve.scalar_tensor_tensor(out=oo[:, h, :], in0=oo[:, h, :], scalar=pp[:, 2, h:h + 1],
                                                       in1=sq8[:, h, :], op0=ALU.mult, op1=ALU.mult)
                    ins.then_inc(mix_t, 1)

            dve.memset(inv[:, :], 1.0 / D)
            dve.memset(one[:, :], 1.0).then_inc(cst, 1)
            dve.memset(t1[:, :, :], 0.0).then_inc(hid_lo, 2)
            dve.memset(kl[:, :, :], 0.0)
            ones128_t = place("ones128_t", o_hs + 31 * KB, [P, P])
            ones128 = ones128_t[:, :]
            dve.memset(ones128, 1.0)
            link(dve.memset(sc[:, :, :, :, :], 0.0))
            for i in range(4):
                dve.wait_ge(x_arrived[i], 16)
            dve.wait_ge(par_arrived, 16 * 6)
            split(0, 0)
            split(1, 1)
            root(0)
            make_xs(0, gain[:, 0, :], meanwhile=lambda i: split(2 + i, 2 + i) if i < 2 else None)
            def bounds():
                dve.wait_ge(mix_arrived, 16 * 5)
                link(dve.tensor_tensor(lbm[:, :], lb2[:, 0, :], lb2[:, 1, :], ALU.max))
                link(dve.tensor_tensor(lb2[:, 0, :], lb2[:, 0, :], lbm[:, :], ALU.subtract))
                dve.tensor_tensor(lb2[:, 1, :], lb2[:, 1, :], lbm[:, :], ALU.subtract).then_inc(lb_s, 1)
                dve.wait_ge(silu_e, 1)
                link(dve.tensor_tensor(sc_c[:, :], sc_c[:, :], cf[:, :], ALU.mult))
                dve.wait_ge(lb_s, 2)
                link(dve.tensor_tensor(lbm[:, :], lb2[:, 0, :], lb2[:, 1, :], ALU.add))
                link(dve.reciprocal(lbm[:, :], lbm[:, :]))
                link(dve.tensor_tensor(lbt[:, :], lb2[:, 0, :], lbm[:, :], ALU.mult))
                link(dve.tensor_scalar(oml[:, :], lbt[:, :], -1.0, 1.0, ALU.mult, ALU.add))

            for j in range(G_OUT):
                def after(i, j=j):
                    for hf, j0 in ((0, 2), (1, 4)):
                        l = (j - j0) * 8 + i
                        if l == 0:
                            prep(hf)
                        if l == 1:
                            sums(hf)
                        if 2 <= l <= len(LEVELS) + 1:
                            operands(hf, l - 2)
                        if 4 <= l <= len(LEVELS) + 4:
                            keep(hf, l - 4)
                    if (j, i) == (1, 0):
                        bounds()
                    if (j, i) == (6, 0):
                        dve.wait_ge(h_sc, 18)
                        dve.memset(uu[:, :, 0:PAD], 0.0)
                        link(dve.memset(sa[:, :, 0:PAD], 0.0))
                        dve.memset(sb_[:, :, 0:PAD], 0.0).then_inc(ms_ready, 1)
                    if (j, i) in ((8, 0), (8, 1), (8, 2)):
                        pooled(i)
                    if (j, i) == (8, 7):
                        pool_out()
                    if (j, i) == (9, 0):
                        for k in range(4):
                            mix_lower(k)
                    if (j, i) == (9, 1):
                        gate_heads(0)
                    if (j, i) == (9, 5):
                        norm_heads(0)
                body(j * GU, lambda: gate_heads(1) if j == G_OUT - 1 else None, after=after)
            for g in range(4):
                def after(i, g=g):
                    if (g, i) == (0, 0):
                        mix_lower(4)
                        mix_lower(5)
                    if (g, i) == (0, 1):
                        norm_heads(1)
                    if (g, i) == (0, 2):
                        mix_lower(6)
                        mix_lower(7)
                body((G_OUT + g) * GU, lambda: None, after=after)
            root(1)
            normed_into_x(0, 1)
            root(2)
            make_xs(1, gain[:, 2, :])
            dve.memset(acc[:, :, :], 0.0)
            link(dve.memset(aacc[:, :], 0.0))
            def mlp_quarter(q):
                with dve.Fori(0, 2) as p:
                    for a in range(2):
                        j = q * 8 + p * 2 + (G_MLP + a)
                        g = q * 8 + p * 2 + a
                        h = q * 4 + p * 2 + a
                        body(j * GU, lambda: [hidden_lo(h, p * 8 + 4 * a, b) for b in range(2)],
                             k=g * ADA_PER_GROUP, kt=p * 4 + 2 * a)
                with dve.Fori(0, 2) as p:
                    for a in range(2):
                        j = q * 8 + p * 2 + (G_MLP + 4 + a)
                        g = q * 8 + p * 2 + (4 + a)
                        body(j * GU, lambda: add_up(j, a, p * 8 + 4 * a), k=g * ADA_PER_GROUP, kt=p * 4 + (8 + 2 * a))
                ada_take(q)

            with dve.Fori(0, 4) as q, step.loop(q, 4, 1):
                mlp_quarter(q)
            dve.wait_ge(ada_read, 4)
            link(dve.scalar_tensor_tensor(out=geff[:, :], in0=mod[:, 1, :], scalar=1.0, in1=gain[:, 4, :],
                                          op0=ALU.add, op1=ALU.mult))
            root(3)
            normed_into_x(1, 3)
            root(4)
            make_xs(2, geff[:, :], shift=mod[:, 0, :])
            with dve.Fori(0, 4) as p:
                for a in range(2):
                    j = p * 2 + (G_AV + a)
                    body(j * GU, lambda: None, k=(p * 2 + (32 + a)) * ADA_PER_GROUP, kt=p * 4 + 2 * a)
            ada_take(4)
            dve.wait_ge(ssv_ready, 1)
            for b in range(2):
                ins = dve.tensor_reduce(rv[:, b:b + 1], ssv[:, b, :], AX.X, ALU.add)
            link(ins)
            dve.tensor_scalar(rv[:, :], rv[:, :], 1.0 / AV, EPS, ALU.mult, ALU.add).then_inc(var_v, 1)
            dve.wait_ge(sd_v, 1)
            link(dve.reciprocal(rv[:, :], rv[:, :]))
            dve.wait_ge(ws_arrived, 32)
            for half in range(2):
                with dve.Fori(0, 2) as p, step.loop(p, 2, 4):
                    for a in range(2):
                        j = p * 2 + (G_AU + 8 * half + a)
                        g = p * 2 + (4 * half + a)
                        kw = dict(k=(p * 2 + (40 + a)) * ADA_PER_GROUP, kt=p * 4 + 2 * a) if half == 0 else {}
                        body(j * GU, lambda: spatial_gate(j, g, g + H_A, p * 8 + 4 * a), pre=lambda: scaled_v(g), **kw)
                with dve.Fori(0, 2) as p:
                    for a in range(2):
                        j = p * 2 + (G_AU + 8 * half + 4 + a)
                        kw = dict(k=(p * 2 + (44 + a)) * ADA_PER_GROUP, kt=p * 4 + (8 + 2 * a)) if half == 0 else {}
                        body(j * GU, lambda: gated_into_x(j * GU + GU, a, p * 8 + 4 * a, 2), **kw)
                if half == 0:
                    ada_take(5)
            dve.wait_ge(ada_read, 6)
            link(dve.scalar_tensor_tensor(out=geff[:, :], in0=mod[:, 4, :], scalar=1.0, in1=gain[:, 5, :],
                                          op0=ALU.add, op1=ALU.mult))
            root(5)
            make_xs(3, geff[:, :], shift=mod[:, 3, :])
            with dve.Fori(0, 2) as c, step.loop(c, 2, 16):
                with dve.Fori(0, 4) as p, step.loop(p, 4, 4):
                    j = c * 12 + p * 2 + G_FF
                    pair = c * 4 + p
                    body(j * GU, lambda: gate(j, 0, pair), late=True)
                    body((j + 1) * GU, lambda: value(j + 1, 1, pair, pair + H_F, p * 4), late=True)
                with dve.Fori(0, 2) as p:
                    for a in range(2):
                        j = c * 12 + p * 2 + (G_FF + 8 + a)
                        body(j * GU, lambda: gated_into_x(j * GU + GU, a, p * 8 + 4 * a, 5))
            with dve.Fori(0, 3) as p, step.loop(p, 3, 4):
                j = p * 2 + G_FT
                body(j * GU, lambda: gate(j, 0, p + 8), late=True)
                body((j + 1) * GU, lambda: value(j + 1, 1, p + 8, p + (H_F + 8), p * 4), late=True)
            for g in range(4):
                n = G_DT * GU + g * DTU
                body(n, lambda: gated_into_x(n + DTU, g % 2, 4 * g, 5), units=DTU, s0=2 * (g % 2))
            root(6)
            for t in range(KT):
                ins = dve.scalar_tensor_tensor(out=acc[:, t, :], in0=x[:, t, :], scalar=gain[:, 6, t:t + 1],
                                               in1=rstd[:, :], op0=ALU.mult, op1=ALU.mult)
                if t % 4 == 3:
                    ins.then_inc(out_ready, 1)


def kernel(**inputs):
    import numpy as np
    import concourse.bacc as bacc
    from concourse.bass_utils import run_bass_kernel_spmd as run

    def get(name):
        return np.asarray(inputs[name])

    def units(w, cols, rows=None):
        w = w if rows is None else w[rows[0]:rows[1]]
        k = w.shape[0] // (UK * P)
        return [w[:, c:c + NC].reshape(k, UK, P, NC).transpose(0, 2, 1, 3).reshape(k, P, UW) for c in cols]

    w_in, w_out = get("w_in")[0], get("w_out")[0]
    w1, w2 = get("w_mlp_in")[0], get("w_mlp_out")[0]
    aw, ao = get("a_w_in_2")[0], get("a_w_out_2")[0]
    fu, fd = get("ffn_w_up_2")[0], get("ffn_w_down_2")[0]
    all4 = [0, NC, 2 * NC, 3 * NC]
    s = []
    s += units(w_in, [2048, 1024, 2560, 1536, 3072, 3584, 0, 512, 4096, 4608])
    s += units(w_out, all4)
    for q in range(4):
        s += units(w1, [q * D + c for c in all4])
        s += units(w2, all4, (q * D, (q + 1) * D))
    s += units(aw, [AV + NC * i for i in range(8)])
    for h in range(2):
        s += units(aw, [h * D + c for c in all4])
        s += units(ao, all4, (h * D, (h + 1) * D))
    for c in range(3):
        for p in range(4 if c < 2 else 3):
            s += units(fu, [c * D + p * NC, FF2T * P + c * D + p * NC])
        s += units(fd, all4, (c * D, min((c + 1) * D, FF2T * P)))
    wstream = np.concatenate(s)
    ada = get("ada_w_2")[0].reshape(KT, P, 6, 2, UW).transpose(2, 0, 3, 1, 4).reshape(-1, P, UW)

    def cols(v):
        return v.reshape(-1, P).T

    gains = np.stack([cols(get("norm_mix_pre")[0]), cols(get("norm_mix_post")[0]), cols(get("norm_mlp_pre")[0]),
                      cols(get("norm_mlp_post")[0]), cols(get("norm_g_2")[0, 0]), cols(get("norm_g_2")[0, 1]),
                      cols(get("final_g_2"))], axis=1)
    cw = np.stack([cols(get("ffn_conv_w_2")[0, i]) for i in range(3)] + [cols(get("ffn_conv_b_2")[0])], axis=2)
    masks = np.zeros((P, 7 * 64 + P), np.int32)
    for l, m in enumerate(LEVELS[1:]):
        for t in range(64):
            blk = t // m
            masks[2 * m * blk:2 * m * blk + m, l * 64 + t] = 1
    masks[np.arange(P), 7 * 64 + np.arange(P)] = 1
    corr = np.ones((P, 4, 16), np.float32)
    for g, w in enumerate(WINDOWS):
        for t in range(w - 1):
            corr[:, g, t] = w / (t + 1)
    arrays = {
        "xT": get("x")[0].T.reshape(KT, P, T).transpose(1, 0, 2),
        "wstream": wstream,
        "astream": ada,
        "cT": cols(get("c_2")[0]),
        "adab": get("ada_b_2")[0].reshape(6, KT, P).transpose(2, 0, 1),
        "gains": gains,
        "cwp": cw,
        "gvp": cols(get("a_g_v_2")[0]),
        "bsp": get("a_b_s_2")[0],
        "wsT": get("a_w_s_2")[0].transpose(2, 0, 1),
        "poolw": get("pool_w")[0].reshape(4, 2, P, T).transpose(2, 0, 1, 3).reshape(P, 8, T),
        "poolp": np.stack([cols(get("pool_b")[0].reshape(-1)), cols(get("pool_scale")[0]), cols(get("hgrn_norm_w")[0])], axis=1),
        "lbl": get("lb_logits").reshape(2, HEADS, HD).transpose(2, 0, 1),
        "masks": masks,
        "corr": corr,
        "eye": np.eye(P, dtype=np.float32),
    }
    nc = bacc.Bacc("TRN2", target_bir_lowering=False, num_devices=1, dynamic_dma_scratch_size=RING_OF_POOL)
    args = []
    for name, a in arrays.items():
        a = arrays[name] = np.ascontiguousarray(a)
        args.append(nc.dram_tensor(name, a.shape, mybir.dt.from_np(a.dtype), kind="ExternalInput").ap())
    args.append(nc.dram_tensor("outT", (P, KT, T), F32, kind="ExternalOutput").ap())
    build(nc, *args)
    r = run(nc, [arrays], core_ids=[0])
    return r.results[0]["outT"].transpose(2, 1, 0).reshape(1, T, D)
```

```python
import concourse.bass as bass
from concourse import mybir
from contextlib import ExitStack, contextmanager

F32 = mybir.dt.float32
F32R = mybir.dt.float32r
I32 = mybir.dt.int32
ACT = mybir.ActivationFunctionType
ALU = mybir.AluOpType
AX = mybir.AxisListType

P = 128
T = 256
D = 2048
KT = D // P
NC = 512
MT = NC // P
UK = 2
UW = UK * NC
RING = 4
GU = KT // UK
EPS = 1e-6
EARLY = 4
SPAN = 218 * 1024
RING_OF_POOL = 1024
HEADS = 8
HD = 128
POOLT = 8
WINDOWS = (2, 4, 8, 16)
PAD = 16
LEVELS = (128, 64, 32, 16, 8, 4, 2, 1)
FF1 = 8192
FF2T = 5632 // P
AV = 4096

G_IN = 0
G_OUT = 10
G_MLP = 14
G_AV = G_MLP + 32
G_AU = G_AV + 8
G_FF = G_AU + 16
G_FT = G_FF + 24
G_DT = G_FT + 6
DTU = 6
UNITS = GU * G_DT + 4 * DTU
ADA_PER_GROUP = 4
ADA_GROUPS = 48
ADA_PER_VEC = 32
BY_POOL = (1, 3, 5, 6)
POOL_ADDS = (2, 5)
DVE_ADDS = 8 - len(POOL_ADDS)
H_A, H_F = 16, 24


class Count:

    def __init__(self, sem):
        self.sem, self.done, self.off = sem, 0, 0

    def value(self):
        return self.off + self.done

    @contextmanager
    def loop(self, i, trips, per, start=0):
        off, done = self.off, self.done
        self.off = off + i * per - start * per
        yield
        assert self.done - done == per, (self.done - done, per)
        self.off, self.done = off, done + trips * per


def build(nc, xT, wstream, astream, cT, adab, gains, cwp, gvp, bsp, wsT, poolw, poolp, lbl, masks, corr, eye_in, out):
    ctx = ExitStack()
    with ctx:
        slab = ctx.enter_context(nc.sbuf_tensor("slab", [P, SPAN // 4], F32))
        base = nc.sbuf_base - SPAN
        at = [base]

        def region(size):
            o = at[0]
            at[0] += size
            assert at[0] <= base + SPAN, at[0] - base
            return o

        def place(name, offset, shape, dt=F32):
            return nc.alloc_sbuf_tensor_at(name, shape, dt, offset=offset)

        sem = lambda n: ctx.enter_context(nc.semaphore(n))
        KB = 1024
        raw = place("raw", region(16 * KB), [P, RING, UW])
        whi = place("whi", region(16 * KB), [P, RING, UW], F32R)
        wlo = place("wlo", region(16 * KB), [P, RING, UW], F32R)
        xs = place("xs", region(32 * KB), [P, KT, 2 * T], F32R)
        o_hs = region(32 * KB)
        hs = place("hs", o_hs, [P, KT, 2 * T], F32R)
        x = place("x", region(16 * KB), [P, KT, T])
        o_v = region(32 * KB)
        o_out = region(16 * KB)
        o_ada = region(16 * KB)
        o_vs = region(4 * KB)
        sqs = place("sqs", region(2 * KB), [P, 2 * T])
        t0 = place("t0", region(4 * KB), [P, 2, 2 * T])
        t1 = place("t1", region(4 * KB), [P, 2, 2 * T])

        vtok = place("vtok", o_v, [P, 2, AV])
        vs = place("vs", o_vs, [P, 2, NC])
        ws = place("ws", o_out, [P, 16, P])
        bs = place("bs", o_out + 8 * KB, [P, 16, P])
        zt = place("zt", o_v, [P, MT, T])
        gt = place("gt", o_v + 4 * KB, [P, MT, T])
        acc = place("acc", o_out, [P, KT, T])
        aring = place("aring", o_ada, [P, 2, UW])
        aacc = place("aacc", o_ada + 8 * KB, [P, D])
        rstd = place("rstd", o_vs, [P, T])
        ssa = place("ssa", o_vs + KB, [P, T])

        fg = place("fg", o_v, [P, HEADS, T])
        qq = place("qq", o_v + 8 * KB, [P, HEADS, T])
        mixf = place("mixf", o_v + 8 * KB, [P, HEADS, T])
        vv = place("vv", o_v + 16 * KB, [P, 2, HEADS * HD])
        oo = place("oo", o_v + 24 * KB, [P, HEADS, T])
        kk = place("kk", o_out, [P, 4 * T])
        bb = place("bb", o_out + 4 * KB, [P, 4 * T])
        kl = place("kl", o_out + 8 * KB, [P, 2, 4 * T])
        arg = place("arg", o_ada, [P, 2, 2, 2 * T])
        qe = place("qe", o_ada + 8 * KB, [P, 2, 2 * T])
        lgf = place("lgf", o_ada + 12 * KB, [P, 4 * T])
        PW = PAD + T
        uu = place("uu", o_out, [P, POOLT, PW])
        sa = place("sa", o_out + 9 * KB, [P, POOLT, PW])
        sb_ = place("sb_", o_out + 18 * KB, [P, POOLT, PW])
        sq8 = place("sq8", o_out + 9 * KB, [P, HEADS, T])
        sc = place("sc", o_hs, [P, 2, 3, 4, P])
        pw = place("pw", o_hs + 12 * KB, [P, 8, T])
        sgf = place("sgf", o_hs + 20 * KB, [P, 4 * T])
        fft = place("fft", o_hs + 24 * KB, [P, 4 * T])
        NM = 7 * 64 + P
        mk = place("mk", o_hs + 28 * KB, [P, NM], I32)

        gain = place("gain", region(7 * 64), [P, 7, KT])
        cw = place("cw", region(2 * FF2T * 4 * 4), [P, 2 * FF2T, 4])
        gv = place("gv", region(128), [P, 32])
        ab = place("ab", region(6 * 64), [P, 6, KT])
        mod = place("mod", region(6 * 64), [P, 6, KT])
        sc_c = place("sc_c", region(64), [P, KT])
        geff = place("geff", region(64), [P, KT])
        asum = place("asum", region(64), [P, KT])
        eye = place("eye", region(512), [P, P])
        inv = place("inv", region(512), [P, P])
        one = place("one", region(32), [P, 1])
        eps = place("eps", region(32), [P, 1])
        junk = place("junk", region(32), [P, 1])
        ssv = place("ssv", region(64), [P, 2, 8])
        rv = place("rv", region(32), [P, 2])
        pp = place("pp", o_vs + 3 * KB, [P, 3, 8])
        lb2 = place("lb2", o_vs + 3 * KB + 96, [P, 2, 8])
        lbt = place("lbt", o_vs + 3 * KB + 160, [P, 8])
        oml = place("oml", o_vs + 3 * KB + 192, [P, 8])
        lbm = place("lbm", o_vs + 3 * KB + 224, [P, 8])
        cor = place("cor", o_vs + 3 * KB + 256, [P, 4, 16])
        cf = place("cf", o_vs + 3 * KB + 512, [P, KT])

        bank = [ctx.enter_context(nc.psum_tensor(f"bank{i}", [P, NC], F32)) for i in range(4)]
        mis = [ctx.enter_context(nc.psum_tensor(f"mis{i}", [P, NC], F32)) for i in range(4)]

        raw_arrived = [sem(f"raw_arrived{i}") for i in range(RING)]
        ada_arrived = [sem(f"ada_arrived{i}") for i in range(2)]
        x_arrived = [sem(f"x_arrived{i}") for i in range(4)]
        par_arrived = sem("par_arrived")
        mix_arrived = sem("mix_arrived")
        ws_arrived = sem("ws_arrived")
        out_sent = sem("out_sent")
        hi_ready = sem("hi_ready")
        lo_ready = sem("lo_ready")
        unit_used = sem("unit_used")
        bank_free = sem("bank_free")
        hid_hi = sem("hid_hi")
        hid_lo = sem("hid_lo")
        prod_ready = sem("prod_ready")
        mixs_ready = sem("mixs_ready")
        vs_ready = sem("vs_ready")
        zt_ready = sem("zt_ready")
        sg_ready = sem("sg_ready")
        gate_ready = sem("gate_ready")
        ada_used = sem("ada_used")
        ada_sum = sem("ada_sum")
        ada_read = sem("ada_read")
        sq_ready = sem("sq_ready")
        sq_used = sem("sq_used")
        acc_clear = sem("acc_clear")
        aacc_clear = sem("aacc_clear")
        sd_ready = sem("sd_ready")
        nt_ready = sem("nt_ready")
        xs_hi = sem("xs_hi")
        xs_lo = sem("xs_lo")
        mix_t = sem("mix_t")
        mix_hi = sem("mix_hi")
        mix_lo = sem("mix_lo")
        h_sg = sem("h_sg")
        h_ff = sem("h_ff")
        h_ln = sem("h_ln")
        h_arg = sem("h_arg")
        h_exp = sem("h_exp")
        h_ops = sem("h_ops")
        h_sc = sem("h_sc")
        h_evac = sem("h_evac")
        h_o = sem("h_o")
        h_oc = sem("h_oc")
        p_d = sem("p_d")
        p_mm = sem("p_mm")
        h_gs = sem("h_gs")
        h_og = sem("h_og")
        h_sq = sem("h_sq")
        h_ss = sem("h_ss")
        h_sd = sem("h_sd")
        silu_e = sem("silu_e")
        lb_s = sem("lb_s")
        cst = sem("cst")
        out_ready = sem("out_ready")
        dve_step = sem("dve_step")
        act_step = sem("act_step")
        ms_ready = sem("ms_ready")
        x_sum = sem("x_sum")
        x_sum_pool = sem("x_sum_pool")
        term_ready = sem("term_ready")
        lg_sum = sem("lg_sum")
        ssv_ready = sem("ssv_ready")
        var_v = sem("var_v")
        sd_v = sem("sd_v")

        def half_level(hf, l):
            return hf * (len(LEVELS) + 1) + l

        def two_before(hf, l):
            if l >= 2:
                return half_level(hf, l - 2)
            return half_level(0, len(LEVELS) - 2 + l) if hf else None

        block = ctx.enter_context(nc.Block())

        def halves(ap, m):
            return ap.rearrange("p (n s m) -> p n s m", s=2, m=m)

        @block.sync
        def _(sp):
            def unit(n, slot):
                if not (isinstance(n, int) and n < RING):
                    sp.wait_ge(lo_ready, n - RING + 1)
                sp.dma_start(raw[:, slot, :], wstream[bass.ds(n, 1), :, :].rearrange("o p w -> p (o w)")
                             ).then_inc(raw_arrived[slot], 16)

            def ada(k, slot, wait=True):
                if wait:
                    sp.wait_ge(ada_used, k - 1)
                sp.dma_start(aring[:, slot, :], astream[bass.ds(k, 1), :, :].rearrange("o p w -> p (o w)")
                             ).then_inc(ada_arrived[slot], 16)

            def group(n, k=None, first=False, early=False):
                for i in range(GU):
                    unit(n + i, i % RING)
                    d = i - EARLY if early and i >= 2 else i
                    if k is not None and (i < 2 or 2 <= d < ADA_PER_GROUP):
                        ada(k + d, d % 2, wait=not (first and d < 2))

            for i in range(4):
                sp.dma_start(x[:, 4 * i:4 * i + 4, :], xT[:, 4 * i:4 * i + 4, :]).then_inc(x_arrived[i], 16)
            for dst, src in ((gain, gains), (cw, cwp), (gv, gvp), (ab, adab), (cf, cT), (eye, eye_in)):
                sp.dma_start(dst[:], src).then_inc(par_arrived, 16)
            for i in range(RING):
                unit(i, i)
            for dst, src in ((pw, poolw), (pp, poolp), (lb2, lbl), (mk, masks), (cor, corr)):
                sp.dma_start(dst[:], src).then_inc(mix_arrived, 16)
            with sp.Fori(0, G_MLP) as g:
                group(g * GU + RING)
            sp.wait_ge(mix_lo, 8)
            group(G_MLP * GU + RING, 0, first=True, early=True)
            with sp.Fori(1, 32) as g:
                group(g * GU + (G_MLP * GU + RING), g * ADA_PER_GROUP)
            group((G_MLP + 32) * GU + RING, 32 * ADA_PER_GROUP, early=True)

            def spatial_part(g):
                part = bass.ds(g * 2, 2)
                sp.dma_start(ws[:, part, :], wsT[:, part, :]).then_inc(ws_arrived, 16)
                sp.dma_start(bs[:, part, :], bsp.rearrange("(o g) q -> o g q", o=1)[:, part, :].to_broadcast([P, 2, P])
                             ).then_inc(ws_arrived, 16)

            sp.wait_ge(x_sum, 2 * DVE_ADDS)
            sp.wait_ge(x_sum_pool, 2 * len(POOL_ADDS))
            spatial_part(0)
            with sp.Fori(1, 8) as g:
                group(g * GU + ((G_MLP + 32) * GU + RING), g * ADA_PER_GROUP + 32 * ADA_PER_GROUP)
                spatial_part(g)
            with sp.Fori(40, ADA_GROUPS) as g:
                group(g * GU + (G_MLP * GU + RING), g * ADA_PER_GROUP)
            with sp.Fori(G_MLP + ADA_GROUPS, G_DT) as g:
                group(g * GU + RING)
            for n in range(G_DT * GU + RING, UNITS):
                unit(n, n % RING)
            for i in range(4):
                sp.wait_ge(out_ready, i + 1)
                sp.dma_start(out[:, 4 * i:4 * i + 4, :], acc[:, 4 * i:4 * i + 4, :]).then_inc(out_sent, 16)
            sp.wait_ge(out_sent, 64)

        @block.tensor
        def _(pe):
            def feature_unit(src, kt0, n, slot, first, last, pb, wait=None):
                if wait is not None:
                    pe.wait_ge(*wait)
                pe.wait_ge(lo_ready, n + 1)
                for k in range(UK):
                    for m in range(MT):
                        o = bank[pb + m // 2][:, (m % 2) * T:(m % 2 + 1) * T]
                        c = slice(k * NC + m * P, k * NC + (m + 1) * P)
                        h, l = src[:, kt0 + k, 0:T], src[:, kt0 + k, T:2 * T]
                        st = first and k == 0 and m % 2 == 0
                        sp_ = last and k == UK - 1
                        pe.matmul(o, whi[:, slot, c], h, start=st, stop=False, skip_group_check=True)
                        pe.matmul(o, whi[:, slot, c], l, start=False, stop=False, skip_group_check=True)
                        mm = pe.matmul(o, wlo[:, slot, c], h, start=False, stop=sp_, skip_group_check=True)
                mm.then_inc(unit_used, 1)

            def token_unit(kt0, n, slot, first, last, pb, wait=None):
                if wait is not None:
                    pe.wait_ge(*wait)
                pe.wait_ge(lo_ready, n + 1)
                for k in range(UK):
                    c = slice(k * NC, (k + 1) * NC)
                    for b in range(2):
                        o = bank[pb + b][:, :]
                        h = xs[:, kt0 + k, b * P:(b + 1) * P]
                        l = xs[:, kt0 + k, T + b * P:T + (b + 1) * P]
                        pe.matmul(o, h, whi[:, slot, c], start=first and k == 0, stop=False)
                        pe.matmul(o, l, whi[:, slot, c], start=False, stop=False)
                        mm = pe.matmul(o, h, wlo[:, slot, c], start=False, stop=last and k == UK - 1)
                mm.then_inc(unit_used, 1)

            def group(j, src, pb, n=None, wait=None, token=False, units=GU, s0=0, between=None):
                n = j * GU if n is None else n
                if not (isinstance(j, int) and j < 2):
                    pe.wait_ge(bank_free, j * 2 - 2)
                for u in range(units):
                    w = wait(u) if wait else None
                    if token:
                        token_unit(UK * u, n + u, (s0 + u) % RING, u == 0, u == units - 1, pb, w)
                    else:
                        feature_unit(src, UK * u, n + u, (s0 + u) % RING, u == 0, u == units - 1, pb, w)
                    if between:
                        between(u)

            def mean_of(src, first, last):
                pe.matmul(bank[0][:, 0:T], inv[:, :], src[:, 0:T], start=first, stop=False)
                return pe.matmul(bank[0][:, 0:T], inv[:, :], src[:, T:2 * T], start=False, stop=last)

            def stats(s):
                for i in range(8):
                    pe.wait_ge(sq_ready, 8 * s + i + 1)
                    mean_of(t0[:, i % 2, :], i == 0, i == 7).then_inc(sq_used, 1)

            def stats_of_sum(s):
                pe.wait_ge(sq_used, 8 * s + 6)
                mean_of(sqs[:, :], True, False)
                for i in (6, 7):
                    pe.wait_ge(sq_ready, 8 * s + i + 1)
                    mean_of(t0[:, i % 2, :], False, i == 7).then_inc(sq_used, 1)

            def ada_reduce(m):
                def between(u):
                    if u == 5:
                        pe.wait_ge(ada_used, m * ADA_PER_VEC + ADA_PER_VEC)
                    if u in (5, 6):
                        for c in range(8 * (u - 5), 8 * (u - 4)):
                            mm = pe.transpose(mis[c // MT][:, (c % MT) * P:(c % MT + 1) * P],
                                              aacc[:, c * P:(c + 1) * P], eye[:, :])
                        mm.then_inc(ada_sum, 1)
                return between

            def level(hf, l):
                i = l % 2
                b = mis[i]
                pe.wait_ge(h_ops, hf * 8 + l + 1)
                if two_before(hf, l) is not None:
                    pe.wait_ge(h_evac, two_before(hf, l) + 1)
                if LEVELS[l] == 128:
                    for h in range(4):
                        mm = pe.matmul(b[:, h * P:(h + 1) * P], kl[:, i, h * T:h * T + P],
                                       qe[:, i, h * P:(h + 1) * P], start=True, stop=True)
                else:
                    for s in range(8):
                        h, tt = s // 2, s % 2
                        mm = pe.matmul(b[:, s * 64:(s + 1) * 64],
                                       kl[:, i, h * T + tt * P:h * T + (tt + 1) * P],
                                       qe[:, i, s * 64:(s + 1) * 64], start=True, stop=True)
                mm.then_inc(h_sc, 1)

            def diagonal(hf):
                pe.wait_ge(lg_sum, hf + 1)
                if hf:
                    pe.wait_ge(h_evac, half_level(0, len(LEVELS)) + 1)
                for s in range(8):
                    h, tt = s // 2, s % 2
                    mm = pe.matmul(mis[2 + tt][:, h * P:(h + 1) * P], kk[:, h * T + tt * P:h * T + (tt + 1) * P],
                                   qq[:, 4 * hf + h, tt * P:(tt + 1) * P], start=True, stop=True)
                mm.then_inc(h_sc, 1)

            def weigh(hf):
                pe.wait_ge(h_evac, half_level(hf, len(LEVELS)) + 1)
                pe.wait_ge(bank_free, 12)
                if hf == 0:
                    pe.wait_ge(h_evac, half_level(1, len(LEVELS)) + 1)
                for h in range(4):
                    hh = 4 * hf + h
                    b = mis[hh // 2]
                    o = (hh % 2) * T
                    v = [vv[:, c, hh * P:(hh + 1) * P] for c in range(2)]
                    pe.matmul(b[:, o:o + P], v[0], sc[:, hf, 0, h, :], start=True, stop=True)
                    pe.matmul(b[:, o + P:o + T], v[0], sc[:, hf, 2, h, :], start=True, stop=False)
                    mm = pe.matmul(b[:, o + P:o + T], v[1], sc[:, hf, 1, h, :], start=False, stop=True)
                mm.then_inc(h_o, 1)

            def pool():
                pe.wait_ge(p_d, 1)
                pe.wait_ge(h_oc, 2)
                for e in range(POOLT):
                    for k in range(2):
                        mm = pe.matmul(mis[e // 2][:, (e % 2) * T:(e % 2 + 1) * T],
                                       pw[:, 2 * (e // 2) + k, (e % 2) * P:(e % 2 + 1) * P],
                                       uu[:, 2 * (e // 2) + k, PAD:], start=k == 0, stop=k == 1)
                mm.then_inc(p_mm, 1)

            def head_stats(hf):
                pe.wait_ge(h_sq, hf + 1)
                pe.wait_ge(mix_t, 4)
                for i in range(2 * hf, 2 * hf + 2):
                    mm = pe.matmul(mis[i][:, :], inv[:, :], sq8[:, 2 * i:2 * i + 2, :], start=True, stop=True)
                mm.then_inc(h_ss, 1)

            pe.wait_ge(cst, 1)
            stats(0)
            xs0 = lambda z: (lambda u: (xs_lo, 8 * z + u + 1))
            work = {}
            for l in range(9):
                work[(2 + (l + 5) // 8, (l + 5) % 8)] = (0, l)
                work[(4 + (l + 5) // 8, (l + 5) % 8)] = (1, l)
            for j in range(G_OUT):
                def between(u, j=j):
                    if (j, u) in work:
                        hf, l = work[(j, u)]
                        level(hf, l) if l < len(LEVELS) else diagonal(hf)
                    if (j, u) == (6, 1):
                        weigh(0)
                        weigh(1)
                    if (j, u) == (8, 5):
                        pool()
                    if (j, u) == (9, 5):
                        head_stats(0)
                group(j, xs, 2 * (j % 2), wait=xs0(0), token=j in (4, 5), between=between)
            for i in range(2 * GU):
                g, u = i // (GU // 2) % 2, i % (GU // 2) + i // GU * (GU // 2)
                if u == 0:
                    pe.wait_ge(bank_free, 2 * (G_OUT + g) - 2)
                feature_unit(hs, UK * u, G_OUT * GU + i, i % RING, u == 0, u == GU - 1, 2 * g, (mix_lo, u + 1))
                if i == 3:
                    head_stats(1)
            for g in (2, 3):
                group(G_OUT + g, hs, 2 * (g % 2))
            stats_of_sum(1)
            stats(2)
            with pe.Fori(0, 4) as q:
                with pe.Fori(0, 2) as p:
                    for a in range(2):
                        group(q * 8 + p * 2 + (G_MLP + a), xs, 2 * a, wait=xs0(1))
                for g in range(4):
                    group(q * 8 + (G_MLP + 4 + g), hs, 2 * (g % 2), between=ada_reduce(q) if g == 3 else None,
                          wait=lambda u: (hid_lo, q * 8 + (2 + 2 * (u // 2 + 1))))
            stats_of_sum(3)
            stats(4)
            with pe.Fori(0, 3) as p:
                for a in range(2):
                    group(p * 2 + (G_AV + a), xs, 2 * a, wait=xs0(2), token=True)
            for a in range(2):
                group(G_AV + 6 + a, xs, 2 * a, wait=xs0(2), token=True, between=ada_reduce(4) if a else None)

            def spatial(g):
                pe.wait_ge(vs_ready, g + 1)
                pe.wait_ge(hid_lo, g * 2 + (2 + 2 * H_A))
                for t in range(MT):
                    for c in range(2):
                        mm = pe.matmul(mis[t // 2][:, (t % 2) * T + c * P:(t % 2) * T + (c + 1) * P],
                                       vs[:, c, t * P:(t + 1) * P], ws[:, bass.ds(g * 2 + t // 2, 1), :],
                                       start=True, stop=True)
                    if t % 2:
                        mm.then_inc(mixs_ready, 1)

            pe.wait_ge(ws_arrived, 32 * 8)
            for half in range(2):
                with pe.Fori(0, 2) as p:
                    for a in range(2):
                        group(p * 2 + (G_AU + 8 * half + a), xs, 2 * a, wait=xs0(2))
                        spatial(p * 2 + (4 * half + a))
                hid = lambda u: (hid_lo, 2 + 2 * (H_A + 4 * half + u // 2 + 1))
                with pe.Fori(0, 2 if half else 1) as p:
                    for a in range(2):
                        group(p * 2 + (G_AU + 8 * half + 4 + a), hs, 2 * a, wait=hid)
                if not half:
                    for a in range(2):
                        group(G_AU + 6 + a, hs, 2 * a, wait=hid, between=ada_reduce(5) if a else None)
            stats_of_sum(5)
            with pe.Fori(0, 2) as c:
                with pe.Fori(0, 4) as p:
                    for a in range(2):
                        group(c * 12 + p * 2 + (G_FF + a), xs, 2 * a, wait=xs0(3))
                with pe.Fori(0, 2) as p:
                    for a in range(2):
                        group(c * 12 + p * 2 + (G_FF + 8 + a), hs, 2 * a,
                              wait=lambda u: (hid_lo, c * 8 + (2 + 2 * (H_F + u // 2 + 1))))
            with pe.Fori(0, 3) as p:
                for a in range(2):
                    group(p * 2 + (G_FT + a), xs, 2 * a, wait=xs0(3))
            for g in range(4):
                group(G_DT + g, hs, 2 * (g % 2), n=G_DT * GU + g * DTU, units=DTU, s0=2 * (g % 2),
                      wait=lambda u: (hid_lo, 2 + 2 * (H_F + 8 + u // 2 + 1)))
            stats_of_sum(6)

        @block.scalar
        def _(act):
            step = Count(act_step)

            def link(ins):
                ins.then_inc(act_step, 1)
                step.done += 1
                act.wait_ge(act_step, step.value())

            def split(n, slot):
                act.wait_ge(raw_arrived[slot], rounds(n, slot))
                if not (isinstance(n, int) and n < RING):
                    act.wait_ge(unit_used, n - RING + 1)
                act.activation(whi[:, slot, :], raw[:, slot, :], ACT.Copy).then_inc(hi_ready, 1)

            def rounds(n, slot):
                return 16 * (n // RING + 1) if isinstance(n, int) else (n - slot) * 4 + 16

            def body(n, evac, units=GU, s0=0, after=None, late=False, done=0):
                for i in range(units):
                    if i == units - 1 and not late:
                        evac()
                    if isinstance(n, int) and n + RING + i >= UNITS:
                        continue
                    if i >= done:
                        split(n + RING + i, (s0 + i) % RING)
                    if after:
                        after(i)
                if late:
                    evac()

            def squares(s, src, first=0, last=8, ready=None):
                if last == 8:
                    link(act.activation(junk[:, :], one[:, :], ACT.Sqrt))
                for i in range(first, last):
                    if ready is not None:
                        act.wait_ge(*ready(i))
                    if 8 * s + i - 1 > 0:
                        act.wait_ge(sq_used, 8 * s + i - 1)
                    act.activation(t0[:, i % 2, :], src[:, 2 * i:2 * i + 2, :], ACT.Square).then_inc(sq_ready, 1)

            def sum_ready(v, i):
                if i in POOL_ADDS:
                    return x_sum_pool, len(POOL_ADDS) * v + POOL_ADDS.index(i) + 1
                return x_sum, DVE_ADDS * v + i + 1 - sum(k < i for k in POOL_ADDS)

            def root(s):
                act.wait_ge(sq_used, 8 * s + 8)
                act.activation(ssa[:, :], bank[0][:, 0:T], ACT.Sqrt, bias=eps[:, :]).then_inc(sd_ready, 1)

            def group_squares(s, src, j, g):
                squares(s, src, 2 * g, 2 * g + 2, ready=lambda i: (bank_free, 2 * j + 1 + i % 2))

            def split_xs(z, first=0, last=8, shift=None, meanwhile=None):
                for i in range(first, last):
                    act.wait_ge(nt_ready, 8 * z + i + 1)
                    if shift is not None:
                        for m in range(2):
                            t = 2 * i + m
                            ins = act.activation(xs[:, t, 0:T], t1[:, i % 2, m * T:(m + 1) * T], ACT.Identity,
                                                 bias=shift[:, t:t + 1])
                        ins.then_inc(xs_hi, 1)
                    else:
                        act.activation(xs[:, 2 * i:2 * i + 2, 0:T], t1[:, i % 2, :], ACT.Copy).then_inc(xs_hi, 1)
                    if meanwhile:
                        meanwhile(i)

            def early_splits(j):
                return lambda i: split(j * GU + RING + i - 2, i - 2) if 2 <= i < 2 + EARLY else None

            def copy_out(dst, j, n, units=GU):
                act.wait_ge(unit_used, n + units)
                for b in range(2):
                    act.activation(dst(b), bank[2 * (j % 2) + b][:, :], ACT.Copy).then_inc(bank_free, 1)

            def relu2(j, h, a, tile):
                act.wait_ge(unit_used, j * GU + GU)
                for b in range(2):
                    act.wait_ge(hid_lo, h * 2 + (b + 1))
                    act.activation(t0[:, b, :], bank[2 * a + b][:, :], ACT.Relu).then_inc(bank_free, 1)
                    act.wait_ge(bank_free, j * 2 + (b + 1))
                    link(act.activation(t1[:, b, :], t0[:, b, :], ACT.Square))
                    act.activation(hs[:, bass.ds(tile + 2 * b, 2), 0:T], t1[:, b, :], ACT.Copy).then_inc(hid_hi, 1)

            def gelu_v(j, g, a):
                act.wait_ge(unit_used, j * GU + GU)
                for b in range(2):
                    dst = vtok[:, b, bass.ds(g * NC, NC)]
                    act.activation(dst, bank[2 * a + b][:, :], ACT.Gelu_apprx_tanh).then_inc(bank_free, 1)
                    act.wait_ge(bank_free, j * 2 + (b + 1))
                    act.activation(t0[:, b, :], dst, ACT.Square, accum_out=ssv[:, b, bass.ds(g, 1)])

            def gelu_u(j, g, h, a, tile):
                act.wait_ge(unit_used, j * GU + GU)
                for b in range(2):
                    act.wait_ge(hid_lo, h * 2 + (b + 1))
                    act.activation(t0[:, b, :], bank[2 * a + b][:, :], ACT.Gelu_apprx_tanh).then_inc(bank_free, 1)
                for b in range(2):
                    act.wait_ge(prod_ready, g * 2 + (b + 1))
                    act.activation(hs[:, bass.ds(tile + 2 * b, 2), 0:T], t1[:, b, :], ACT.Copy).then_inc(hid_hi, 1)

            def conv(j, a, pair, off, h):
                act.wait_ge(unit_used, j * GU + GU)
                if off == 0:
                    act.wait_ge(hid_lo, h * 2 + 2)
                for b in range(2):
                    if off:
                        act.wait_ge(gate_ready, pair * 2 + (b + 1))
                    for m in range(2):
                        tile = pair * 4 + (off + 2 * b + m)
                        ins = act.activation(zt[:, 2 * b + m, :], bank[2 * a + b][:, m * T:(m + 1) * T], ACT.Identity,
                                             bias=cw[:, bass.ds(tile, 1), 3], scale=cw[:, bass.ds(tile, 1), 1])
                    ins.then_inc(zt_ready, 1)

            def gate(j, a, pair, h):
                conv(j, a, pair, 0, h)
                for b in range(2):
                    act.wait_ge(bank_free, j * 2 + (b + 1))
                    act.activation(gt[:, 2 * b:2 * b + 2, :], zt[:, 2 * b:2 * b + 2, :], ACT.Sigmoid
                                   ).then_inc(sg_ready, 1)

            def value(j, a, pair, h, tile):
                conv(j, a, pair, FF2T, h)
                for b in range(2):
                    act.wait_ge(prod_ready, pair * 2 + (b + 1 + 16))
                    act.activation(hs[:, bass.ds(tile + 2 * b, 2), 0:T], t1[:, b, :], ACT.Copy).then_inc(hid_hi, 1)

            def prep(hf):
                act.wait_ge(bank_free, 4 * hf + 4)
                if hf:
                    act.wait_ge(h_ff, 1)
                act.activation(sgf[:, :], fg[:, 4 * hf:4 * hf + 4, :], ACT.Sigmoid).then_inc(h_sg, 1)

            def logs(hf):
                act.wait_ge(h_ff, hf + 1)
                if hf:
                    act.wait_ge(lg_sum, 1)
                act.activation(lgf[:, :], fft[:, :], ACT.Ln).then_inc(h_ln, 1)

            def exps(hf, l):
                i = l
                act.wait_ge(h_arg, hf * 8 + l + 1)
                act.activation(arg[:, i % 2, :, :], arg[:, i % 2, :, :], ACT.Exp).then_inc(h_exp, 1)

            act.wait_ge(cst, 1)
            squares(0, x, ready=lambda i: (x_arrived[i // 2], 16))
            split(0, 0)
            root(0)
            split(1, 1)
            split_xs(0, 0, 1)
            split(2, 2)
            split_xs(0, 1, 2)
            split(3, 3)
            split_xs(0, 2)

            def bounds():
                act.activation(sc_c[:, :], cf[:, :], ACT.Sigmoid).then_inc(silu_e, 1)
                act.wait_ge(lb_s, 1)
                act.activation(lb2[:, :, :], lb2[:, :, :], ACT.Exp).then_inc(lb_s, 1)

            dsts = [lambda b: fg[:, 2 * b:2 * b + 2, :], lambda b: qq[:, 2 * b:2 * b + 2, :],
                    lambda b: fg[:, 4 + 2 * b:6 + 2 * b, :], lambda b: qq[:, 4 + 2 * b:6 + 2 * b, :],
                    lambda b: vv[:, b, 0:NC], lambda b: vv[:, b, NC:2 * NC],
                    lambda b: uu[:, 2 * b:2 * b + 2, PAD:], lambda b: uu[:, 4 + 2 * b:6 + 2 * b, PAD:],
                    lambda b: fg[:, 2 * b:2 * b + 2, :], lambda b: fg[:, 4 + 2 * b:6 + 2 * b, :]]

            def gate_heads(hf):
                h4 = slice(4 * hf, 4 * hf + 4)
                act.wait_ge(bank_free, 2 * (8 + hf) + 2)
                act.activation(fg[:, h4, :], fg[:, h4, :], ACT.Sigmoid).then_inc(h_gs, 1)
                act.wait_ge(h_og, hf + 1)
                act.activation(sq8[:, h4, :], oo[:, h4, :], ACT.Square).then_inc(h_sq, 1)

            def root_heads(hf):
                act.wait_ge(h_ss, hf + 1)
                for i in range(2 * hf, 2 * hf + 2):
                    act.activation(sq8[:, 2 * i:2 * i + 2, :], mis[i][:, :], ACT.Sqrt, bias=eps[:, :],
                                   scale=float(D // HD)).then_inc(h_sd, 1)

            def mix_half(lo, hi):
                for i in range(lo, hi):
                    act.wait_ge(mix_t, i + 1)
                    src = mixf if i < 4 else oo
                    i4 = i % 4
                    act.activation(hs[:, 2 * i:2 * i + 2, 0:T], src[:, 2 * i4:2 * i4 + 2, :], ACT.Copy
                                   ).then_inc(mix_hi, 1)

            for j in range(G_OUT):
                def after(i, j=j):
                    if (j, i) == (1, 0):
                        act.wait_ge(par_arrived, 16 * 6)
                        bounds()
                    for hf, j0 in ((0, 2), (1, 4)):
                        l = (j - j0) * 8 + i
                        if l == 0:
                            prep(hf)
                        if l == 1:
                            logs(hf)
                        if 2 <= l <= len(LEVELS) + 1:
                            exps(hf, l - 2)
                    if (j, i) == (6, 3):
                        for hf in range(2):
                            act.wait_ge(h_o, hf + 1)
                            for b in range(2):
                                ins = act.activation(oo[:, 4 * hf + 2 * b:4 * hf + 2 * b + 2, :], mis[2 * hf + b][:, :],
                                                     ACT.Copy)
                            ins.then_inc(h_oc, 1)
                    if (j, i) == (8, 7):
                        mix_half(0, 4)
                    if (j, i) == (9, 1):
                        gate_heads(0)
                    if (j, i) == (9, 5):
                        root_heads(0)

                def evac(j=j):
                    if j == 6:
                        act.wait_ge(ms_ready, 1)
                    if j == 8:
                        act.wait_ge(h_ff, 2)
                    copy_out(dsts[j], j, j * GU)
                    if j == G_OUT - 1:
                        gate_heads(1)
                body(j * GU, evac, after=after)
            for g in range(4):
                def take(g):
                    j = G_OUT + g
                    copy_out(lambda b: acc[:, 4 * g + 2 * b:4 * g + 2 * b + 2, :], j, j * GU if g else j * GU + GU // 2)
                    group_squares(1, acc, j, g)

                def after(i, g=g):
                    i += g * GU
                    if i == 3:
                        root_heads(1)
                    if i in (1, 2, 5, 7):
                        k = 4 + (1, 2, 5, 7).index(i)
                        mix_half(k, k + 1)
                    if i == 11:
                        take(0)
                body((G_OUT + g) * GU, lambda g=g: take(g) if g else None, after=after)
            root(1)
            squares(2, x, ready=lambda i: sum_ready(0, i))
            root(2)
            split_xs(1, meanwhile=early_splits(G_MLP))

            def mlp_quarter(q, last=False, early=False):
                def up(p, early=False):
                    for a in range(2):
                        j = q * 8 + p * 2 + (G_MLP + a)
                        body(j * GU, lambda: relu2(j, q * 4 + p * 2 + a, a, p * 8 + 4 * a),
                             done=0 if a or not early else EARLY)

                if early:
                    up(0, True)
                    up(1)
                else:
                    with act.Fori(0, 2) as p, step.loop(p, 2, 4):
                        up(p)
                if last:
                    for g in range(4):
                        j = G_MLP + 28 + g
                        body(j * GU, lambda: group_squares(3, acc, j, g))
                else:
                    with act.Fori(0, 2) as p:
                        for a in range(2):
                            body((q * 8 + p * 2 + (G_MLP + 4 + a)) * GU, lambda: None)

            mlp_quarter(0, early=True)
            with act.Fori(1, 3) as q, step.loop(q, 2, 8, start=1):
                mlp_quarter(q)
            mlp_quarter(3, last=True)
            root(3)
            squares(4, x, ready=lambda i: sum_ready(1, i))
            root(4)
            split_xs(2, shift=mod[:, 0, :], meanwhile=early_splits(G_AV))

            def gated_values(p, early=False):
                for a in range(2):
                    j = p * 2 + (G_AV + a)
                    body(j * GU, lambda: gelu_v(j, p * 2 + a, a), done=0 if a or not early else EARLY)

            gated_values(0, True)
            with act.Fori(1, 4) as p:
                gated_values(p)
            act.activation(t0[:, 0, 0:1], one[:, :], ACT.Copy).then_inc(ssv_ready, 1)
            act.wait_ge(var_v, 1)
            act.activation(rv[:, :], rv[:, :], ACT.Sqrt).then_inc(sd_v, 1)
            for half in range(2):
                with act.Fori(0, 2) as p:
                    for a in range(2):
                        j = p * 2 + (G_AU + 8 * half + a)
                        g = p * 2 + (4 * half + a)
                        body(j * GU, lambda: gelu_u(j, g, g + H_A, a, p * 8 + 4 * a))
                if half:
                    for g in range(4):
                        j = G_AU + 12 + g
                        body(j * GU, lambda: group_squares(5, x, j, g))
                else:
                    with act.Fori(0, 2) as p:
                        for a in range(2):
                            body((p * 2 + (G_AU + 4 + a)) * GU, lambda: None)
            root(5)
            split_xs(3, shift=mod[:, 3, :], meanwhile=early_splits(G_FF))

            def ffn_chunk(c, early=False):
                def up(p, early=False):
                    j = c * 12 + p * 2 + G_FF
                    pair = c * 4 + p
                    body(j * GU, lambda: gate(j, 0, pair, pair + H_F), late=True, done=EARLY if early else 0)
                    body((j + 1) * GU, lambda: value(j + 1, 1, pair, pair + H_F, p * 4), late=True)

                if early:
                    up(0, True)
                with act.Fori(1 if early else 0, 4) as p:
                    up(p)
                with act.Fori(0, 2) as p:
                    for a in range(2):
                        body((c * 12 + p * 2 + (G_FF + 8 + a)) * GU, lambda: None)

            ffn_chunk(0, early=True)
            ffn_chunk(1)
            with act.Fori(0, 3) as p:
                j = p * 2 + G_FT
                body(j * GU, lambda: gate(j, 0, p + 8, p + (H_F + 8)), late=True)
                body((j + 1) * GU, lambda: value(j + 1, 1, p + 8, p + (H_F + 8), p * 4), late=True)
            for g in range(4):
                body(G_DT * GU + g * DTU, lambda: group_squares(6, x, G_DT + g, g), units=DTU, s0=2 * (g % 2))
            root(6)

        @block.gpsimd
        def _(pool):
            def args(hf, l):
                i, m = l, LEVELS[l]
                n = 4 * T // (2 * m)
                if hf * 8 + l >= 2:
                    pool.wait_ge(h_ops, hf * 8 + l - 1)
                v = halves(bb[:, :], m)
                end = v[:, :, 0, m - 1:m].to_broadcast([P, n, m])
                o = arg[:, i % 2, :, :].rearrange("p s (n m) -> p s n m", m=m)
                pool.tensor_tensor(o[:, 0], end, v[:, :, 0, :], ALU.subtract)
                if m == 128:
                    pool.tensor_copy(o[:, 1], v[:, :, 1, :]).then_inc(h_arg, 1)
                else:
                    pool.tensor_tensor(o[:, 1], v[:, :, 1, :], end, ALU.subtract).then_inc(h_arg, 1)

            for hf in range(2):
                pool.wait_ge(lg_sum, hf + 1)
                for l in range(len(LEVELS)):
                    args(hf, l)

            def add_pairs(v):
                for i in POOL_ADDS:
                    c = slice(2 * i, 2 * i + 2)
                    pool.wait_ge(term_ready, 8 * v + i + 1)
                    pool.tensor_tensor(x[:, c, :], x[:, c, :], acc[:, c, :], ALU.add).then_inc(x_sum_pool, 1)

            def clear_aacc(m):
                pool.wait_ge(ada_sum, m * 2 + 2)
                pool.memset(aacc[:, :], 0.0).then_inc(aacc_clear, 1)

            for s in BY_POOL:
                if s == 3:
                    add_pairs(0)
                    pool.wait_ge(x_sum_pool, len(POOL_ADDS))
                    pool.wait_ge(x_sum, DVE_ADDS)
                    pool.memset(aacc[:, :], 0.0).then_inc(aacc_clear, 1)
                    pool.memset(acc[:, :, :], 0.0).then_inc(acc_clear, 1)
                    for m in range(3):
                        clear_aacc(m)
                if s == 5:
                    add_pairs(1)
                    clear_aacc(3)
                    clear_aacc(4)
                for i in range(6):
                    pool.wait_ge(sq_ready, 8 * s + i + 1)
                    if i == 0:
                        pool.tensor_copy(sqs[:, :], t0[:, 0, :]).then_inc(sq_used, 1)
                    else:
                        pool.wait_ge(sq_used, 8 * s + i)
                        pool.tensor_tensor(sqs[:, :], sqs[:, :], t0[:, i % 2, :], ALU.add).then_inc(sq_used, 1)

        @block.vector
        def _(dve):
            step = Count(dve_step)

            def link(ins):
                ins.then_inc(dve_step, 1)
                step.done += 1
                dve.wait_ge(dve_step, step.value())

            def split(n, slot):
                dve.wait_ge(hi_ready, n + 1)
                dve.tensor_tensor(wlo[:, slot, :], raw[:, slot, :], whi[:, slot, :].bitcast(F32), ALU.subtract
                                  ).then_inc(lo_ready, 1)

            def ada(k, slot, kt, half):
                dve.wait_ge(ada_arrived[slot], (k - slot) * 8 + 16)
                a = aacc[:, half * UW:(half + 1) * UW]
                dve.wait_ge(ada_used, k)
                dve.scalar_tensor_tensor(out=a, in0=aring[:, slot, :], scalar=sc_c[:, bass.ds(kt, 1)], in1=a,
                                         op0=ALU.mult, op1=ALU.add).then_inc(ada_used, 1)

            def body(n, evac, units=GU, s0=0, after=None, k=None, kt=None, pre=None, late=False, done=0):
                if pre:
                    pre()
                for i in range(units):
                    if i == units - 1 and not late:
                        evac()
                    if isinstance(n, int) and n + RING + i >= UNITS:
                        continue
                    if i >= done:
                        split(n + RING + i, (s0 + i) % RING)
                    d = i - done
                    if k is not None and 0 <= d < ADA_PER_GROUP:
                        ada(k + d, d % 2, kt + d // 2, d % 2)
                    if after:
                        after(i)
                if late:
                    evac()

            def early_splits(j):
                return lambda i: split(j * GU + RING + i - 2, i - 2) if 2 <= i < 2 + EARLY else None

            def ada_take(m):
                dve.wait_ge(ada_sum, m * 2 + 2)
                for b in range(4):
                    ins = dve.tensor_reduce(asum[:, 4 * b:4 * b + 4], mis[b][:, :].rearrange("p (c k) -> p c k", c=4),
                                            AX.X, ALU.add)
                link(ins)
                dve.tensor_tensor(mod[:, bass.ds(m, 1), :], asum[:, :], ab[:, bass.ds(m, 1), :], ALU.add
                                  ).then_inc(ada_read, 1)

            def root(s):
                dve.wait_ge(sd_ready, s + 1)
                link(dve.reciprocal(rstd[:, :], ssa[:, :]))

            def normed_into_x(v, g):
                for i in range(9):
                    if i < 8:
                        for t in range(2 * i, 2 * i + 2):
                            ins = dve.scalar_tensor_tensor(out=acc[:, t, :], in0=acc[:, t, :],
                                                           scalar=gain[:, g, t:t + 1], in1=rstd[:, :],
                                                           op0=ALU.mult, op1=ALU.mult)
                        ins.then_inc(term_ready, 1)
                    if i >= 1:
                        c = slice(2 * i - 2, 2 * i)
                        if i - 1 in POOL_ADDS:
                            continue
                        dve.wait_ge(term_ready, 8 * v + i)
                        dve.tensor_tensor(x[:, c, :], x[:, c, :], acc[:, c, :], ALU.add).then_inc(x_sum, 1)
                dve.wait_ge(x_sum_pool, len(POOL_ADDS) * (v + 1))

            def make_xs(z, gn, shift=None, first=None, meanwhile=None):
                def normed(i):
                    if i >= 2:
                        dve.wait_ge(xs_lo, 8 * z + i - 1)
                    for m in range(2):
                        ins = dve.scalar_tensor_tensor(out=t1[:, i % 2, m * T:(m + 1) * T], in0=x[:, 2 * i + m, :],
                                                       scalar=gn[:, 2 * i + m:2 * i + m + 1], in1=rstd[:, :],
                                                       op0=ALU.mult, op1=ALU.mult)
                    ins.then_inc(nt_ready, 1)

                normed(0)
                if first:
                    first()
                for i in range(8):
                    if i < 7:
                        normed(i + 1)
                    dve.wait_ge(xs_hi, 8 * z + i + 1)
                    if shift is None:
                        dve.tensor_tensor(xs[:, 2 * i:2 * i + 2, T:2 * T],
                                          t1[:, i % 2, :].rearrange("p (a t) -> p a t", a=2),
                                          xs[:, 2 * i:2 * i + 2, 0:T].bitcast(F32), ALU.subtract).then_inc(xs_lo, 1)
                    else:
                        for m in range(2):
                            t = 2 * i + m
                            ins = dve.scalar_tensor_tensor(out=xs[:, t, T:2 * T], in0=t1[:, i % 2, m * T:(m + 1) * T],
                                                           scalar=shift[:, t:t + 1], in1=xs[:, t, 0:T].bitcast(F32),
                                                           op0=ALU.add, op1=ALU.subtract)
                        ins.then_inc(xs_lo, 1)
                    if meanwhile:
                        meanwhile(i)

            def hidden_lo(h, tile, b):
                dve.wait_ge(hid_hi, h * 2 + (b + 1))
                dve.tensor_tensor(hs[:, bass.ds(tile + 2 * b, 2), T:2 * T], t1[:, b, :].rearrange("p (a t) -> p a t", a=2),
                                  hs[:, bass.ds(tile + 2 * b, 2), 0:T].bitcast(F32), ALU.subtract).then_inc(hid_lo, 1)

            def add_up(j, a, tile):
                dve.wait_ge(unit_used, j * GU + GU)
                for b in range(2):
                    o = acc[:, bass.ds(tile + 2 * b, 2), :]
                    dve.tensor_tensor(o, bank[2 * a + b][:, :].rearrange("p (a t) -> p a t", a=2), o, ALU.add
                                      ).then_inc(bank_free, 1)

            def gated_into_x(n_done, a, tile, gate):
                dve.wait_ge(unit_used, n_done)
                for m in range(MT):
                    o = x[:, bass.ds(tile + m, 1), :]
                    ins = dve.scalar_tensor_tensor(out=o, in0=bank[2 * a + m // 2][:, (m % 2) * T:(m % 2 + 1) * T],
                                                   scalar=mod[:, gate, bass.ds(tile + m, 1)], in1=o,
                                                   op0=ALU.mult, op1=ALU.add)
                    if m % 2:
                        ins.then_inc(bank_free, 1)

            def scaled_v(g):
                for b in range(2):
                    ins = dve.tensor_scalar(vs[:, b, :], vtok[:, b, bass.ds(g * NC, NC)], rv[:, b:b + 1], None, ALU.mult)
                ins.then_inc(vs_ready, 1)

            def spatial_gate(j, g, h, tile):
                for b in range(2):
                    dve.wait_ge(mixs_ready, g * 2 + (b + 1))
                    for m in range(2):
                        o = t1[:, b, m * T:(m + 1) * T].rearrange("p (c q) -> p c q", c=2)
                        ins = dve.scalar_tensor_tensor(
                            out=o, in0=mis[b][:, m * T:(m + 1) * T].rearrange("p (c q) -> p c q", c=2),
                            scalar=gv[:, bass.ds(g * 4 + (2 * b + m), 1)],
                            in1=bs[:, bass.ds(g * 2 + b, 1), :].to_broadcast([P, 2, P]), op0=ALU.mult, op1=ALU.add)
                    link(ins)
                    dve.wait_ge(bank_free, j * 2 + (b + 1))
                    dve.tensor_tensor(t1[:, b, :], t1[:, b, :], t0[:, b, :], ALU.mult).then_inc(prod_ready, 1)
                for b in range(2):
                    hidden_lo(h, tile, b)

            def conv(j, a, pair, off):
                for b in range(2):
                    dve.wait_ge(zt_ready, pair * 4 + (b + 1 + (2 if off else 0)))
                    for tap in (0, 2):
                        for m in range(2):
                            tile = pair * 4 + (off + 2 * b + m)
                            o = zt[:, 2 * b + m, 1:T] if tap == 0 else zt[:, 2 * b + m, 0:T - 1]
                            s = m * T + (0 if tap == 0 else 1)
                            ins = dve.scalar_tensor_tensor(out=o, in0=bank[2 * a + b][:, s:s + T - 1],
                                                           scalar=cw[:, bass.ds(tile, 1), tap], in1=o,
                                                           op0=ALU.mult, op1=ALU.add)
                        if tap == 0:
                            link(ins)
                    ins.then_inc(bank_free, 1)

            def gate(j, a, pair):
                conv(j, a, pair, 0)
                for b in range(2):
                    dve.wait_ge(sg_ready, pair * 2 + (b + 1))
                    g2 = gt[:, 2 * b:2 * b + 2, :]
                    dve.tensor_tensor(g2, g2, zt[:, 2 * b:2 * b + 2, :], ALU.mult).then_inc(gate_ready, 1)

            def value(j, a, pair, h, tile):
                conv(j, a, pair, FF2T)
                for b in range(2):
                    dve.wait_ge(bank_free, j * 2 + (b + 1))
                    dve.tensor_tensor(t1[:, b, :].rearrange("p (a t) -> p a t", a=2), gt[:, 2 * b:2 * b + 2, :],
                                      zt[:, 2 * b:2 * b + 2, :], ALU.mult).then_inc(prod_ready, 1)
                for b in range(2):
                    hidden_lo(h, tile, b)

            def prep(hf):
                dve.wait_ge(h_sg, hf + 1)
                if hf:
                    dve.wait_ge(h_sc, len(LEVELS) + 1)
                link(dve.tensor_scalar(kk[:, :], sgf[:, :], -1.0, 1.0, ALU.mult, ALU.add))
                for h in range(4):
                    hh, c = 4 * hf + h, slice(h * T, (h + 1) * T)
                    ins = dve.tensor_scalar(fft[:, c], sgf[:, c], oml[:, hh:hh + 1], lbt[:, hh:hh + 1], ALU.mult, ALU.add)
                ins.then_inc(h_ff, 1)
                for h in range(4):
                    hh, c = 4 * hf + h, slice(h * T, (h + 1) * T)
                    ins = dve.tensor_scalar(kk[:, c], kk[:, c], oml[:, hh:hh + 1], None, ALU.mult)
                link(ins)

            def sums(hf):
                dve.wait_ge(h_ln, hf + 1)
                if hf:
                    dve.wait_ge(h_arg, len(LEVELS))
                for s in range(8):
                    c = slice(s * P, (s + 1) * P)
                    ins = dve.tensor_tensor_scan(bb[:, c], ones128, lgf[:, c], 0.0, ALU.mult, ALU.add)
                ins.then_inc(lg_sum, 1)

            def operands(hf, l):
                i, m = l, LEVELS[l]
                dve.wait_ge(h_exp, hf * 8 + l + 1)
                if two_before(hf, l) is not None:
                    dve.wait_ge(h_sc, two_before(hf, l) + 1)
                e = arg[:, i % 2, :, :].rearrange("p s (n m) -> p s n m", m=m)
                dve.tensor_tensor(halves(kl[:, i % 2, :], m)[:, :, 0, :], halves(kk[:, :], m)[:, :, 0, :], e[:, 0], ALU.mult)
                qh = qq[:, 4 * hf:4 * hf + 4, :].rearrange("p h t -> p (h t)")
                dve.tensor_tensor(qe[:, i % 2, :].rearrange("p (n m) -> p n m", m=m), halves(qh, m)[:, :, 1, :], e[:, 1],
                                  ALU.mult).then_inc(h_ops, 1)

            def keep(hf, l):
                i = half_level(hf, l)
                dve.wait_ge(h_sc, i + 1)
                if l >= 2:
                    dve.wait_ge(h_evac, i)
                if l == len(LEVELS):
                    for tt in range(2):
                        ins = dve.copy_predicated(sc[:, hf, tt, :, :],
                                                  mk[:, NM - P:].rearrange("p (o t) -> p o t", o=1).to_broadcast([P, 4, P]),
                                                  mis[2 + tt][:, :].rearrange("p (h t) -> p h t", h=4))
                    ins.then_inc(h_evac, 1)
                    return
                m, b = LEVELS[l], mis[l % 2]
                if m == 128:
                    dve.tensor_copy(sc[:, hf, 2, :, :], b[:, :].rearrange("p (h t) -> p h t", h=4)).then_inc(h_evac, 1)
                    return
                mask = mk[:, (l - 1) * 64:l * 64].rearrange("p (n m) -> p n m", m=m)
                n = 64 // m
                for tt in range(2):
                    for h in range(4):
                        o = halves(sc[:, hf, tt, h, :], m)[:, :, 1, :]
                        d = b[:, (2 * h + tt) * 64:(2 * h + tt + 1) * 64].rearrange("p (n m) -> p n m", m=m)
                        ins = dve.copy_predicated(o, mask, d)
                ins.then_inc(h_evac, 1)

            def pooled(part):
                if part == 0:
                    dve.wait_ge(bank_free, 16)
                    link(dve.tensor_tensor(sa[:, :, 1:], uu[:, :, 1:], uu[:, :, :PW - 1], ALU.add))
                    return
                if part == 1:
                    link(dve.tensor_tensor(sb_[:, 2:, 3:], sa[:, 2:, 3:], sa[:, 2:, 1:PW - 2], ALU.add))
                    link(dve.tensor_tensor(sa[:, 4:, 7:], sb_[:, 4:, 7:], sb_[:, 4:, 3:PW - 4], ALU.add))
                    return
                link(dve.tensor_tensor(sb_[:, 6:, 15:], sa[:, 6:, 15:], sa[:, 6:, 7:PW - 8], ALU.add))
                for g in range(4):
                    s = (sa, sb_)[g % 2]
                    o = s[:, 2 * g:2 * g + 2, PAD:PAD + 16]
                    ins = dve.tensor_tensor(o, o, cor[:, g:g + 1, :].to_broadcast([P, 2, 16]), ALU.mult)
                link(ins)
                for g, w in enumerate(WINDOWS):
                    s = (sa, sb_)[g % 2]
                    o = uu[:, 2 * g:2 * g + 2, PAD:]
                    ins = dve.scalar_tensor_tensor(out=o, in0=s[:, 2 * g:2 * g + 2, PAD:], scalar=1.0 / w, in1=o,
                                                   op0=ALU.mult, op1=ALU.subtract)
                ins.then_inc(p_d, 1)

            def mix_lower(i):
                src = mixf if i < 4 else oo
                i4 = i % 4
                dve.wait_ge(mix_hi, i + 1)
                dve.tensor_tensor(hs[:, 2 * i:2 * i + 2, T:2 * T], src[:, 2 * i4:2 * i4 + 2, :],
                                  hs[:, 2 * i:2 * i + 2, 0:T].bitcast(F32), ALU.subtract).then_inc(mix_lo, 1)

            def pool_out():
                dve.wait_ge(p_mm, 1)
                for e in range(POOLT):
                    ins = dve.tensor_scalar(mixf[:, e, :], mis[e // 2][:, (e % 2) * T:(e % 2 + 1) * T], pp[:, 0, e:e + 1],
                                            pp[:, 1, e:e + 1], ALU.add, ALU.mult)
                    if e % 2:
                        ins.then_inc(mix_t, 1)

            def gate_heads(hf):
                h4 = slice(4 * hf, 4 * hf + 4)
                dve.wait_ge(h_gs, hf + 1)
                dve.wait_ge(h_oc, 2)
                dve.tensor_tensor(oo[:, h4, :], oo[:, h4, :], fg[:, h4, :], ALU.mult).then_inc(h_og, 1)

            def norm_heads(i):
                dve.wait_ge(h_sd, i + 1)
                link(dve.reciprocal(sq8[:, 2 * i:2 * i + 2, :], sq8[:, 2 * i:2 * i + 2, :]))
                for h in range(2 * i, 2 * i + 2):
                    ins = dve.scalar_tensor_tensor(out=oo[:, h, :], in0=oo[:, h, :], scalar=pp[:, 2, h:h + 1],
                                                   in1=sq8[:, h, :], op0=ALU.mult, op1=ALU.mult)
                ins.then_inc(mix_t, 1)

            dve.memset(inv[:, :], 1.0 / D)
            dve.memset(eps[:, :], EPS)
            dve.memset(one[:, :], 1.0).then_inc(cst, 1)
            dve.memset(t1[:, :, :], 0.0).then_inc(hid_lo, 2)
            dve.memset(kl[:, :, :], 0.0)
            ones128_t = place("ones128_t", o_hs + 31 * KB, [P, P])
            ones128 = ones128_t[:, :]
            dve.memset(ones128, 1.0)
            link(dve.memset(sc[:, :, :, :, :], 0.0))
            for i in range(4):
                dve.wait_ge(x_arrived[i], 16)
            dve.wait_ge(par_arrived, 16 * 6)
            root(0)
            make_xs(0, gain[:, 0, :], first=lambda: split(0, 0),
                    meanwhile=lambda i: split(1 + i, 1 + i) if i < RING - 1 else None)
            def bounds():
                dve.wait_ge(mix_arrived, 16 * 5)
                link(dve.tensor_tensor(lbm[:, :], lb2[:, 0, :], lb2[:, 1, :], ALU.max))
                link(dve.tensor_tensor(lb2[:, 0, :], lb2[:, 0, :], lbm[:, :], ALU.subtract))
                dve.tensor_tensor(lb2[:, 1, :], lb2[:, 1, :], lbm[:, :], ALU.subtract).then_inc(lb_s, 1)
                dve.wait_ge(silu_e, 1)
                link(dve.tensor_tensor(sc_c[:, :], sc_c[:, :], cf[:, :], ALU.mult))
                dve.wait_ge(lb_s, 2)
                link(dve.tensor_tensor(lbm[:, :], lb2[:, 0, :], lb2[:, 1, :], ALU.add))
                link(dve.reciprocal(lbm[:, :], lbm[:, :]))
                link(dve.tensor_tensor(lbt[:, :], lb2[:, 0, :], lbm[:, :], ALU.mult))
                link(dve.tensor_scalar(oml[:, :], lbt[:, :], -1.0, 1.0, ALU.mult, ALU.add))

            for j in range(G_OUT):
                def after(i, j=j):
                    for hf, j0 in ((0, 2), (1, 4)):
                        l = (j - j0) * 8 + i
                        if l == 0:
                            prep(hf)
                        if l == 1:
                            sums(hf)
                        if 2 <= l <= len(LEVELS) + 1:
                            operands(hf, l - 2)
                        if 4 <= l <= len(LEVELS) + 4:
                            keep(hf, l - 4)
                    if (j, i) == (1, 0):
                        bounds()
                    if (j, i) == (6, 0):
                        dve.wait_ge(h_sc, 18)
                        dve.memset(uu[:, :, 0:PAD], 0.0)
                        link(dve.memset(sa[:, :, 0:PAD], 0.0))
                        dve.memset(sb_[:, :, 0:PAD], 0.0).then_inc(ms_ready, 1)
                    if (j, i) in ((8, 0), (8, 1), (8, 2)):
                        pooled(i)
                    if (j, i) == (8, 7):
                        pool_out()
                    if (j, i) == (9, 0):
                        for k in range(4):
                            mix_lower(k)
                    if (j, i) == (9, 1):
                        gate_heads(0)
                    if (j, i) == (9, 6):
                        norm_heads(0)
                body(j * GU, lambda: gate_heads(1) if j == G_OUT - 1 else None, after=after)
            for g in range(4):
                def after(i, g=g):
                    i += g * GU
                    if i in (0, 3, 5):
                        norm_heads(1 + (0, 3, 5).index(i))
                    if i in (2, 4, 6, 8):
                        mix_lower(3 + i // 2)
                body((G_OUT + g) * GU, lambda: None, after=after)
            root(1)
            normed_into_x(0, 1)
            root(2)
            make_xs(1, gain[:, 2, :], meanwhile=early_splits(G_MLP))
            dve.wait_ge(acc_clear, 1)

            def mlp_quarter(q, early=False):
                def up(p, early=False):
                    dve.wait_ge(aacc_clear, q + 1)
                    for a in range(2):
                        j = q * 8 + p * 2 + (G_MLP + a)
                        g = q * 8 + p * 2 + a
                        h = q * 4 + p * 2 + a
                        body(j * GU, lambda: [hidden_lo(h, p * 8 + 4 * a, b) for b in range(2)],
                             k=g * ADA_PER_GROUP, kt=p * 4 + 2 * a, done=0 if a or not early else EARLY)

                if early:
                    up(0, True)
                    up(1)
                else:
                    with dve.Fori(0, 2) as p:
                        up(p)
                with dve.Fori(0, 2) as p:
                    for a in range(2):
                        j = q * 8 + p * 2 + (G_MLP + 4 + a)
                        g = q * 8 + p * 2 + (4 + a)
                        body(j * GU, lambda: add_up(j, a, p * 8 + 4 * a), k=g * ADA_PER_GROUP, kt=p * 4 + (8 + 2 * a))

            mlp_quarter(0, early=True)
            ada_take(0)
            with dve.Fori(1, 3) as q, step.loop(q, 2, 1, start=1):
                mlp_quarter(q)
                ada_take(q)
            mlp_quarter(3)
            dve.wait_ge(ada_read, 3)
            link(dve.scalar_tensor_tensor(out=geff[:, :], in0=mod[:, 1, :], scalar=1.0, in1=gain[:, 4, :],
                                          op0=ALU.add, op1=ALU.mult))
            root(3)
            normed_into_x(1, 3)
            root(4)
            make_xs(2, geff[:, :], shift=mod[:, 0, :], meanwhile=early_splits(G_AV))
            ada_take(3)

            def gated_values(p, early=False):
                for a in range(2):
                    j = p * 2 + (G_AV + a)
                    body(j * GU, lambda: None, k=(p * 2 + (32 + a)) * ADA_PER_GROUP, kt=p * 4 + 2 * a,
                         done=0 if a or not early else EARLY)

            dve.wait_ge(aacc_clear, 5)
            gated_values(0, True)
            with dve.Fori(1, 4) as p:
                gated_values(p)
            ada_take(4)
            dve.wait_ge(ssv_ready, 1)
            for b in range(2):
                ins = dve.tensor_reduce(rv[:, b:b + 1], ssv[:, b, :], AX.X, ALU.add)
            link(ins)
            dve.tensor_scalar(rv[:, :], rv[:, :], 1.0 / AV, EPS, ALU.mult, ALU.add).then_inc(var_v, 1)
            dve.wait_ge(sd_v, 1)
            link(dve.reciprocal(rv[:, :], rv[:, :]))
            dve.wait_ge(ws_arrived, 32 * 8)
            dve.wait_ge(aacc_clear, 6)
            for half in range(2):
                with dve.Fori(0, 2) as p, step.loop(p, 2, 4):
                    for a in range(2):
                        j = p * 2 + (G_AU + 8 * half + a)
                        g = p * 2 + (4 * half + a)
                        kw = dict(k=(p * 2 + (40 + a)) * ADA_PER_GROUP, kt=p * 4 + 2 * a) if half == 0 else {}
                        body(j * GU, lambda: spatial_gate(j, g, g + H_A, p * 8 + 4 * a), pre=lambda: scaled_v(g), **kw)
                with dve.Fori(0, 2) as p:
                    for a in range(2):
                        j = p * 2 + (G_AU + 8 * half + 4 + a)
                        kw = dict(k=(p * 2 + (44 + a)) * ADA_PER_GROUP, kt=p * 4 + (8 + 2 * a)) if half == 0 else {}
                        body(j * GU, lambda: gated_into_x(j * GU + GU, a, p * 8 + 4 * a, 2), **kw)
                if half == 0:
                    ada_take(5)
            dve.wait_ge(ada_read, 6)
            link(dve.scalar_tensor_tensor(out=geff[:, :], in0=mod[:, 4, :], scalar=1.0, in1=gain[:, 5, :],
                                          op0=ALU.add, op1=ALU.mult))
            root(5)
            make_xs(3, geff[:, :], shift=mod[:, 3, :], meanwhile=early_splits(G_FF))

            def ffn_chunk(c, early=False):
                def up(p, early=False):
                    j = c * 12 + p * 2 + G_FF
                    pair = c * 4 + p
                    body(j * GU, lambda: gate(j, 0, pair), late=True, done=EARLY if early else 0)
                    body((j + 1) * GU, lambda: value(j + 1, 1, pair, pair + H_F, p * 4), late=True)

                if early:
                    up(0, True)
                    with dve.Fori(1, 4) as p, step.loop(p, 3, 4, start=1):
                        up(p)
                else:
                    with dve.Fori(0, 4) as p, step.loop(p, 4, 4):
                        up(p)
                with dve.Fori(0, 2) as p:
                    for a in range(2):
                        j = c * 12 + p * 2 + (G_FF + 8 + a)
                        body(j * GU, lambda: gated_into_x(j * GU + GU, a, p * 8 + 4 * a, 5))

            ffn_chunk(0, early=True)
            ffn_chunk(1)
            with dve.Fori(0, 3) as p, step.loop(p, 3, 4):
                j = p * 2 + G_FT
                body(j * GU, lambda: gate(j, 0, p + 8), late=True)
                body((j + 1) * GU, lambda: value(j + 1, 1, p + 8, p + (H_F + 8), p * 4), late=True)
            for g in range(4):
                n = G_DT * GU + g * DTU
                body(n, lambda: gated_into_x(n + DTU, g % 2, 4 * g, 5), units=DTU, s0=2 * (g % 2))
            root(6)
            for t in range(KT):
                ins = dve.scalar_tensor_tensor(out=acc[:, t, :], in0=x[:, t, :], scalar=gain[:, 6, t:t + 1],
                                               in1=rstd[:, :], op0=ALU.mult, op1=ALU.mult)
                if t % 4 == 3:
                    ins.then_inc(out_ready, 1)


def kernel(**inputs):
    import numpy as np
    import concourse.bacc as bacc
    from concourse.bass_utils import run_bass_kernel_spmd as run

    def get(name):
        return np.asarray(inputs[name])

    def units(w, cols, rows=None):
        w = w if rows is None else w[rows[0]:rows[1]]
        k = w.shape[0] // (UK * P)
        return [w[:, c:c + NC].reshape(k, UK, P, NC).transpose(0, 2, 1, 3).reshape(k, P, UW) for c in cols]

    w_in, w_out = get("w_in")[0], get("w_out")[0]
    w1, w2 = get("w_mlp_in")[0], get("w_mlp_out")[0]
    aw, ao = get("a_w_in_2")[0], get("a_w_out_2")[0]
    fu, fd = get("ffn_w_up_2")[0], get("ffn_w_down_2")[0]
    all4 = [0, NC, 2 * NC, 3 * NC]
    s = []
    s += units(w_in, [2048, 1024, 2560, 1536, 3072, 3584, 0, 512, 4096, 4608])
    wo = units(w_out, all4)
    s += [wo[g][h:h + GU // 2] for h in (0, GU // 2) for g in (0, 1)] + wo[2:]
    for q in range(4):
        s += units(w1, [q * D + c for c in all4])
        s += units(w2, all4, (q * D, (q + 1) * D))
    s += units(aw, [AV + NC * i for i in range(8)])
    for h in range(2):
        s += units(aw, [h * D + c for c in all4])
        s += units(ao, all4, (h * D, (h + 1) * D))
    for c in range(3):
        for p in range(4 if c < 2 else 3):
            s += units(fu, [c * D + p * NC, FF2T * P + c * D + p * NC])
        s += units(fd, all4, (c * D, min((c + 1) * D, FF2T * P)))
    wstream = np.concatenate(s)
    ada = get("ada_w_2")[0].reshape(KT, P, 6, 2, UW).transpose(2, 0, 3, 1, 4).reshape(-1, P, UW)

    def cols(v):
        return v.reshape(-1, P).T

    gains = np.stack([cols(get("norm_mix_pre")[0]), cols(get("norm_mix_post")[0]), cols(get("norm_mlp_pre")[0]),
                      cols(get("norm_mlp_post")[0]), cols(get("norm_g_2")[0, 0]), cols(get("norm_g_2")[0, 1]),
                      cols(get("final_g_2"))], axis=1)
    cw = np.stack([cols(get("ffn_conv_w_2")[0, i]) for i in range(3)] + [cols(get("ffn_conv_b_2")[0])], axis=2)
    masks = np.zeros((P, 7 * 64 + P), np.int32)
    for l, m in enumerate(LEVELS[1:]):
        for t in range(64):
            blk = t // m
            masks[2 * m * blk:2 * m * blk + m, l * 64 + t] = 1
    masks[np.arange(P), 7 * 64 + np.arange(P)] = 1
    corr = np.ones((P, 4, 16), np.float32)
    for g, w in enumerate(WINDOWS):
        for t in range(w - 1):
            corr[:, g, t] = w / (t + 1)
    arrays = {
        "xT": get("x")[0].T.reshape(KT, P, T).transpose(1, 0, 2),
        "wstream": wstream,
        "astream": ada,
        "cT": cols(get("c_2")[0]),
        "adab": get("ada_b_2")[0].reshape(6, KT, P).transpose(2, 0, 1),
        "gains": gains,
        "cwp": cw,
        "gvp": cols(get("a_g_v_2")[0]),
        "bsp": get("a_b_s_2")[0],
        "wsT": get("a_w_s_2")[0].transpose(2, 0, 1),
        "poolw": get("pool_w")[0].reshape(4, 2, P, T).transpose(2, 0, 1, 3).reshape(P, 8, T),
        "poolp": np.stack([cols(get("pool_b")[0].reshape(-1)), cols(get("pool_scale")[0]), cols(get("hgrn_norm_w")[0])], axis=1),
        "lbl": get("lb_logits").reshape(2, HEADS, HD).transpose(2, 0, 1),
        "masks": masks,
        "corr": corr,
        "eye": np.eye(P, dtype=np.float32),
    }
    nc = bacc.Bacc("TRN2", target_bir_lowering=False, num_devices=1, dynamic_dma_scratch_size=RING_OF_POOL)
    args = []
    for name, a in arrays.items():
        a = arrays[name] = np.ascontiguousarray(a)
        args.append(nc.dram_tensor(name, a.shape, mybir.dt.from_np(a.dtype), kind="ExternalInput").ap())
    args.append(nc.dram_tensor("outT", (P, KT, T), F32, kind="ExternalOutput").ap())
    build(nc, *args)
    r = run(nc, [arrays], core_ids=[0])
    return r.results[0]["outT"].transpose(2, 1, 0).reshape(1, T, D)
```
